# Optimizing a Trainium2 kernel written in Bass

```python
import math
import numpy as np
import jax
import jax.numpy as jnp
from jax import lax

D_MODEL = 2048
BATCH = 1
SEQ = 512
DEPTH = 1

HEAD_DIM = 128
N_FOX_HEADS = 8
N_NSA_HEADS = 8
N_NSA_KV_HEADS = 2
NSA_GROUP = N_NSA_HEADS // N_NSA_KV_HEADS
FOX_WIDTH = N_FOX_HEADS * HEAD_DIM
NSA_WIDTH = N_NSA_HEADS * HEAD_DIM
NSA_KV_WIDTH = N_NSA_KV_HEADS * HEAD_DIM
MIX_WIDTH = FOX_WIDTH + NSA_WIDTH
N_BRANCH = 3
CMP_BLOCK = 32
CMP_STRIDE = 16
SEL_BLOCK = 64
N_SEL = 8
WINDOW = 512
Q_BLOCK = 128
N_BUCKETS = 32
MAX_DISTANCE = 128
D_FF = -(-(8 * D_MODEL) // (3 * 256)) * 256
N_MOD = 6
IN_SPLITS = (FOX_WIDTH, FOX_WIDTH, FOX_WIDTH, N_FOX_HEADS, NSA_WIDTH,
             N_BRANCH * NSA_KV_WIDTH, N_BRANCH * NSA_KV_WIDTH, N_BRANCH * N_NSA_HEADS)
IN_WIDTH = 3 * FOX_WIDTH + N_FOX_HEADS + NSA_WIDTH + 2 * N_BRANCH * NSA_KV_WIDTH + N_BRANCH * N_NSA_HEADS
SCALE = HEAD_DIM ** -0.5
EPS = 1e-6
NEG = -1e30
FORCE = 1e6

kernel_name = 'hymba_fox_nsa_adaln_block'

def rms_norm(x, gain):
    xf = x.astype(jnp.float32)
    y = xf * lax.rsqrt(jnp.mean(xf * xf, axis=-1, keepdims=True) + EPS)
    return (y * gain.astype(jnp.float32)).astype(x.dtype)

def masked_softmax(logits, valid):
    p = jax.nn.softmax(jnp.where(valid, logits, NEG), axis=-1)
    return jnp.where(valid, p, 0.0)

def t5_bucket(dist):
    n = jnp.maximum(dist, 0)
    max_exact = N_BUCKETS // 2
    nf = jnp.maximum(n, 1).astype(jnp.float32)
    large = max_exact + (jnp.log(nf / max_exact) / math.log(MAX_DISTANCE / max_exact)
                         * (N_BUCKETS - max_exact)).astype(jnp.int32)
    large = jnp.minimum(large, N_BUCKETS - 1)
    return jnp.where(n < max_exact, n, large)

def to_blocks(a):
    b, s = a.shape[:2]
    return jnp.moveaxis(a.reshape(b, s // Q_BLOCK, Q_BLOCK, *a.shape[2:]), 1, 0)

def from_blocks(a):
    nb, b, qb = a.shape[:3]
    return jnp.moveaxis(a, 0, 1).reshape(b, nb * qb, *a.shape[3:])

def forgetting_attention(q, k, v, f_logit, f_bias):
    b, s = q.shape[:2]
    log_f = jax.nn.log_sigmoid(f_logit.astype(jnp.float32) + f_bias.astype(jnp.float32))
    cum = jnp.cumsum(log_f, axis=1)
    cum_k = jnp.transpose(cum, (0, 2, 1))
    kpos = jnp.arange(s)

    def one_block(args):
        qb, cq, q0 = args
        qpos = q0 + jnp.arange(Q_BLOCK)
        logits = jnp.einsum('bqhd,bkhd->bhqk', qb, k).astype(jnp.float32) * SCALE
        logits = logits + jnp.transpose(cq, (0, 2, 1))[..., None] - cum_k[:, :, None, :]
        p = masked_softmax(logits, kpos[None, :] <= qpos[:, None])
        return jnp.einsum('bhqk,bkhd->bqhd', p.astype(v.dtype), v)

    starts = jnp.arange(s // Q_BLOCK, dtype=jnp.int32) * Q_BLOCK
    return from_blocks(lax.map(one_block, (to_blocks(q), to_blocks(cum), starts)))

def compress_blocks(kv, pos_emb, w1, w2):
    b, s = kv.shape[:2]
    n_cmp = (s - CMP_BLOCK) // CMP_STRIDE + 1
    idx = np.arange(n_cmp)[:, None] * CMP_STRIDE + np.arange(CMP_BLOCK)[None, :]
    blocks = kv[:, idx] + pos_emb[None, None, :, None, :]
    flat = jnp.transpose(blocks, (0, 1, 3, 2, 4)).reshape(b, n_cmp, N_NSA_KV_HEADS, CMP_BLOCK * HEAD_DIM)
    return jax.nn.silu(flat @ w1) @ w2

def selection_matrix(n_cmp, n_slc):
    r, q = SEL_BLOCK // CMP_STRIDE, CMP_BLOCK // CMP_STRIDE
    tgt = (r * np.arange(n_slc)[:, None, None] + np.arange(r)[None, :, None]
           - np.arange(q)[None, None, :]).reshape(n_slc, -1)
    return (np.arange(n_cmp)[:, None, None] == tgt[None]).sum(-1).astype(np.float32)

def native_sparse_attention(q, k_br, v_br, gates, k_gain, cmp_pos, cmp_w1, cmp_w2, rel_bias):
    b, s = q.shape[:2]
    hkv, grp = N_NSA_KV_HEADS, NSA_GROUP
    kc = rms_norm(compress_blocks(k_br[:, :, 0], cmp_pos[0], cmp_w1[0], cmp_w2[0]), k_gain[0])
    vc = compress_blocks(v_br[:, :, 0], cmp_pos[1], cmp_w1[1], cmp_w2[1])
    k_slc = rms_norm(k_br[:, :, 1], k_gain[1])
    k_win = rms_norm(k_br[:, :, 2], k_gain[2])
    n_cmp = kc.shape[1]
    n_slc = s // SEL_BLOCK
    top_n = min(N_SEL, n_slc)
    cmp_end = jnp.arange(n_cmp) * CMP_STRIDE + CMP_BLOCK - 1
    sel_m = jnp.asarray(selection_matrix(n_cmp, n_slc))
    ksb = k_slc.reshape(b, n_slc, SEL_BLOCK, hkv, HEAD_DIM).transpose(0, 3, 1, 2, 4)
    vsb = v_br[:, :, 1].reshape(b, n_slc, SEL_BLOCK, hkv, HEAD_DIM).transpose(0, 3, 1, 2, 4)
    pad = ((0, 0), (WINDOW, 0), (0, 0), (0, 0))
    kw = jnp.pad(k_win, pad)
    vw = jnp.pad(v_br[:, :, 2], pad)
    tb = rel_bias.reshape(N_BUCKETS, hkv, grp)
    b_ix = jnp.arange(b)[:, None, None, None]
    h_ix = jnp.arange(hkv)[None, None, :, None]
    blk_ids = jnp.arange(n_slc)

    def one_block(args):
        qb, gb, q0 = args
        qpos = q0 + jnp.arange(Q_BLOCK)
        qg = qb.reshape(b, Q_BLOCK, hkv, grp, HEAD_DIM)
        d_c = qpos[:, None] - cmp_end[None, :]
        s_c = jnp.einsum('bqhgd,bchd->bqhgc', qg, kc).astype(jnp.float32) * SCALE
        s_c = s_c + tb[t5_bucket(d_c)].transpose(0, 2, 3, 1)
        p_c = masked_softmax(s_c, (d_c >= 0)[:, None, None, :])
        o_c = jnp.einsum('bqhgc,bchd->bqhgd', p_c.astype(vc.dtype), vc)
        imp = jnp.einsum('bqhc,cj->bqhj', p_c.sum(axis=3), sel_m)
        cur = (qpos // SEL_BLOCK)[:, None]
        forced = (blk_ids[None, :] == 0) | (blk_ids[None, :] == cur) | (blk_ids[None, :] == cur - 1)
        imp = jnp.where(forced[None, :, None, :], FORCE, imp)
        imp = jnp.where((blk_ids[None, :] <= cur)[None, :, None, :], imp, -jnp.inf)
        top_s, top_i = lax.top_k(imp, top_n)
        ks = ksb[b_ix, h_ix, top_i].reshape(b, Q_BLOCK, hkv, top_n * SEL_BLOCK, HEAD_DIM)
        vs = vsb[b_ix, h_ix, top_i].reshape(b, Q_BLOCK, hkv, top_n * SEL_BLOCK, HEAD_DIM)
        spos = (top_i[..., None] * SEL_BLOCK + jnp.arange(SEL_BLOCK)).reshape(b, Q_BLOCK, hkv, -1)
        d_s = qpos[None, :, None, None] - spos
        valid_s = (d_s >= 0) & jnp.repeat(jnp.isfinite(top_s), SEL_BLOCK, axis=-1)
        s_s = jnp.einsum('bqhgd,bqhkd->bqhgk', qg, ks).astype(jnp.float32) * SCALE
        s_s = s_s + tb[t5_bucket(d_s), h_ix].transpose(0, 1, 2, 4, 3)
        p_s = masked_softmax(s_s, valid_s[:, :, :, None, :])
        o_s = jnp.einsum('bqhgk,bqhkd->bqhgd', p_s.astype(vs.dtype), vs)
        kwb = lax.dynamic_slice_in_dim(kw, q0, WINDOW + Q_BLOCK, axis=1)
        vwb = lax.dynamic_slice_in_dim(vw, q0, WINDOW + Q_BLOCK, axis=1)
        wpos = q0 - WINDOW + jnp.arange(WINDOW + Q_BLOCK)
        d_w = qpos[:, None] - wpos[None, :]
        valid_w = (d_w >= 0) & (d_w < WINDOW) & (wpos[None, :] >= 0)
        s_w = jnp.einsum('bqhgd,bkhd->bqhgk', qg, kwb).astype(jnp.float32) * SCALE
        s_w = s_w + tb[t5_bucket(d_w)].transpose(0, 2, 3, 1)
        p_w = masked_softmax(s_w, valid_w[:, None, None, :])
        o_w = jnp.einsum('bqhgk,bkhd->bqhgd', p_w.astype(vwb.dtype), vwb)
        g = gb.reshape(b, Q_BLOCK, hkv, grp, N_BRANCH)
        o = g[..., 0:1] * o_c + g[..., 1:2] * o_s + g[..., 2:3] * o_w
        return o.reshape(b, Q_BLOCK, N_NSA_HEADS, HEAD_DIM)

    starts = jnp.arange(s // Q_BLOCK, dtype=jnp.int32) * Q_BLOCK
    return from_blocks(lax.map(one_block, (to_blocks(q), to_blocks(gates), starts)))

def setup_inputs(seed: int = 0) -> dict:
    key = jax.random.key(seed)
    ks = jax.random.split(key, 20)
    nrm = lambda k, shape, sc: jax.random.normal(k, shape, jnp.float32) * sc
    gain = lambda k, shape: 1.0 + 0.02 * jax.random.normal(k, shape, jnp.float32)
    return {
        'x': nrm(ks[0], (BATCH, SEQ, D_MODEL), 1.0),
        'c': nrm(ks[1], (BATCH, D_MODEL), 1.0),
        'ada_w': nrm(ks[2], (DEPTH, D_MODEL, N_MOD * D_MODEL), 0.02),
        'ada_b': nrm(ks[3], (DEPTH, N_MOD * D_MODEL), 0.02),
        'norm1_gain': gain(ks[4], (DEPTH, D_MODEL)),
        'norm2_gain': gain(ks[5], (DEPTH, D_MODEL)),
        'w_in': nrm(ks[6], (DEPTH, D_MODEL, IN_WIDTH), D_MODEL ** -0.5),
        'fox_f_bias': jax.random.uniform(ks[7], (DEPTH, N_FOX_HEADS), jnp.float32, 1.0, 4.0),
        'fox_q_gain': gain(ks[8], (DEPTH, HEAD_DIM)),
        'fox_k_gain': gain(ks[9], (DEPTH, HEAD_DIM)),
        'nsa_q_gain': gain(ks[10], (DEPTH, HEAD_DIM)),
        'nsa_k_gain': gain(ks[11], (DEPTH, N_BRANCH, HEAD_DIM)),
        'nsa_cmp_pos': nrm(ks[12], (DEPTH, 2, CMP_BLOCK, HEAD_DIM), 0.1),
        'nsa_cmp_w1': nrm(ks[13], (DEPTH, 2, CMP_BLOCK * HEAD_DIM, HEAD_DIM), (CMP_BLOCK * HEAD_DIM) ** -0.5),
        'nsa_cmp_w2': nrm(ks[14], (DEPTH, 2, HEAD_DIM, HEAD_DIM), HEAD_DIM ** -0.5),
        'rel_bias': nrm(ks[15], (N_BUCKETS, N_NSA_HEADS), 0.1),
        'mix_out_gain': gain(ks[16], (DEPTH, MIX_WIDTH)),
        'w_out': nrm(ks[17], (DEPTH, MIX_WIDTH, D_MODEL), MIX_WIDTH ** -0.5),
        'ffn_w_gate': nrm(ks[18], (DEPTH, D_MODEL, D_FF), D_MODEL ** -0.5),
        'ffn_w_up': nrm(jax.random.fold_in(ks[18], 1), (DEPTH, D_MODEL, D_FF), D_MODEL ** -0.5),
        'ffn_w_down': nrm(ks[19], (DEPTH, D_FF, D_MODEL), D_FF ** -0.5),
    }

def reference(x, c, ada_w, ada_b, norm1_gain, norm2_gain, w_in, fox_f_bias, fox_q_gain, fox_k_gain,
              nsa_q_gain, nsa_k_gain, nsa_cmp_pos, nsa_cmp_w1, nsa_cmp_w2, rel_bias, mix_out_gain,
              w_out, ffn_w_gate, ffn_w_up, ffn_w_down):
    b, s = x.shape[:2]
    split_points = np.cumsum(IN_SPLITS)[:-1].tolist()
    for layer in range(DEPTH):
        mod = (jax.nn.silu(c) @ ada_w[layer] + ada_b[layer])[:, None, :]
        sh1, sc1, g1, sh2, sc2, g2 = jnp.split(mod, N_MOD, axis=-1)
        h = rms_norm(x, norm1_gain[layer]) * (1 + sc1) + sh1
        proj = h @ w_in[layer]
        fq, fk, fv, ff, nq, nk, nv, ng = jnp.split(proj, split_points, axis=-1)
        fq = rms_norm(fq.reshape(b, s, N_FOX_HEADS, HEAD_DIM), fox_q_gain[layer])
        fk = rms_norm(fk.reshape(b, s, N_FOX_HEADS, HEAD_DIM), fox_k_gain[layer])
        fv = fv.reshape(b, s, N_FOX_HEADS, HEAD_DIM)
        o_fox = forgetting_attention(fq, fk, fv, ff, fox_f_bias[layer])
        nq = rms_norm(nq.reshape(b, s, N_NSA_HEADS, HEAD_DIM), nsa_q_gain[layer])
        nk = nk.reshape(b, s, N_BRANCH, N_NSA_KV_HEADS, HEAD_DIM)
        nv = nv.reshape(b, s, N_BRANCH, N_NSA_KV_HEADS, HEAD_DIM)
        ng = jax.nn.sigmoid(ng.reshape(b, s, N_NSA_HEADS, N_BRANCH))
        o_nsa = native_sparse_attention(nq, nk, nv, ng, nsa_k_gain[layer], nsa_cmp_pos[layer],
                                        nsa_cmp_w1[layer], nsa_cmp_w2[layer], rel_bias)
        y = jnp.concatenate([
            rms_norm(o_fox.reshape(b, s, FOX_WIDTH), mix_out_gain[layer, :FOX_WIDTH]),
            rms_norm(o_nsa.reshape(b, s, NSA_WIDTH), mix_out_gain[layer, FOX_WIDTH:]),
        ], axis=-1)
        x = x + g1 * (y @ w_out[layer])
        h2 = rms_norm(x, norm2_gain[layer]) * (1 + sc2) + sh2
        ffn = (jax.nn.silu(h2 @ ffn_w_gate[layer]) * (h2 @ ffn_w_up[layer])) @ ffn_w_down[layer]
        x = x + g2 * ffn
    return x


_drawn_inputs = setup_inputs


def setup_inputs(seed=0):
    import zlib

    import numpy as np

    out = dict(_drawn_inputs(seed))
    spreads = {}
    factors = {'norm1_gain': 7.249,
     'norm2_gain': 4.745,
     'fox_q_gain': 8.0,
     'fox_k_gain': 8.0,
     'nsa_q_gain': 8.0,
     'nsa_k_gain': 8.0,
     'rel_bias': 6.188,
     'mix_out_gain': 5.473}
    for name, (base, spread) in spreads.items():
        noise = np.random.default_rng([zlib.crc32(name.encode()), seed]).standard_normal(out[name].shape)
        drawn = base * np.exp(spread * noise) if base else spread * noise
        out[name] = jnp.asarray(drawn.astype(out[name].dtype))
    for name, factor in factors.items():
        out[name] = (out[name] * factor).astype(out[name].dtype)
    return out
```

```python
from contextlib import ExitStack

import numpy as np

import concourse.bass as bass
from concourse import mybir

F32 = mybir.dt.float32
F32R = mybir.dt.float32r
BF16 = mybir.dt.bfloat16
ALU = mybir.AluOpType
ACT = mybir.ActivationFunctionType
AX = mybir.AxisListType

P = 128
S = 512
ST = S // P
D = 2048
KT = D // P
NH = 8
DFF = 5632
NBUCKET, MAXDIST = 32, 128
CB, CS = 32, 16
NCMP = (S - CB) // CS + 1
SCALE = P ** -0.5
EPS = 1e-6
NEG = -1e30
C_FQ, C_FV, C_FF, C_NQ, C_NK = 0, 2048, 3072, 3080, 4104
C_NV = C_NK + 768
C_NG = C_NV + 768
NSMALL = 32
CK = 2
CW = 512
NSTAGE, NW = 4, 2
GCH = KT // CK
G_OUT, G_FF = 11, 15
NFB = DFF // CW
NREV, NFWD = 640, 992
R_C, R_N1, R_N2, R_MIX, R_FQ, R_FK, R_NQ, R_NK = 0, 16, 32, 48, 64, 65, 66, 67
NPAR = 70
TS = (3, 2, 1, 0)
S_AT = {3: (0, 0), 2: (1, 0), 1: (2, 0), 0: (2, 256)}
T_AT = {0: (3, 0), 1: (4, 0), 3: (4, 384), 2: (5, 0)}
T_SB = {0: 0, 1: 512, 3: 896, 2: 1024}
P_SB = {3: 0, 2: 512, 1: 896, 0: 1152}
ADA_STEPS = 128


def ada_plan():
    plan = {}
    for groups, first in ((range(0, 6), 0), (range(6, 11), ADA_STEPS // 2)):
        slots = [(g, j) for g in groups for j in range(GCH)]
        n = ADA_STEPS // 2
        for i, slot in enumerate(slots):
            plan[slot] = range(first + i * n // len(slots), first + (i + 1) * n // len(slots))
    return plan


def hybrid_layer(nc, A, out):
    with ExitStack() as ctx:
        base = (nc.sbuf_base + 63) // 64 * 64
        RH, RQ = base, base + 65536
        RW = RQ + 57344
        RX = RW + 32768
        RM = RX + 32768

        def at(name, shape, dt, offset):
            return nc.alloc_sbuf_tensor_at(name, shape, dt, offset=offset)

        def sem(name):
            return ctx.enter_context(nc.semaphore(name))

        hhi = at("hhi", [P, KT, S], F32R, RH)
        hlo = at("hlo", [P, KT, S], F32R, RH + 32768)
        ada_first = [at(f"ada_first{b}", [P, 2 * D], F32, RH + 16384 * b) for b in range(3)]
        onehot = at("onehot", [NBUCKET + 1, NREV + NFWD], F32, RH + 49152)
        line = at("line", [NH, NREV + NFWD], F32, RH + 49152 + 6656)
        cmp_bias = at("cmp_bias", [NCMP, NH, S], F32, RH)
        rel = at("rel", [P, NH, S], F32, RH + 16384)
        rel_rev = at("rel_rev", [P, NH, S], F32, RW)
        w1 = [at(f"w1_{b}", [P, CB, P], F32, RH + 32768 + 16384 * b) for b in range(2)]
        xt0 = at("xt0", [P, KT, S], F32, RQ)
        acc_first = at("acc_first", [P, 2 * D], F32, RQ + 32768)
        wsmall_hi = at("wsmall_hi", [P, KT, NSMALL], F32R, RQ + 49152)
        wsmall_lo = at("wsmall_lo", [P, KT, NSMALL], F32R, RQ + 51200)
        fl = at("fl", [NSMALL, S], F32, RQ + 53248)
        fl2 = at("fl2", [NSMALL, S], F32, RQ + 55296)
        acc_sq = at("acc_sq", [P, D], F32, RQ)
        fq = at("fq", [P, NH, S], F32, RQ)
        fk = at("fk", [P, NH, S], F32, RQ + 16384)
        fv = at("fv", [P, ST, 2 * CW], F32, RQ + 32768)
        nq = at("nq", [P, NH, S], F32, RQ + 16384)
        nk = at("nk", [P, NH, S], F32, RQ + 32768)
        nv = at("nv", [P, ST, CW], F32, RQ + 49152)
        silu_g = at("silu_g", [P, 4, S], F32, RQ)
        ghi = at("ghi", [P, 4, S], F32R, RQ + 8192)
        glo = at("glo", [P, 4, S], F32R, RQ + 16384)
        gfull = at("gfull", [P, 4, S], F32, RQ + 24576)
        ostage = at("ostage", [P, 2, ST, CW], F32, RQ + 32768)
        stage = at("stage", [P, NSTAGE, CK, CW], F32, RW)
        whi = at("whi", [P, NW, CK, CW], F32R, RW + 16384)
        wlo = at("wlo", [P, NW, CK, CW], F32R, RW + 24576)
        xnat = at("xnat", [P, ST, D], F32, RX)
        sq = at("sq", [P, 4, S], F32, RX)
        rb = at("rb", [P, 4, S], F32, RX + 8192)
        ada_ring = at("ada_ring", [P, 3, D // 2], F32, RX + 16384)
        wsmall = at("wsmall", [P, KT, NSMALL], F32, RX + 28672)
        prob = at("prob", [P, 1280], F32, RX + 16384)
        probT = at("probT", [P, 1280], F32, RX + 21504)
        probc = at("probc", [P, ST, NCMP + 1], F32, RX + 26624)
        probcT = at("probcT", [NCMP, S], F32, RX + 27136)
        o_sq = at("o_sq", [P, S], F32, RX)
        ssn = at("ssn", [P, S], F32, RX + 2048)
        fa = at("fa", [NH, S], F32, RX + 28672)
        fb = at("fb", [NH, S], F32, RX + 30720)
        sel = at("sel", [72, NH, P], BF16, RQ + 49152)
        cumb = at("cumb", [72, S], BF16, RQ + 51200)
        cumt = at("cumt", [NH, S], BF16, RQ + 52224)
        unfold = at("unfold", [P, 2, CB, 2 * NCMP], F32, RX)
        xT = at("xT", [P, KT, S], F32, RX)
        acc = at("acc", [P, 2, D], F32, RM)
        m = RM + 16384

        def small(name, shape, dt=F32):
            nonlocal m
            size = 4 if dt == F32 else 2
            for n in shape[1:]:
                size *= n
            t = at(name, shape, dt, m)
            m += (size + 31) // 32 * 32
            return t

        par = small("par", [P, NPAR])
        adab = small("adab", [P, 96])
        mod = small("mod", [P, 6, KT])
        fbias = small("fbias", [NH, 1])
        cpos = small("cpos", [P, 2 * CB])
        silu_c = small("silu_c", [P, KT])
        t16 = small("t16", [P, KT])
        ident = small("ident", [P, P])
        flip = small("flip", [P, P])
        flipc = small("flipc", [NCMP, NCMP])
        ones = small("ones", [P, P])
        identb = small("identb", [P, P], BF16)
        maskb = small("maskb", [P, P], BF16)
        eps = small("eps", [P, 1])
        ssx = small("ssx", [P, ST])
        rx = small("rx", [P, ST])
        nmax = small("nmax", [P, ST])
        psum_row = small("psum_row", [P, ST])
        rinv = small("rinv", [P, ST])
        cmax = small("cmax", [P, ST])
        csum = small("csum", [P, ST])
        gate = small("gate", [P, ST, NSMALL])
        rowok = small("rowok", [P, ST])
        kc = small("kc", [P, 2, NCMP + 1])
        vc = small("vc", [NCMP, 2, P])
        ssf = small("ssf", [P, S])
        assert m <= nc.sbuf_usable_end, m - nc.sbuf_usable_end
        parn = at("parn", [NPAR, P], F32, RM)
        adabn = at("adabn", [96, P], F32, RM + 512)
        cposn = at("cposn", [2 * CB, P], F32, RM + 1024)
        relb = at("relb", [NBUCKET + 1, NH], F32, RM + 1536)
        w2 = at("w2", [P, 2, P], F32, RX + 29184)
        hid = at("hid", [P, 2, 2 * NCMP], F32, RX + 30208)
        hid2 = at("hid2", [P, 2, 2 * NCMP], F32, RX + 30720)

        PS = ctx.enter_context(nc.psum_tensor("PS", [P, 8, S], F32))
        xT_d = nc.dram_tensor("xT_d", [P, KT * S], F32, kind="Internal").ap()
        line_d = nc.dram_tensor("line_d", [NH, NREV + NFWD], F32, kind="Internal").ap()

        consts = sem("consts")
        par_in, x_in, lines_in, small_in = sem("par_in"), sem("x_in"), sem("lines_in"), sem("small_in")
        first_in = [sem(f"ada_first_in{b}") for b in range(3)]
        par_t, par_done, act_s, dve_s = sem("par_t"), sem("par_done"), sem("act_self"), sem("dve_self")
        exp_c = sem("exp_c")
        first_acc = sem("first_acc")
        line_pe, line_sb, line_out = sem("line_pe"), sem("line_sb"), sem("line_out")
        xt_pe, xt_sb, xt_out = sem("xt_pe"), sem("xt_sb"), sem("xt_out")
        rx_done, xn_done, nt_pe, nt_sb = sem("rx_done"), sem("xn_done"), sem("nt_pe"), sem("nt_sb")
        mod_pe, mod_done = sem("mod_pe"), sem("mod_done")
        h_full, h_hi, h_lo = sem("h_full"), sem("h_hi"), sem("h_lo")
        ws_hi, ws_lo, small_pe = sem("ws_hi"), sem("ws_lo"), sem("small_pe")
        gates_e, z_done, fexp, forget_ready, gates_ready, gates_pe, gates_nat = (sem(n) for n in (
            "gates_exp", "z_done", "forget_exp", "forget_ready", "gates_ready", "gates_pe", "gates_nat"))
        stage_in = [sem(f"stage_in{b}") for b in range(NSTAGE)]
        split_in = [sem(f"split_in{b}") for b in range(NSTAGE)]
        w_hi, w_lo, w_used = sem("w_hi"), sem("w_lo"), sem("w_used")
        tile_done = sem("tile_done")
        bank_free = [sem(f"bank_free{b}") for b in range(8)]
        evac, sq_done, ss_pe, ln_done, r_done, norm_done = (sem(n) for n in (
            "evac", "sq_done", "ss_pe", "ln_done", "r_done", "norm_done"))
        ada_in = [sem(f"ada_in{b}") for b in range(3)]
        ada_acc = sem("ada_acc")
        sel_ready, ready_small = sem("sel_ready"), sem("ready_small")
        s_pe, s_max, s_exp, p_done, t_pe, t_act, t_dve, o_pe, o_sb, o_ssq, ss_acc = (sem(n) for n in (
            "scores_pe", "scores_max", "scores_exp", "probs_done", "transposed_pe", "transposed_act",
            "transposed_dve", "out_pe", "out_sb", "out_squared", "squares_summed"))
        rel_in, w1_in, unf, hid_pe, hid_exp, hid_done, kcv_pe, kc_copied, kc_sq, kc_ss, kc_r, kc_ready, vc_ready = (
            sem(n) for n in ("rel_in", "w1_in", "unfolded", "hid_pe", "hid_exp", "hid_done", "kcv_pe",
                             "kc_copied", "kc_squared", "kc_ss", "kc_r", "kc_ready", "vc_ready"))
        sc_pe, sc_sub, sc_exp, pc_done, pct_pe, pct_sb = (sem(n) for n in (
            "cmp_scores", "cmp_shifted", "cmp_exp", "cmp_probs", "cmp_transposed", "cmp_transposed_sb"))
        pv_done, ry_ln, rh_ln, kc_ln = (sem(n) for n in ("pv_done", "ry_ln", "rh_ln", "kc_ln"))
        flip_pe, flip_sb, cmpb_in = sem("flip_pe"), sem("flip_sb"), sem("cmpb_in")
        mod2_pe, mod2_done = sem("mod2_pe"), sem("mod2_done")
        y_full, y_hi, y_lo = sem("y_full"), sem("y_hi"), sem("y_lo")
        ssy_pe, ry_done = sem("ssy_pe"), sem("ry_done")
        xT_in, x1_sq, x1_acc = sem("xT_in"), sem("x1_sq"), sem("x1_acc")
        ssh_pe, rh_done, h2_t, h2_hi, h2_lo = sem("ssh_pe"), sem("rh_done"), sem("h2_t"), sem("h2_hi"), sem("h2_lo")
        g_hi, g_lo, pool_s = sem("g_hi"), sem("g_lo"), sem("pool_self")
        fin_pe, fin_sb = sem("fin_pe"), sem("fin_sb")
        out_sent = [sem(f"out_sent{b}") for b in range(2)]

        plan = ada_plan()
        w_in, w_o = A["w_in"][0], A["w_out"][0]
        w_in_t = w_in.rearrange("(k p) n -> p k n", p=P)
        ada_t = A["ada_w"][0].rearrange("(k p) n -> k p n", p=P)

        def group_cols(g):
            if g < 4:
                return [(C_FQ + CW * g, CW)]
            if g < 6:
                return [(C_FV + CW * (g - 4), CW)]
            if g < 8:
                return [(C_NQ + CW * (g - 6), CW)]
            if g == 8:
                return [(C_NK + 256, CW)]
            if g == 9:
                return [(C_NK, 256), (C_NV, 256)]
            return [(C_NV + 256, CW)]

        NATURAL = (4, 5, 10)
        NORMED = (0, 1, 2, 3, 6, 7, 8)

        def tile_of(g, t):
            if g < 2:
                return fq[:, 4 * g + t, :]
            if g < 4:
                return fk[:, 4 * (g - 2) + t, :]
            if g < 6:
                return fv[:, t, CW * (g - 4):CW * (g - 3)]
            if g < 8:
                return nq[:, 4 * (g - 6) + t, :]
            if g == 8:
                return nk[:, t, :]
            if g == 9:
                return nk[:, 4 + t, :]
            return nv[:, t, :]

        def gain_of(g, t):
            r = R_FQ if g < 2 else R_FK if g < 4 else R_NQ if g < 8 else R_NK + 1 + t // 2
            return par[:, r:r + 1]

        def bank(g, t):
            return 4 * (g % 2) + t

        def uses(g):
            return 1 + g // 2

        def normed_before(g):
            return 4 * sum(x < g for x in NORMED)

        def parts(t):
            return P_SB[t], P * (t + 1)

        UF = NH

        def await_tile(eng, g, t):
            if t < 3:
                eng.wait_ge(tile_done, 3 * g + t + 1)
            else:
                eng.wait_ge(w_used, GCH * (g + 1))

        def await_ff(eng, t, tiles, chunks):
            if t < 3:
                eng.wait_ge(tile_done, tiles + t + 1)
            else:
                eng.wait_ge(w_used, chunks)

        x1_sqt = at("x1_sqt", [P, 2, S], F32, RQ + 32768)
        h2t = at("h2t", [P, 4, S], F32, RQ + 40960)

        block = ctx.enter_context(nc.Block())

        @block.sync
        def _(sp):
            rows = [("c", R_C, 16), ("norm1_gain", R_N1, 16), ("norm2_gain", R_N2, 16), ("mix_out_gain", R_MIX, 16),
                    ("fox_q_gain", R_FQ, 1), ("fox_k_gain", R_FK, 1), ("nsa_q_gain", R_NQ, 1)]
            for name, r, n in rows:
                sp.dma_start(parn[r:r + n, :], A[name].rearrange("a (r d) -> (a r) d", d=P)).then_inc(par_in, 16)
            sp.dma_start(parn[R_NK:R_NK + 3, :], A["nsa_k_gain"][0]).then_inc(par_in, 16)
            sp.dma_start(adabn[:, :], A["ada_b"].rearrange("a (r d) -> (a r) d", d=P)).then_inc(par_in, 16)
            sp.dma_start(cposn[:, :], A["nsa_cmp_pos"][0].rearrange("a b d -> (a b) d")).then_inc(par_in, 16)
            sp.dma_start(fbias[:, :], A["fox_f_bias"].rearrange("a h -> h a")).then_inc(par_in, 16)
            for t in range(ST):
                sp.dma_start(xnat[:, t, :], A["x"][0, P * t:P * (t + 1), :]).then_inc(x_in, 16)
            for k in range(3):
                sp.dma_start(ada_first[k][:, :], ada_t[k, :, 0:2 * D]).then_inc(first_in[k], 16)
            sp.dma_start(relb[0:NBUCKET, :], A["rel_bias"]).then_inc(lines_in, 16)
            sp.dma_start(onehot[:, :], A["bucket_onehot"]).then_inc(lines_in, 16)
            for k in range(3, KT):
                sp.wait_ge(first_acc, k - 2)
                sp.dma_start(ada_first[k % 3][:, :], ada_t[k, :, 0:2 * D]).then_inc(first_in[k % 3], 16)
                if k == 6:
                    sp.wait_ge(line_sb, 4)
                    sp.dma_start(line_d, line[:, :]).then_inc(line_out, 16)
                if k == 9:
                    sp.wait_ge(xt_sb, KT)
                    sp.dma_start(xT_d, xt0[:, :, :].rearrange("p k s -> p (k s)")).then_inc(xt_out, 16)
            sp.wait_ge(nt_pe, KT)
            sp.dma_start(wsmall[:, :, 0:8], w_in_t[:, :, C_FF:C_FF + 8]).then_inc(small_in, 16)
            sp.dma_start(wsmall[:, :, 8:32], w_in_t[:, :, C_NG:C_NG + 24]).then_inc(small_in, 16)

            def ada(a):
                if a >= 3:
                    sp.wait_ge(ada_acc, a - 2)
                comp, k, half = 2 + a // 32, a % 32 // 2, a % 2
                c0 = D * comp + 1024 * half
                sp.dma_start(ada_ring[:, a % 3, :], ada_t[k, :, c0:c0 + 1024]).then_inc(ada_in[a % 3], 16)

            def free_stage(c):
                if c >= NSTAGE:
                    sp.wait_ge(w_lo, c - NSTAGE + 1)

            def project_in(g):
                for j in range(GCH):
                    c = GCH * g + j
                    free_stage(c)
                    pieces = group_cols(g)
                    if len(pieces) == 2:
                        for (c0, n), n0, landed in zip(pieces, (0, 256), (split_in, stage_in)):
                            sp.dma_start(stage[:, c % NSTAGE, :, n0:n0 + n],
                                         w_in_t[:, CK * j:CK * j + CK, c0:c0 + n]).then_inc(landed[c % NSTAGE], 16)
                    else:
                        c0, n = pieces[0]
                        sp.dma_start(stage[:, c % NSTAGE, :, :],
                                     w_in_t[:, CK * j:CK * j + CK, c0:c0 + n]).then_inc(stage_in[c % NSTAGE], 16)
                    for a in plan[g, j]:
                        ada(a)

            for g in range(6):
                project_in(g)
            for g in range(6, 11):
                if g == 6:
                    sp.wait_ge(pv_done, UF)
                project_in(g)

            sp.wait_ge(line_out, 16)
            sp.wait_ge(w_lo, 11 * GCH)
            for h in range(NH):
                at_h = h * (NREV + NFWD)
                sp.dma_start(rel_rev[:, h, :], bass.AP(tensor=line_d.tensor, offset=at_h,
                                                       ap=[[1, P], [1, S]])).then_inc(rel_in, 16)
            sp.wait_ge(w_used, 11 * GCH)
            for h in range(NH):
                at_h = h * (NREV + NFWD) + NREV + S - 1 - (CB - 1) - CS * (NCMP - 1)
                sp.dma_start(cmp_bias[:, h, :], bass.AP(tensor=line_d.tensor, offset=at_h,
                                                        ap=[[CS, NCMP], [1, S]])).then_inc(cmpb_in, 16)
            for b in range(2):
                sp.dma_start(w1[b][:, :, :], A["nsa_cmp_w1"][0, b].rearrange("(j d) n -> d j n", d=P)).then_inc(w1_in, 16)
            sp.dma_start(w2[:, :, :], A["nsa_cmp_w2"][0].rearrange("b d n -> d b n")).then_inc(w1_in, 16)

            sp.wait_ge(flip_pe, NH)
            w_o_t = w_o.rearrange("(k p) n -> p k n", p=P)
            for g in range(G_OUT, G_FF):
                for j in range(GCH):
                    c = GCH * g + j
                    free_stage(c)
                    c0 = CW * (g - G_OUT)
                    sp.dma_start(stage[:, c % NSTAGE, :, :],
                                 w_o_t[:, CK * j:CK * j + CK, c0:c0 + CW]).then_inc(stage_in[c % NSTAGE], 16)
                if g == G_OUT:
                    sp.wait_ge(y_full, KT)
                    sp.dma_start(xT[:, :, :].rearrange("p k s -> p (k s)"), xT_d).then_inc(xT_in, 16)

            gate_w = A["ffn_w_gate"][0].rearrange("(k p) n -> p k n", p=P)
            up_w = A["ffn_w_up"][0].rearrange("(k p) n -> p k n", p=P)
            down_w = A["ffn_w_down"][0].rearrange("(k p) n -> p k n", p=P)

            def columns(w, i, c):
                for j in range(GCH):
                    sp.wait_ge(w_lo, c + j - NSTAGE + 1)
                    sp.dma_start(stage[:, j % NSTAGE, :, :],
                                 w[:, CK * j:CK * j + CK, bass.ds(CW * i, CW)]).then_inc(stage_in[j % NSTAGE], 16)

            def rows_of_down(i, c):
                for j in range(GCH):
                    sp.wait_ge(w_lo, c + j - NSTAGE + 1)
                    c0 = CW * (j // 2)
                    sp.dma_start(stage[:, j % NSTAGE, :, :],
                                 down_w[:, bass.ds(4 * i + CK * (j % 2), CK), c0:c0 + CW]
                                 ).then_inc(stage_in[j % NSTAGE], 16)

            c = GCH * G_FF
            columns(gate_w, 0, c)
            with sp.Fori(0, NFB - 1) as i:
                at_i = c + GCH + 3 * GCH * i
                columns(up_w, i, at_i)
                columns(gate_w, i + 1, at_i + GCH)
                rows_of_down(i, at_i + 2 * GCH)
            last = c + GCH + 3 * GCH * (NFB - 1)
            columns(up_w, NFB - 1, last)
            rows_of_down(NFB - 1, last + GCH)

            out_t = out[0].rearrange("(t p) n -> p t n", p=P)
            for dg in range(4):
                sp.wait_ge(fin_sb, 4 * (dg + 1))
                sp.dma_start(out_t[:, :, CW * dg:CW * (dg + 1)], ostage[:, dg % 2, :, :]).then_inc(out_sent[dg % 2], 16)
            for b in range(2):
                sp.wait_ge(out_sent[b], 32)

        @block.tensor
        def _(pe):
            mm, tr = nc.tensor.matmul, nc.tensor.transpose

            pe.wait_ge(consts, 1)
            pe.wait_ge(par_in, 11 * 16)
            tr(PS[:, 0, 0:NPAR], parn[:, :], ident[0:NPAR, 0:NPAR]).then_inc(par_t, 1)
            tr(PS[:, 1, 0:96], adabn[:, :], ident[0:96, 0:96]).then_inc(par_t, 1)
            tr(PS[:, 2, 0:2 * CB], cposn[:, :], ident[0:2 * CB, 0:2 * CB]).then_inc(par_t, 1)
            pe.wait_ge(x_in, 16 * ST)
            for k in range(KT):
                if k == 0:
                    pe.wait_ge(par_done, 3)
                if k >= 8:
                    pe.wait_ge(xt_sb, k - 7)
                for t in range(ST):
                    last = tr(PS[:, k % 8, P * t:P * (t + 1)], xnat[:, t, P * k:P * (k + 1)], ident[:, :])
                last.then_inc(xt_pe, 1)
            pe.wait_ge(lines_in, 32)
            pe.wait_ge(xt_sb, KT)
            n = (NREV + NFWD) // 4
            for b in range(4):
                mm(PS[0:NH, b, 0:n], relb[:, :], onehot[:, n * b:n * (b + 1)], start=True, stop=True).then_inc(line_pe, 1)
            pe.wait_ge(xn_done, ST)
            pe.wait_ge(line_sb, 4)
            for k in range(KT):
                if k >= 8:
                    pe.wait_ge(nt_sb, k - 7)
                for t in range(ST):
                    last = tr(PS[:, k % 8, P * t:P * (t + 1)], xnat[:, t, P * k:P * (k + 1)], ident[:, :])
                last.then_inc(nt_pe, 1)
            pe.wait_ge(nt_sb, KT)
            pe.wait_ge(first_acc, KT)
            for comp in range(2):
                for k in range(KT):
                    c0 = D * comp + P * k
                    last = mm(PS[:, 7, KT * comp + k:KT * comp + k + 1], acc_first[:, c0:c0 + P], ones[:, 0:1],
                              start=True, stop=True)
            last.then_inc(mod_pe, 1)
            pe.wait_ge(ws_lo, 1)
            for k in range(KT):
                pe.wait_ge(h_lo, k + 1)
                mm(PS[0:NSMALL, 6, :], wsmall_hi[:, k, :], hhi[:, k, :], start=(k == 0), stop=False)
                mm(PS[0:NSMALL, 6, :], wsmall_hi[:, k, :], hlo[:, k, :], start=False, stop=False)
                last = mm(PS[0:NSMALL, 6, :], wsmall_lo[:, k, :], hhi[:, k, :], start=False, stop=(k == KT - 1))
            last.then_inc(small_pe, 1)

            def columns_tile(b, slot, kk, t, k, start, stop, rhi=None, rlo=None):
                cols = slice(P * t, P * (t + 1))
                rhi = hhi[:, k, :] if rhi is None else rhi
                rlo = hlo[:, k, :] if rlo is None else rlo
                mm(PS[:, b, :], whi[:, slot, kk, cols], rhi, start=start, stop=False)
                mm(PS[:, b, :], whi[:, slot, kk, cols], rlo, start=False, stop=False)
                return mm(PS[:, b, :], wlo[:, slot, kk, cols], rhi, start=False, stop=stop)

            def tokens_tile(b, slot, kk, t, k, start, stop):
                rows = slice(P * t, P * (t + 1))
                mm(PS[:, b, :], hhi[:, k, rows], whi[:, slot, kk, :], start=start, stop=False)
                mm(PS[:, b, :], hhi[:, k, rows], wlo[:, slot, kk, :], start=False, stop=False)
                return mm(PS[:, b, :], hlo[:, k, rows], whi[:, slot, kk, :], start=False, stop=stop)

            def gemm(c, first_bank, free, tile, chunks=GCH, mid=None, before=None):
                for j in range(chunks):
                    pe.wait_ge(w_lo, c + j + 1)
                    for t in range(4):
                        if j == 0:
                            pe.wait_ge(bank_free[first_bank + t], free)
                        for kk in range(CK):
                            k = CK * j + kk
                            if before is not None and t == 0:
                                before(k)
                            last = tile(first_bank + t, j % NW, kk, t, k, k == 0, k == CK * chunks - 1)
                        if j == chunks - 1 and t < 3:
                            last.then_inc(tile_done, 1)
                    last.then_inc(w_used, 1)
                    if mid is not None and j == 3:
                        mid()

            def squares(g):
                for t in range(4):
                    n = normed_before(g) + t + 1
                    pe.wait_ge(sq_done, n)
                    mm(PS[:, bank(g, t), :], ones[:, :], sq[:, t, :], start=True, stop=True).then_inc(ss_pe, 1)

            def project_in(g):
                mid = (lambda: squares(g - 1)) if g - 1 in NORMED and g != 6 else None
                gemm(GCH * g, bank(g, 0), uses(g), tokens_tile if g in NATURAL else columns_tile, mid=mid)

            def scores(u, q_of, k_of, bias=None):
                for i, t in enumerate(TS):
                    b, c0 = S_AT[t]
                    n = P * (t + 1)
                    o = PS[:, b, c0:c0 + n]
                    last = mm(o, q_of(t), k_of(n), start=True, stop=bias is None)
                    if bias is not None:
                        last = bias(o, t, n)
                    last.then_inc(s_pe, 1)

            def transposes(u):
                for i, t in enumerate(TS):
                    pe.wait_ge(p_done, 4 * u + i + 1)
                    for kb in range(t + 1):
                        b, c0 = T_AT[kb]
                        c0 += P * (t - kb)
                        c1 = parts(t)[0] + P * kb
                        last = tr(PS[:, b, c0:c0 + P], prob[:, c1:c1 + P], ident[:, :])
                    last.then_inc(t_pe, 1)

            def values(u, v_of, start, stop):
                pe.wait_ge(t_act, u + 1)
                pe.wait_ge(t_dve, 2 * (u + 1))
                for kb in range(4):
                    n = S - P * kb
                    last = mm(PS[:, 6, P * kb:S], v_of(kb), probT[:, T_SB[kb]:T_SB[kb] + n],
                              start=start and kb == 0, stop=stop and kb == 3)
                return last

            for g in range(6):
                project_in(g)

            pe.wait_ge(sel_ready, 1)
            pe.wait_ge(forget_ready, 3)
            pe.wait_ge(gates_ready, 1)
            for b in range(8):
                pe.wait_ge(bank_free[b], uses(6 + b // 4))
            pe.wait_ge(norm_done, 16)
            for t in range(ST):
                last = tr(PS[:, 7, NSMALL * t:NSMALL * (t + 1)], fl2[:, P * t:P * (t + 1)],
                          ident[0:NSMALL, 0:NSMALL])
            last.then_inc(gates_pe, 1)
            pe.wait_ge(ada_acc, ADA_STEPS // 2)
            for n in range(2 * KT):
                last = mm(PS[:, 7, 128 + n:129 + n], acc[:, n // KT, P * (n % KT):P * (n % KT + 1)],
                          ones[:, 0:1], start=True, stop=True)
            last.then_inc(mod2_pe, 1)

            def fox_scores(h):
                def bias(o, t, n):
                    mm(o, sel[:, h, :], cumb[:, 0:n], start=False, stop=False)
                    return mm(o[:, n - P:n], identb[:, :], maskb[:, :], start=False, stop=True)

                scores(h, lambda t: fq[:, h, P * t:P * (t + 1)], lambda n: fk[:, h, 0:n], bias)

            fox_scores(0)
            for h in range(NH):
                transposes(h)
                if h + 1 < NH:
                    fox_scores(h + 1)
                if h >= 1:
                    pe.wait_ge(o_sb, h)
                values(h, lambda kb, h=h: fv[:, kb, P * h:P * (h + 1)], True, True).then_inc(pv_done, 1)
            pe.wait_ge(ss_acc, NH)
            pe.wait_ge(gates_nat, 1)
            pe.wait_ge(mod2_done, 1)
            mm(PS[:, 7, :], ones[:, :], ssf[:, :], start=True, stop=True).then_inc(ssy_pe, 1)

            pe.wait_ge(o_sb, NH)
            pe.wait_ge(ry_done, 1)
            for g in range(6, 11):
                project_in(g)

            for b in range(8):
                pe.wait_ge(bank_free[b], uses(12 - b // 4))
            pe.wait_ge(rel_in, 16 * NH)
            for h in range(NH):
                if h >= 3:
                    pe.wait_ge(flip_sb, h - 2)
                mm(PS[:, 4 + h % 3, :], flip[:, :], rel_rev[:, h, :], start=True, stop=True).then_inc(flip_pe, 1)
            pe.wait_ge(w1_in, 48)
            pe.wait_ge(unf, 2)
            for b in range(2):
                for j in range(CB):
                    last = mm(PS[:, b, 0:2 * NCMP], w1[b][:, j, :], unfold[:, b, j, :],
                              start=(j == 0), stop=(j == CB - 1))
                last.then_inc(hid_pe, 1)
            pe.wait_ge(hid_done, 1)
            mm(PS[:, 2, 0:2 * NCMP], w2[:, 0, :], hid[:, 0, :], start=True, stop=True).then_inc(kcv_pe, 1)
            pe.wait_ge(hid_done, 2)
            for kv in range(2):
                mm(PS[0:NCMP, 3, P * kv:P * (kv + 1)], hid[:, 1, NCMP * kv:NCMP * (kv + 1)], w2[:, 1, :],
                   start=True, stop=True).then_inc(kcv_pe, 1)
            pe.wait_ge(kc_sq, 1)
            mm(PS[:, 2, 64:64 + 2 * NCMP], ones[:, :], hid2[:, 0, :], start=True, stop=True).then_inc(kc_ss, 1)
            pe.wait_ge(ada_acc, ADA_STEPS)
            for n in range(2 * KT):
                last = mm(PS[:, 7, 128 + n:129 + n], acc[:, n // KT, P * (n % KT):P * (n % KT + 1)],
                          ones[:, 0:1], start=True, stop=True)
            last.then_inc(mod2_pe, 1)
            pe.wait_ge(norm_done, 28)
            pe.wait_ge(kc_ready, 1)
            pe.wait_ge(vc_ready, 1)
            pe.wait_ge(mod2_done, 2)

            def nsa_scores(h, win):
                kv = h // 4
                scores(UF + 2 * h + win, lambda t: nq[:, h, P * t:P * (t + 1)],
                       lambda n: nk[:, 2 * win + kv, 0:n])

            def cmp_scores(h):
                if h >= 1:
                    pe.wait_ge(pct_sb, h)
                for t in range(ST):
                    o = PS[:, 7, NSMALL * t:NSMALL * t + NCMP]
                    mm(o, nq[:, h, P * t:P * (t + 1)], kc[:, h // 4, 0:NCMP], start=True, stop=False)
                    last = mm(o, cmp_bias[:, h, P * t:P * (t + 1)], flipc[:, :], start=False, stop=True)
                last.then_inc(sc_pe, 1)

            pe.wait_ge(flip_sb, NH)
            pe.wait_ge(cmpb_in, 16 * NH)
            nsa_scores(0, 0)
            for h in range(NH):
                kv = h // 4
                for win in range(2):
                    u = UF + 2 * h + win
                    transposes(u)
                    if win == 0:
                        nsa_scores(h, 1)
                        cmp_scores(h)
                        if h >= 1:
                            pe.wait_ge(o_sb, UF + h)
                    else:
                        if h + 1 < NH:
                            nsa_scores(h + 1, 0)
                        pe.wait_ge(pc_done, h + 1)
                        for t in range(ST):
                            last = tr(PS[0:NCMP, 7, P * t:P * (t + 1)], probc[:, t, 0:NCMP], ident[:, :])
                        last.then_inc(pct_pe, 1)
                    values(u, lambda kb, c0=2 * P * win + P * kv: nv[:, kb, c0:c0 + P], win == 0, False).then_inc(pv_done, 1)
                pe.wait_ge(pct_sb, h + 1)
                mm(PS[:, 6, :], vc[:, kv, :], probcT[:, :], start=False, stop=True).then_inc(o_pe, 1)
            pe.wait_ge(ss_acc, 2 * NH)
            mm(PS[:, 7, :], ones[:, :], ssn[:, :], start=True, stop=True).then_inc(ssy_pe, 1)

            pe.wait_ge(o_sb, 2 * NH)
            pe.wait_ge(ry_done, 2)
            for g in range(G_OUT, G_FF):
                gemm(GCH * g, bank(g, 0), uses(g), columns_tile,
                     before=(lambda k: pe.wait_ge(y_lo, k + 1)) if g == G_OUT else None)
            pe.wait_ge(x1_acc, KT)
            pe.wait_ge(bank_free[0], uses(16))
            mm(PS[:, 0, :], ones[:, :], ssf[:, :], start=True, stop=True).then_inc(ssh_pe, 1)
            pe.wait_ge(rh_done, 1)

            def down_tile(half):
                def tile(b, slot, kk, t, k, start, stop):
                    f = CK * half + kk
                    return columns_tile(b, slot, kk, t, k, half == 0 and kk == 0, half == 1 and kk == 1,
                                        ghi[:, f, :], glo[:, f, :])
                return tile

            def down_blocks(c, used, lots):
                pe.wait_ge(g_lo, lots)
                for dg in range(4):
                    first = 4 * (dg % 2)
                    for half in range(2):
                        j = 2 * dg + half
                        pe.wait_ge(w_lo, c + j + 1)
                        for t in range(4):
                            if half == 0:
                                pe.wait_ge(bank_free[first + t], used[dg % 2] + dg // 2)
                            for kk in range(CK):
                                last = down_tile(half)(first + t, j % NW, kk, t, 0, None, None)
                            if half == 1 and t < 3:
                                last.then_inc(tile_done, 1)
                        last.then_inc(w_used, 1)

            c = GCH * G_FF
            gemm(c, 4, uses(15), columns_tile, before=lambda k: pe.wait_ge(h2_lo, k + 1))
            with pe.Fori(0, NFB - 1) as i:
                at_i = c + GCH + 3 * GCH * i
                gemm(at_i, 0, uses(16) + 3 * i, columns_tile)
                gemm(at_i + GCH, 4, uses(15) + 1 + 3 * i, columns_tile)
                down_blocks(at_i + 2 * GCH, (uses(16) + 1 + 3 * i, uses(15) + 2 + 3 * i), 4 * i + 4)
            n = NFB - 1
            last_c = c + GCH + 3 * GCH * n
            gemm(last_c, 0, uses(16) + 3 * n, columns_tile)
            down_blocks(last_c + GCH, (uses(16) + 1 + 3 * n, uses(15) + 1 + 3 * n), 4 * n + 4)
            for dg in range(4):
                for t in range(4):
                    pe.wait_ge(bank_free[t], uses(16) + 3 * n + 3)
                    if dg >= 1:
                        pe.wait_ge(bank_free[4 + t], uses(15) + 3 * n + 3)
                for t in range(ST):
                    b = 4 * (dg % 2) + t
                    if dg >= 2:
                        pe.wait_ge(fin_sb, 4 * (dg - 2) + t + 1)
                    for d in range(4):
                        last = tr(PS[:, b, P * d:P * (d + 1)], xT[:, 4 * dg + d, P * t:P * (t + 1)], ident[:, :])
                    last.then_inc(fin_pe, 1)

        @block.scalar
        def _(act):
            f = nc.scalar.activation
            act.preload_act_table_set("natural_log_exp_and_others")
            act.wait_ge(consts, 1)
            act.wait_ge(x_in, 16 * ST)
            for t in range(ST):
                f(acc_sq[:, :], xnat[:, t, :], ACT.Square, accum_out=ssx[:, t:t + 1]).then_inc(act_s, 1)
                act.wait_ge(act_s, t + 1)
            f(rx[:, :], ssx[:, :], ACT.Ln, bias=eps[:, :], scale=1.0 / D).then_inc(act_s, 1)
            act.wait_ge(act_s, ST + 1)
            f(rx[:, :], rx[:, :], ACT.Exp, scale=-0.5).then_inc(rx_done, 1)
            act.wait_ge(par_done, 3)
            f(t16[:, :], par[:, R_C:R_C + KT], ACT.Exp, scale=-1.0).then_inc(exp_c, 1)
            for k in range(KT):
                act.wait_ge(xt_pe, k + 1)
                f(xt0[:, k, :], PS[:, k % 8, :], ACT.Copy).then_inc(xt_sb, 1)
            for b in range(4):
                act.wait_ge(line_pe, b + 1)
                n = (NREV + NFWD) // 4
                f(line[:, n * b:n * (b + 1)], PS[0:NH, b, 0:n], ACT.Copy).then_inc(line_sb, 1)
            act.wait_ge(xt_out, 16)
            for k in range(KT):
                act.wait_ge(nt_pe, k + 1)
                f(xt0[:, k, :], PS[:, k % 8, :], ACT.Copy).then_inc(nt_sb, 1)
            act.wait_ge(nt_sb, KT)
            for b in range(6):
                act.sem_inc(bank_free[b], 1)
            act.wait_ge(small_in, 32)
            f(wsmall_hi[:, :, :], wsmall[:, :, :], ACT.Copy).then_inc(ws_hi, 1)

            def hi(c):
                if c // GCH == 9:
                    act.wait_ge(split_in[c % NSTAGE], 16 * (c % GCH // NSTAGE + 1))
                act.wait_ge(stage_in[c % NSTAGE], 16 * (c // NSTAGE + 1))
                if c >= NW:
                    act.wait_ge(w_used, c - NW + 1)
                f(whi[:, c % NW, :, :], stage[:, c % NSTAGE, :, :], ACT.Copy).then_inc(w_hi, 1)

            def hi_at(c, j):
                act.wait_ge(stage_in[j % NSTAGE], (c + j - j % NSTAGE) * 4 + 16)
                act.wait_ge(w_used, c + j - NW + 1)
                f(whi[:, j % NW, :, :], stage[:, j % NSTAGE, :, :], ACT.Copy).then_inc(w_hi, 1)

            def square_tiles(g):
                for t in range(4):
                    act.wait_ge(evac, normed_before(g) + t + 1)
                    f(sq[:, t, :], PS[:, bank(g, t), :], ACT.Square).then_inc(sq_done, 1)

            def norm_factors(g):
                for t in range(4):
                    n = normed_before(g) + t + 1
                    act.wait_ge(ss_pe, n)
                    if n > 4:
                        act.wait_ge(norm_done, n - 4)
                    b = bank(g, t)
                    f(rb[:, t, :], PS[:, b, :], ACT.Ln, bias=eps[:, :], scale=1.0 / P).then_inc(bank_free[b], 1)
                    act.wait_ge(bank_free[b], uses(g + 2))
                    f(rb[:, t, :], rb[:, t, :], ACT.Exp, scale=-0.5).then_inc(r_done, 1)

            def project_in(g):
                for j in range(GCH):
                    hi(GCH * g + j)
                    if g - 1 in NORMED and j == 1:
                        square_tiles(g - 1)
                    if g - 1 in NORMED and j == 5:
                        norm_factors(g - 1)

            for k in range(KT):
                act.wait_ge(h_full, k + 1)
                f(hhi[:, k, :], xt0[:, k, :], ACT.Copy).then_inc(h_hi, 1)
                if k == 3:
                    hi(0)
                    hi(1)
            act.wait_ge(small_pe, 1)
            f(fl2[:, :], PS[0:NSMALL, 6, :], ACT.Exp, scale=-1.0).then_inc(gates_e, 1)
            act.wait_ge(z_done, 1)
            f(fb[:, :], fb[:, :], ACT.Exp, scale=-1.0).then_inc(fexp, 1)
            act.wait_ge(fexp, 1)
            f(fb[:, :], fb[:, :], ACT.Ln, bias=ones[0:NH, 0:1]).then_inc(fexp, 1)

            for j in range(2, GCH):
                hi(j)
            for g in range(1, 6):
                project_in(g)

            def exp_tiles(u, fox):
                for i, t in enumerate(TS):
                    b, c0 = S_AT[t]
                    p0, n = parts(t)
                    act.wait_ge(s_max, 4 * u + (4 if fox and i == 2 else i + 1))
                    src = PS[:, b, c0:c0 + n] if fox else prob[:, p0:p0 + n]
                    f(prob[:, p0:p0 + n], src, ACT.Exp, bias=nmax[:, t:t + 1], scale=1.0 if fox else -1.0,
                      accum_out=psum_row[:, t:t + 1]).then_inc(s_exp, 1)

            def transposed_out(u):
                act.wait_ge(t_pe, 4 * (u + 1))
                if u >= 1:
                    act.wait_ge(pv_done, u)
                f(probT[:, 0:S], PS[:, 3, :], ACT.Copy).then_inc(t_act, 1)

            def head_out(n, dst):
                if n < UF:
                    act.wait_ge(pv_done, n + 1)
                else:
                    act.wait_ge(o_pe, n - UF + 1)
                f(dst, PS[:, 6, :], ACT.Copy)
                if n >= 1:
                    act.wait_ge(ss_acc, n)
                f(o_sq[:, :], PS[:, 6, :], ACT.Square).then_inc(o_sb, 1)

            def mean_factor(n, dst, width):
                act.wait_ge(ssy_pe, n)
                f(dst[:, :], PS[:, 7, :], ACT.Ln, bias=eps[:, :], scale=1.0 / width).then_inc(ry_ln, 1)
                act.wait_ge(ry_ln, n)
                f(dst[:, :], dst[:, :], ACT.Exp, scale=-0.5).then_inc(ry_done, 1)

            exp_tiles(0, True)
            for h in range(NH):
                transposed_out(h)
                if h + 1 < NH:
                    exp_tiles(h + 1, True)
                head_out(h, fq[:, h, :])
            mean_factor(1, ssf, NH * P)

            for g in range(6, 11):
                project_in(g)

            for h in range(NH):
                act.wait_ge(flip_pe, h + 1)
                f(rel[:, h, :], PS[:, 4 + h % 3, :], ACT.Copy).then_inc(flip_sb, 1)
            for b in range(2):
                act.wait_ge(hid_pe, b + 1)
                f(hid2[:, b, :], PS[:, b, 0:2 * NCMP], ACT.Exp, scale=-1.0).then_inc(hid_exp, 1)
            act.wait_ge(kcv_pe, 3)
            act.wait_ge(kc_copied, 1)
            f(hid2[:, 0, :], PS[:, 2, 0:2 * NCMP], ACT.Square).then_inc(kc_sq, 1)
            act.wait_ge(kc_ss, 1)
            f(hid2[:, 1, :], PS[:, 2, 64:64 + 2 * NCMP], ACT.Ln, bias=eps[:, :], scale=1.0 / P).then_inc(kc_ln, 1)
            act.wait_ge(kc_ln, 1)
            f(hid2[:, 1, :], hid2[:, 1, :], ACT.Exp, scale=-0.5).then_inc(kc_r, 1)

            exp_tiles(UF, False)
            for h in range(NH):
                for win in range(2):
                    u = UF + 2 * h + win
                    transposed_out(u)
                    if win == 0:
                        exp_tiles(u + 1, False)
                        act.wait_ge(sc_sub, h + 1)
                        f(probc[:, :, 0:NCMP], probc[:, :, 0:NCMP], ACT.Exp).then_inc(sc_exp, 1)
                    else:
                        if h + 1 < NH:
                            exp_tiles(u + 1, False)
                        act.wait_ge(pct_pe, h + 1)
                        f(probcT[:, :], PS[0:NCMP, 7, :], ACT.Copy).then_inc(pct_sb, 1)
                head_out(UF + h, nq[:, h, :])
            mean_factor(2, ssn, NH * P)

            for k in range(KT):
                act.wait_ge(y_full, k + 1)
                src = fq[:, k, :] if k < NH else nq[:, k - NH, :]
                f(hhi[:, k, :], src, ACT.Copy).then_inc(y_hi, 1)
                if k == 1:
                    hi(GCH * G_OUT)
                    hi(GCH * G_OUT + 1)

            def square_x1(g):
                for t in range(4):
                    n = 4 * (g - G_OUT) + t
                    act.wait_ge(bank_free[bank(g, t)], uses(g + 2))
                    if n >= 2:
                        act.wait_ge(x1_acc, n - 1)
                    f(x1_sqt[:, n % 2, :], xT[:, n, :], ACT.Square).then_inc(x1_sq, 1)

            for g in range(G_OUT, G_FF):
                for j in range(2 if g == G_OUT else 0, GCH):
                    hi(GCH * g + j)
                    if g > G_OUT and j == 1:
                        square_x1(g - 1)
            c = GCH * G_FF
            hi(c)
            hi(c + 1)
            square_x1(G_FF - 1)
            act.wait_ge(ssh_pe, 1)
            f(ssf[:, :], PS[:, 0, :], ACT.Ln, bias=eps[:, :], scale=1.0 / D).then_inc(rh_ln, 1)
            act.wait_ge(rh_ln, 1)
            f(ssf[:, :], ssf[:, :], ACT.Exp, scale=-0.5).then_inc(rh_done, 1)
            for k in range(KT):
                act.wait_ge(h2_t, k + 1)
                f(hhi[:, k, :], h2t[:, k % 4, :], ACT.Identity, bias=mod[:, 3, k:k + 1]).then_inc(h2_hi, 1)

            def silu_tiles(tiles, chunks):
                for t in range(4):
                    await_ff(act, t, tiles, chunks)
                    f(silu_g[:, t, :], PS[:, 4 + t, :], ACT.Silu).then_inc(bank_free[4 + t], 1)

            def high_of_g(i):
                for t in range(4):
                    act.wait_ge(bank_free[t], uses(16) + 3 * i + 1)
                    f(ghi[:, t, :], gfull[:, t, :], ACT.Copy).then_inc(g_hi, 1)

            for j in range(2, GCH + 2):
                hi(c + j)
            silu_tiles(3 * G_FF, c + GCH)
            with act.Fori(0, NFB - 1) as i:
                at_i = c + GCH + 3 * GCH * i
                for j in range(2, 3 * GCH + 2):
                    hi_at(at_i, j)
                    if j == GCH + 2:
                        high_of_g(i)
                    if j == 2 * GCH + 1:
                        silu_tiles(3 * (G_FF + 2) + 18 * i, at_i + 2 * GCH)
            n = NFB - 1
            at_n = c + GCH + 3 * GCH * n
            for j in range(2, 2 * GCH):
                hi(at_n + j)
                if j == GCH + 1:
                    high_of_g(n)
            for dg in range(4):
                for t in range(ST):
                    act.wait_ge(fin_pe, 4 * dg + t + 1)
                    if dg >= 2:
                        act.wait_ge(out_sent[dg % 2], 16)
                    f(ostage[:, dg % 2, t, :], PS[:, 4 * (dg % 2) + t, :], ACT.Copy).then_inc(fin_sb, 1)

        @block.vector
        def _(dve):
            v = nc.vector
            own = [0]

            def then(ins):
                own[0] += 1
                ins.then_inc(dve_s, 1)
                dve.wait_ge(dve_s, own[0])

            dve.wait_ge(par_t, 3)
            v.tensor_copy(par[:, :], PS[:, 0, 0:NPAR]).then_inc(par_done, 1)
            v.tensor_copy(adab[:, :], PS[:, 1, 0:96]).then_inc(par_done, 1)
            v.tensor_copy(cpos[:, :], PS[:, 2, 0:2 * CB]).then_inc(par_done, 1)
            dve.wait_ge(par_done, 3)
            then(v.tensor_scalar(par[:, R_FQ:R_FQ + 1], par[:, R_FQ:R_FQ + 1], SCALE, None, ALU.mult))
            then(v.tensor_scalar(par[:, R_NQ:R_NQ + 1], par[:, R_NQ:R_NQ + 1], SCALE, None, ALU.mult))
            dve.wait_ge(exp_c, 1)
            then(v.tensor_scalar(t16[:, :], t16[:, :], 1.0, None, ALU.add))
            then(v.reciprocal(t16[:, :], t16[:, :]))
            then(v.tensor_tensor(silu_c[:, :], t16[:, :], par[:, R_C:R_C + KT], ALU.mult))
            for k in range(KT):
                dve.wait_ge(first_in[k % 3], 16 * (k // 3 + 1))
                if k == 0:
                    v.tensor_scalar(acc_first[:, :], ada_first[0][:, :], silu_c[:, 0:1], None,
                                    ALU.mult).then_inc(first_acc, 1)
                else:
                    dve.wait_ge(first_acc, k)
                    v.scalar_tensor_tensor(out=acc_first[:, :], in0=ada_first[k % 3][:, :], scalar=silu_c[:, k:k + 1],
                                           in1=acc_first[:, :], op0=ALU.mult, op1=ALU.add).then_inc(first_acc, 1)
                if k == 5:
                    dve.wait_ge(rx_done, 1)
                    dve.wait_ge(xt_pe, KT)
                    for t in range(ST):
                        v.tensor_scalar(xnat[:, t, :], xnat[:, t, :], rx[:, t:t + 1], None,
                                        ALU.mult).then_inc(xn_done, 1)
            dve.wait_ge(mod_pe, 1)
            then(v.tensor_tensor(mod[:, 0:2, :], PS[:, 7, 0:2 * KT].rearrange("p (c k) -> p c k", c=2),
                                 adab[:, 0:2 * KT].rearrange("p (c k) -> p c k", c=2), ALU.add))
            then(v.scalar_tensor_tensor(out=mod[:, 1, :], in0=mod[:, 1, :], scalar=1.0, in1=par[:, R_N1:R_N1 + KT],
                                        op0=ALU.add, op1=ALU.mult))
            dve.sem_inc(bank_free[7], 1)
            for k in range(KT + 1):
                if k < KT:
                    v.tensor_scalar(xt0[:, k, :], xt0[:, k, :], mod[:, 1, k:k + 1], mod[:, 0, k:k + 1],
                                    ALU.mult, ALU.add).then_inc(h_full, 1)
                if k == 0:
                    dve.wait_ge(ws_hi, 1)
                    v.tensor_tensor(wsmall_lo[:, :, :], wsmall[:, :, :], wsmall_hi[:, :, :].bitcast(F32),
                                    ALU.subtract).then_inc(ws_lo, 1)
                if k >= 1:
                    dve.wait_ge(h_hi, k)
                    v.tensor_tensor(hlo[:, k - 1, :], xt0[:, k - 1, :], hhi[:, k - 1, :].bitcast(F32),
                                    ALU.subtract).then_inc(h_lo, 1)

            def lo(c):
                dve.wait_ge(w_hi, c + 1)
                v.tensor_tensor(wlo[:, c % NW, :, :], stage[:, c % NSTAGE, :, :], whi[:, c % NW, :, :].bitcast(F32),
                                ALU.subtract).then_inc(w_lo, 1)

            def lo_at(c, j):
                dve.wait_ge(w_hi, c + j + 1)
                v.tensor_tensor(wlo[:, j % NW, :, :], stage[:, j % NSTAGE, :, :], whi[:, j % NW, :, :].bitcast(F32),
                                ALU.subtract).then_inc(w_lo, 1)

            def ada(a):
                k, half = a % 32 // 2, a % 2
                part = acc[:, a // 32 % 2, 1024 * half:1024 * (half + 1)]
                dve.wait_ge(ada_in[a % 3], 16 * (a // 3 + 1))
                src = ada_ring[:, a % 3, :]
                if k == 0:
                    v.tensor_scalar(part, src, silu_c[:, 0:1], None, ALU.mult).then_inc(ada_acc, 1)
                else:
                    dve.wait_ge(ada_acc, a - 1)
                    v.scalar_tensor_tensor(out=part, in0=src, scalar=silu_c[:, k:k + 1], in1=part,
                                           op0=ALU.mult, op1=ALU.add).then_inc(ada_acc, 1)

            def tiles_out(g):
                for t in range(4):
                    await_tile(dve, g, t)
                    if g in NORMED:
                        v.tensor_scalar(tile_of(g, t), PS[:, bank(g, t), :], gain_of(g, t), None,
                                        ALU.mult).then_inc(evac, 1)
                    else:
                        v.tensor_copy(tile_of(g, t), PS[:, bank(g, t), :]).then_inc(bank_free[bank(g, t)], 1)

            def normalise(g):
                for t in range(4):
                    dve.wait_ge(r_done, normed_before(g) + t + 1)
                    v.tensor_tensor(tile_of(g, t), tile_of(g, t), rb[:, t, :], ALU.mult).then_inc(norm_done, 1)

            def project_in(g, first=0):
                for j in range(first, GCH):
                    lo(GCH * g + j)
                    for a in plan[g, j]:
                        ada(a)
                    if g not in (0, 6) and j == 1:
                        tiles_out(g - 1)
                    if g - 1 in NORMED and j == 6:
                        normalise(g - 1)

            lo(0)
            for a in plan[0, 0]:
                ada(a)
            lo(1)
            for a in plan[0, 1]:
                ada(a)
            dve.wait_ge(gates_e, 1)
            then(v.tensor_scalar(fl[0:NH, :], PS[0:NH, 6, :], fbias[:, :], None, ALU.add))
            dve.sem_inc(bank_free[6], 1)
            then(v.tensor_scalar(fa[:, :], fl[0:NH, :], -1.0, None, ALU.mult))
            v.tensor_tensor(fb[:, :], fl[0:NH, :], fa[:, :], ALU.max).then_inc(z_done, 1)
            dve.wait_ge(z_done, 1)
            then(v.tensor_scalar(fa[:, :], fl[0:NH, :], 0.0, None, ALU.min))
            dve.wait_ge(fexp, 2)
            then(v.tensor_tensor(fa[:, :], fb[:, :], fa[:, :], ALU.subtract))
            then(v.memset(fb[:, :], 1.0))
            then(v.tensor_tensor_scan(fl[0:NH, :], fb[:, :], fa[:, :], 0.0, ALU.mult, ALU.add))
            dve.wait_ge(sel_ready, 1)
            v.tensor_copy(cumb[0:NH, :], fl[0:NH, :]).then_inc(forget_ready, 1)
            dve.wait_ge(forget_ready, 1)
            then(v.tensor_tensor(fa[:, :], fl[0:NH, :], cumb[0:NH, :], ALU.subtract))
            then(v.tensor_copy(cumt[:, :], fa[:, :]))
            v.tensor_copy(cumb[32:32 + NH, :], cumt[:, :]).then_inc(forget_ready, 1)
            then(v.tensor_tensor(fa[:, :], fa[:, :], cumt[:, :], ALU.subtract))
            v.tensor_copy(cumb[64:64 + NH, :], fa[:, :]).then_inc(forget_ready, 1)
            then(v.tensor_scalar(fl2[:, :], fl2[:, :], 1.0, None, ALU.add))
            v.reciprocal(fl2[:, :], fl2[:, :]).then_inc(gates_ready, 1)
            project_in(0, 2)
            for g in range(1, 6):
                project_in(g)
            tiles_out(5)

            def modulation(n, first):
                dve.wait_ge(mod2_pe, n)
                then(v.tensor_tensor(mod[:, first:first + 2, :],
                                     PS[:, 7, 128:128 + 2 * KT].rearrange("p (c k) -> p c k", c=2),
                                     adab[:, KT * first:KT * (first + 2)].rearrange("p (c k) -> p c k", c=2), ALU.add))

            def score_tile(u, i, h):
                t = TS[i]
                b, c0 = S_AT[t]
                n = P * (t + 1)
                dve.wait_ge(s_pe, 4 * u + (i + 1 if i < 2 else 4))
                src = PS[:, b, c0:c0 + n]
                if u < UF:
                    v.tensor_reduce(nmax[:, t:t + 1], src, AX.X, ALU.max, negate=True).then_inc(s_max, 1)
                else:
                    p0 = P_SB[t]
                    v.tensor_tensor_reduce(out=prob[:, p0:p0 + n], in0=src, in1=rel[:, h, P * (3 - t):S],
                                           scale=-1.0, scalar=3e38, op0=ALU.add, op1=ALU.min,
                                           accum_out=nmax[:, t:t + 1]).then_inc(s_max, 1)

            def prob_tile(u, i, gate_of):
                t = TS[i]
                p0, n = parts(t)
                dve.wait_ge(s_exp, 4 * u + i + 1)
                then(v.reciprocal(rinv[:, t:t + 1], psum_row[:, t:t + 1]))
                v.tensor_scalar(prob[:, p0:p0 + n], prob[:, p0:p0 + n], rinv[:, t:t + 1], gate_of(t),
                                ALU.mult, ALU.mult if gate_of(t) is not None else ALU.bypass).then_inc(p_done, 1)

            def unit_scores(u, h, gate_of):
                score_tile(u, 0, h)
                score_tile(u, 1, h)
                prob_tile(u, 0, gate_of)
                score_tile(u, 2, h)
                score_tile(u, 3, h)
                prob_tile(u, 1, gate_of)
                prob_tile(u, 2, gate_of)
                prob_tile(u, 3, gate_of)

            def transposed_out(u):
                if u >= 1:
                    dve.wait_ge(pv_done, u)
                dve.wait_ge(t_pe, 4 * u + 2)
                v.tensor_copy(probT[:, T_SB[2]:T_SB[2] + 256], PS[:, 5, 0:256]).then_inc(t_dve, 1)
                dve.wait_ge(t_pe, 4 * u + 3)
                v.tensor_copy(probT[:, T_SB[1]:T_SB[1] + S], PS[:, 4, :]).then_inc(t_dve, 1)

            def sum_squares(n, dst):
                dve.wait_ge(o_sb, n + 1)
                if n % NH == 0:
                    v.tensor_copy(dst[:, :], o_sq[:, :]).then_inc(ss_acc, 1)
                else:
                    dve.wait_ge(ss_acc, n)
                    v.tensor_tensor(dst[:, :], dst[:, :], o_sq[:, :], ALU.add).then_inc(ss_acc, 1)

            unit_scores(0, 0, lambda t: None)
            dve.wait_ge(gates_pe, 1)
            dve.wait_ge(mod2_pe, 1)
            v.tensor_copy(gate[:, :, :], PS[:, 7, 0:ST * NSMALL].rearrange("p (t n) -> p t n", t=ST)).then_inc(gates_nat, 1)
            modulation(1, 2)
            dve.sem_inc(mod2_done, 1)
            for h in range(NH):
                transposed_out(h)
                if h + 1 < NH:
                    unit_scores(h + 1, h + 1, lambda t: None)
                if h >= 1:
                    sum_squares(h - 1, ssf)
            sum_squares(NH - 1, ssf)

            for g in range(6, 11):
                project_in(g)
            tiles_out(10)

            for b in range(2):
                for j in range(CB):
                    for kv in range(2):
                        src = nk[:, 4 + 2 * b + kv, j:j + CS * (NCMP - 1) + 1:CS]
                        last = v.tensor_scalar(unfold[:, b, j, NCMP * kv:NCMP * (kv + 1)], src,
                                               cpos[:, CB * b + j:CB * b + j + 1], None, ALU.add)
                last.then_inc(unf, 1)
            for b in range(2):
                dve.wait_ge(hid_exp, b + 1)
                then(v.tensor_scalar(hid2[:, b, :], hid2[:, b, :], 1.0, None, ALU.add))
                then(v.reciprocal(hid2[:, b, :], hid2[:, b, :]))
                v.tensor_tensor(hid[:, b, :], hid2[:, b, :], PS[:, b, 0:2 * NCMP], ALU.mult).then_inc(hid_done, 1)
            dve.wait_ge(kcv_pe, 1)
            kcs = PS[:, 2, 0:2 * NCMP].rearrange("p (h c) -> p h c", h=2)
            v.tensor_scalar(kc[:, :, 0:NCMP], kcs, par[:, R_NK:R_NK + 1], None, ALU.mult).then_inc(kc_copied, 1)
            dve.wait_ge(kc_r, 1)
            v.tensor_tensor(kc[:, :, 0:NCMP], kc[:, :, 0:NCMP], hid2[:, 1, :].rearrange("p (h c) -> p h c", h=2),
                            ALU.mult).then_inc(kc_ready, 1)
            dve.wait_ge(kcv_pe, 3)
            v.tensor_copy(vc[:, :, :], PS[0:NCMP, 3, 0:2 * P].rearrange("p (h d) -> p h d", h=2)).then_inc(vc_ready, 1)
            modulation(2, 4)
            then(v.scalar_tensor_tensor(out=mod[:, 4, :], in0=mod[:, 4, :], scalar=1.0, in1=par[:, R_N2:R_N2 + KT],
                                        op0=ALU.add, op1=ALU.mult))
            dve.sem_inc(mod2_done, 1)
            dve.wait_ge(flip_sb, NH)
            dve.wait_ge(consts, 1)

            def gate_at(h, branch):
                return lambda t: gate[:, t, NH + 3 * h + branch:NH + 3 * h + branch + 1]

            def cmp_probs(h):
                dve.wait_ge(sc_pe, h + 1)
                s = PS[:, 7, 0:ST * NSMALL].rearrange("p (t n) -> p t n", t=ST)[:, :, 0:NCMP]
                then(v.tensor_reduce(cmax[:, :], s, AX.X, ALU.max))
                if h >= 1:
                    dve.wait_ge(pct_pe, h)
                v.tensor_tensor(probc[:, :, 0:NCMP], s, cmax[:, :].unsqueeze(2).to_broadcast([P, ST, NCMP]),
                                ALU.subtract).then_inc(sc_sub, 1)

            def cmp_weights(h):
                dve.wait_ge(sc_exp, h + 1)
                then(v.tensor_reduce(csum[:, :], probc[:, :, 0:NCMP], AX.X, ALU.add))
                then(v.reciprocal(csum[:, :], csum[:, :]))
                then(v.tensor_tensor(csum[:, :], csum[:, :], gate[:, :, NH + 3 * h], ALU.mult))
                then(v.tensor_tensor(csum[:, :], csum[:, :], rowok[:, :], ALU.mult))
                v.tensor_tensor(probc[:, :, 0:NCMP], probc[:, :, 0:NCMP],
                                csum[:, :].unsqueeze(2).to_broadcast([P, ST, NCMP]), ALU.mult).then_inc(pc_done, 1)

            unit_scores(UF, 0, gate_at(0, 1))
            for h in range(NH):
                for win in range(2):
                    u = UF + 2 * h + win
                    transposed_out(u)
                    if win == 0:
                        unit_scores(u + 1, h, gate_at(h, 2))
                        cmp_probs(h)
                        if h >= 1:
                            sum_squares(UF + h - 1, ssn)
                    else:
                        cmp_weights(h)
                        if h + 1 < NH:
                            unit_scores(u + 1, h + 1, gate_at(h + 1, 1))
            sum_squares(2 * NH - 1, ssn)

            for k in range(KT + 1):
                if k < KT:
                    dve.wait_ge(ry_done, 1 if k < NH else 2)
                    y = fq[:, k, :] if k < NH else nq[:, k - NH, :]
                    v.scalar_tensor_tensor(out=y, in0=y, scalar=par[:, R_MIX + k:R_MIX + k + 1],
                                           in1=(ssf if k < NH else ssn)[:, :], op0=ALU.mult,
                                           op1=ALU.mult).then_inc(y_full, 1)
                if k >= 1:
                    y = fq[:, k - 1, :] if k - 1 < NH else nq[:, k - 1 - NH, :]
                    dve.wait_ge(y_hi, k)
                    v.tensor_tensor(hlo[:, k - 1, :], y, hhi[:, k - 1, :].bitcast(F32), ALU.subtract).then_inc(y_lo, 1)
                if k == 3:
                    lo(GCH * G_OUT)
                    lo(GCH * G_OUT + 1)

            def x1_tiles(g):
                dve.wait_ge(xT_in, 16)
                for t in range(4):
                    n = 4 * (g - G_OUT) + t
                    await_tile(dve, g, t)
                    v.scalar_tensor_tensor(out=xT[:, n, :], in0=PS[:, bank(g, t), :], scalar=mod[:, 2, n:n + 1],
                                           in1=xT[:, n, :], op0=ALU.mult, op1=ALU.add).then_inc(bank_free[bank(g, t)], 1)
                for n in range(4 * (g - G_OUT), 4 * (g - G_OUT) + 4):
                    dve.wait_ge(x1_sq, n + 1)
                    if n == 0:
                        v.tensor_copy(ssf[:, :], x1_sqt[:, 0, :]).then_inc(x1_acc, 1)
                    else:
                        dve.wait_ge(x1_acc, n)
                        v.tensor_tensor(ssf[:, :], ssf[:, :], x1_sqt[:, n % 2, :], ALU.add).then_inc(x1_acc, 1)

            for g in range(G_OUT, G_FF):
                for j in range(2 if g == G_OUT else 0, GCH):
                    lo(GCH * g + j)
                    if g > G_OUT and j == 1:
                        x1_tiles(g - 1)
            c = GCH * G_FF
            lo(c)
            lo(c + 1)
            x1_tiles(G_FF - 1)
            dve.wait_ge(rh_done, 1)
            for k in range(KT + 1):
                if k < KT:
                    if k >= 4:
                        dve.wait_ge(h2_lo, k - 3)
                    v.scalar_tensor_tensor(out=h2t[:, k % 4, :], in0=xT[:, k, :], scalar=mod[:, 4, k:k + 1],
                                           in1=ssf[:, :], op0=ALU.mult, op1=ALU.mult).then_inc(h2_t, 1)
                if k >= 1:
                    dve.wait_ge(h2_hi, k)
                    v.scalar_tensor_tensor(out=hlo[:, k - 1, :], in0=h2t[:, (k - 1) % 4, :], scalar=mod[:, 3, k - 1:k],
                                           in1=hhi[:, k - 1, :].bitcast(F32), op0=ALU.add,
                                           op1=ALU.subtract).then_inc(h2_lo, 1)

            def silu_times_up(i, c):
                for t in range(4):
                    await_ff(dve, t, 3 * (G_FF + 1) + 18 * i, c + GCH)
                    v.tensor_tensor(gfull[:, t, :], PS[:, t, :], silu_g[:, t, :], ALU.mult).then_inc(bank_free[t], 1)

            def low_of_g(i):
                for t in range(4):
                    dve.wait_ge(g_hi, 4 * i + t + 1)
                    v.tensor_tensor(glo[:, t, :], gfull[:, t, :], ghi[:, t, :].bitcast(F32),
                                    ALU.subtract).then_inc(g_lo, 1)

            def down_out(dg, tiles, chunks):
                for t in range(4):
                    n = 4 * dg + t
                    await_ff(dve, t, tiles + 3 * dg, chunks + 2 * dg + 2)
                    b = 4 * (dg % 2) + t
                    v.scalar_tensor_tensor(out=xT[:, n, :], in0=PS[:, b, :], scalar=mod[:, 5, n:n + 1],
                                           in1=xT[:, n, :], op0=ALU.mult, op1=ALU.add).then_inc(bank_free[b], 1)

            for j in range(2, GCH + 2):
                lo(c + j)
            with dve.Fori(0, NFB - 1) as i:
                at_i = c + GCH + 3 * GCH * i
                for j in range(2, 3 * GCH + 2):
                    lo_at(at_i, j)
                    if j == GCH + 1:
                        silu_times_up(i, at_i)
                    if j == GCH + 3:
                        low_of_g(i)
                    if j > 2 * GCH + 2 and j % 2 == 1:
                        down_out((j - 2 * GCH - 3) // 2, 3 * (G_FF + 3) + 18 * i, at_i + 2 * GCH)
            n = NFB - 1
            at_n = c + GCH + 3 * GCH * n
            for j in range(2, GCH):
                lo(at_n + j)
            lo(at_n + GCH)
            lo(at_n + GCH + 1)
            silu_times_up(n, at_n)
            low_of_g(n)
            for j in range(2, GCH + 2):
                if j < GCH:
                    lo(at_n + GCH + j)
                if j % 2 == 1:
                    down_out((j - 3) // 2, 3 * (G_FF + 2) + 18 * n, at_n + GCH)

        @block.gpsimd
        def _(pool):
            g = nc.gpsimd
            done = [0]

            def then(ins):
                done[0] += 1
                ins.then_inc(pool_s, 1)
                pool.wait_ge(pool_s, done[0])

            then(g.memset(ident[:, :], 0.0))
            then(g.affine_select(out=ident[:, :], in_=ident[:, :], pattern=[[-1, P]], compare_op=ALU.not_equal,
                                 fill=1.0, base=0, channel_multiplier=1))
            for f, n in ((flip, P), (flipc, NCMP)):
                then(g.memset(f[:, :], 0.0))
                then(g.affine_select(out=f[:, :], in_=f[:, :], pattern=[[1, n]], compare_op=ALU.not_equal,
                                     fill=1.0, base=1 - n, channel_multiplier=1))
            then(g.memset(ones[:, :], 1.0))
            then(g.memset(eps[:, :], EPS))
            then(g.memset(relb[NBUCKET:NBUCKET + 1, :], NEG))
            then(g.tensor_copy(identb[:, :], ident[:, :]))
            then(g.memset(maskb[:, :], 0.0))
            then(g.affine_select(out=maskb[:, :], in_=maskb[:, :], pattern=[[-1, P]], compare_op=ALU.is_ge,
                                 fill=NEG, base=0, channel_multiplier=1))
            then(g.memset(rowok[:, :], 1.0))
            g.affine_select(out=rowok[:, 0:1], in_=rowok[:, 0:1], pattern=[[0, 1]], compare_op=ALU.is_ge,
                            fill=0.0, base=-(CB - 1), channel_multiplier=1).then_inc(consts, 1)
            pool.wait_ge(small_pe, 1)
            then(g.memset(cumb[:, :], 0.0))
            then(g.memset(sel[:, :, :], 0.0))
            for q in range(3):
                last = g.affine_select(out=sel[:, :, :], in_=sel[:, :, :], pattern=[[-1, NH], [0, P]],
                                       compare_op=ALU.not_equal, fill=1.0, base=-32 * q, channel_multiplier=1)
                if q < 2:
                    then(last)
            last.then_inc(sel_ready, 1)


_INS = ['x', 'c', 'ada_w', 'ada_b', 'norm1_gain', 'norm2_gain', 'w_in', 'fox_f_bias', 'fox_q_gain', 'fox_k_gain',
        'nsa_q_gain', 'nsa_k_gain', 'nsa_cmp_pos', 'nsa_cmp_w1', 'nsa_cmp_w2', 'rel_bias', 'mix_out_gain', 'w_out',
        'ffn_w_gate', 'ffn_w_up', 'ffn_w_down']


def bucket_onehot():
    d = np.concatenate([S - 1 - np.arange(NREV), np.arange(NFWD) - (S - 1)])
    exact = NBUCKET // 2
    n = np.maximum(d, 1).astype(np.float64)
    large = exact + (np.log(n / exact) / np.log(MAXDIST / exact) * (NBUCKET - exact)).astype(np.int64)
    b = np.where(d < exact, d, np.minimum(large, NBUCKET - 1))
    b = np.where(d < 0, NBUCKET, b)
    return (np.arange(NBUCKET + 1)[:, None] == b[None, :]).astype(np.float32)


def kernel(**inputs):
    import concourse.bacc as bacc
    from concourse.bass_utils import run_bass_kernel_spmd

    nc = bacc.Bacc("TRN2", target_bir_lowering=False, num_devices=1)
    arrays, aps = {}, {}
    given = {name: np.ascontiguousarray(inputs[name]) for name in _INS}
    given["bucket_onehot"] = bucket_onehot()
    for name, a in given.items():
        arrays[f"in_{name}"] = a
        aps[name] = nc.dram_tensor(f"in_{name}", a.shape, mybir.dt.from_np(a.dtype), kind="ExternalInput").ap()
    out = nc.dram_tensor("out_0", (1, S, D), F32, kind="ExternalOutput").ap()
    hybrid_layer(nc, aps, out)
    r = run_bass_kernel_spmd(nc, [arrays], core_ids=[0])
    return r.results[0]["out_0"]
```

```python
from contextlib import ExitStack

import numpy as np

import concourse.bass as bass
from concourse import mybir

F32 = mybir.dt.float32
F32R = mybir.dt.float32r
BF16 = mybir.dt.bfloat16
ALU = mybir.AluOpType
ACT = mybir.ActivationFunctionType
AX = mybir.AxisListType

P = 128
S = 512
ST = S // P
D = 2048
KT = D // P
NH = 8
DFF = 5632
NBUCKET, MAXDIST = 32, 128
CB, CS = 32, 16
NCMP = (S - CB) // CS + 1
SCALE = P ** -0.5
EPS = 1e-6
NEG = -1e30
C_FQ, C_FV, C_FF, C_NQ, C_NK = 0, 2048, 3072, 3080, 4104
C_NV = C_NK + 768
C_NG = C_NV + 768
NSMALL = 32
CK = 2
CW = 512
NSTAGE, NW = 4, 2
GCH = KT // CK
G_OUT, G_FF = 11, 15
NFB = DFF // CW
NREV, NFWD = 640, 992
R_C, R_N1, R_N2, R_MIX, R_FQ, R_FK, R_NQ, R_NK = 0, 16, 32, 48, 64, 65, 66, 67
NPAR = 70
TS = (3, 2, 1, 0)
S_AT = {3: (0, 0), 2: (1, 0), 1: (2, 0), 0: (2, 256)}
T_AT = {0: (3, 0), 1: (4, 0), 3: (4, 384), 2: (5, 0)}
T_SB = {0: 0, 1: 512, 3: 896, 2: 1024}
P_SB = {3: 0, 2: 512, 1: 896, 0: 1152}
ACW = 256
ADA_STEPS = 128


def ada_plan():
    plan = {}
    for groups, first in ((range(2, 6), 0), (range(6, 11), ADA_STEPS // 2)):
        slots = [(g, j) for g in groups for j in range(GCH)]
        if first == 0:
            plan.update({slot: range(0) for slot in slots[:2]})
            slots = slots[2:]
        n = ADA_STEPS // 2
        for i, slot in enumerate(slots):
            plan[slot] = range(first + i * n // len(slots), first + (i + 1) * n // len(slots))
    return plan


def hybrid_layer(nc, A, out):
    with ExitStack() as ctx:
        base = (nc.sbuf_base + 63) // 64 * 64
        RH, RQ = base, base + 65536
        RW = RQ + 57344
        RX = RW + 32768
        RM = RX + 32768

        def at(name, shape, dt, offset):
            return nc.alloc_sbuf_tensor_at(name, shape, dt, offset=offset)

        def sem(name):
            return ctx.enter_context(nc.semaphore(name))

        hhi = at("hhi", [P, KT, S], F32R, RH)
        hlo = at("hlo", [P, KT, S], F32R, RH + 32768)
        xnat = at("xnat", [P, ST, D], F32, RH)
        xn = at("xn", [P, KT, S], F32, RH + 32768)
        sq_first = at("sq_first", [P, D], F32, RH + 32768)
        cmp_bias = at("cmp_bias", [NCMP, NH, S], F32, RH + 49152)
        rel = at("rel", [P, NH, S], F32, RH + 16384)
        rel_rev = at("rel_rev", [P, NH, S], F32, RW)
        w1 = [at(f"w1_{b}", [P, CB, P], F32, RH + 32768 * b) for b in range(2)]
        xt0 = at("xt0", [P, KT, S], F32, RQ + 16384)
        acc_first = at("acc_first", [P, 2, 2 * ACW], F32, RQ + 8192)
        partial = at("partial", [P, S], F32, RQ + 12288)
        wsmall_hi = at("wsmall_hi", [P, KT, NSMALL], F32R, RQ + 49152)
        wsmall_lo = at("wsmall_lo", [P, KT, NSMALL], F32R, RQ + 51200)
        wsmall = at("wsmall", [P, KT, NSMALL], F32, RQ + 53248)
        fl = at("fl", [NSMALL, S], F32, RQ + 53248)
        fl2 = at("fl2", [NSMALL, S], F32, RQ + 55296)
        fq = at("fq", [P, NH, S], F32, RQ)
        fk = at("fk", [P, NH, S], F32, RQ + 16384)
        fv = at("fv", [P, ST, 2 * CW], F32, RQ + 32768)
        nq = at("nq", [P, NH, S], F32, RQ + 16384)
        nk = at("nk", [P, NH, S], F32, RQ + 32768)
        nv = at("nv", [P, ST, CW], F32, RQ + 49152)
        silu_g = at("silu_g", [P, 4, S], F32, RQ)
        ghi = at("ghi", [P, 4, S], F32R, RQ + 8192)
        glo = at("glo", [P, 4, S], F32R, RQ + 16384)
        gfull = at("gfull", [P, 4, S], F32, RQ + 24576)
        ostage = at("ostage", [P, 2, ST, CW], F32, RQ + 32768)
        stage = at("stage", [P, NSTAGE, CK, CW], F32, RW)
        whi = at("whi", [P, NW, CK, CW], F32R, RW + 16384)
        wlo = at("wlo", [P, NW, CK, CW], F32R, RW + 24576)
        ada_first = [at(f"ada_first{b}", [P, 4, 2, ACW], F32, offset)
                     for b, offset in enumerate((RX, RX + 8192, RX + 16384, RQ))]
        h1t = at("h1t", [P, 4, S], F32, RX + 24576)
        sq = at("sq", [P, 4, S], F32, RX)
        rb = at("rb", [P, 4, S], F32, RX + 8192)
        ada_ring = at("ada_ring", [P, 3, D // 2], F32, RX + 16384)
        prob = at("prob", [P, 1280], F32, RX + 16384)
        probT = at("probT", [P, 1280], F32, RX + 21504)
        probc = at("probc", [P, ST, NCMP + 1], F32, RX + 26624)
        probcT = at("probcT", [NCMP, S], F32, RX + 27136)
        o_sq = at("o_sq", [P, S], F32, RX)
        ssn = at("ssn", [P, S], F32, RX + 2048)
        fa = at("fa", [NH, S], F32, RX + 28672)
        fb = at("fb", [NH, S], F32, RX + 30720)
        sel = at("sel", [72, NH, P], BF16, RQ + 49152)
        cumb = at("cumb", [72, S], BF16, RQ + 51200)
        cumt = at("cumt", [NH, S], BF16, RQ + 52224)
        unfold = at("unfold", [P, 2, CB, 2 * NCMP], F32, RX)
        xT = at("xT", [P, KT, S], F32, RX)
        acc = at("acc", [P, 2, D], F32, RM)
        m = RM + 16384

        def small(name, shape, dt=F32):
            nonlocal m
            size = 4 if dt == F32 else 2
            for n in shape[1:]:
                size *= n
            t = at(name, shape, dt, m)
            m += (size + 31) // 32 * 32
            return t

        par = small("par", [P, NPAR])
        adab = small("adab", [P, 96])
        mod = small("mod", [P, 6, KT])
        fbias = small("fbias", [NH, 1])
        cpos = small("cpos", [P, 2 * CB])
        silu_c = small("silu_c", [P, KT])
        t16 = small("t16", [P, KT])
        ident = small("ident", [P, P])
        flip = small("flip", [P, P])
        flipc = small("flipc", [NCMP, NCMP])
        ones = small("ones", [P, P])
        identb = small("identb", [P, P], BF16)
        maskb = small("maskb", [P, P], BF16)
        eps = small("eps", [P, 1])
        ssx = small("ssx", [P, ST])
        rx = small("rx", [P, ST])
        nmax = small("nmax", [P, ST])
        psum_row = small("psum_row", [P, ST])
        rinv = small("rinv", [P, ST])
        cmax = small("cmax", [P, ST])
        csum = small("csum", [P, ST])
        gate = small("gate", [P, ST, NSMALL])
        rowok = small("rowok", [P, ST])
        kc = small("kc", [P, 2, NCMP + 1])
        vc = small("vc", [NCMP, 2, P])
        ssf = small("ssf", [P, S])
        assert m <= nc.sbuf_usable_end, m - nc.sbuf_usable_end
        parn = at("parn", [NPAR, P], F32, RM)
        adabn = at("adabn", [96, P], F32, RM + 512)
        cposn = at("cposn", [2 * CB, P], F32, RM + 1024)
        relb = at("relb", [NBUCKET + 1, NH], F32, RM + 1536)
        onehot = at("onehot", [NBUCKET + 1, NREV + NFWD], F32, RM + 2048)
        line = at("line", [NH, NREV + NFWD], F32, RM + 2048 + 6656)
        diag = at("diag", [P, ST, P], F32, RX + 24576)
        w2 = at("w2", [P, 2, P], F32, RX + 29184)
        hid = at("hid", [P, 2, 2 * NCMP], F32, RX + 30208)
        hid2 = at("hid2", [P, 2, 2 * NCMP], F32, RX + 30720)

        PS = ctx.enter_context(nc.psum_tensor("PS", [P, 8, S], F32))
        xT_d = nc.dram_tensor("xT_d", [P, KT * S], F32, kind="Internal").ap()
        line_d = nc.dram_tensor("line_d", [NH, NREV + NFWD], F32, kind="Internal").ap()

        consts = sem("consts")
        par_in, lines_in, small_in = sem("par_in"), sem("lines_in"), sem("small_in")
        x_in = [sem(f"x_in{t}") for t in range(ST)]
        first_in = [sem(f"ada_first_in{b}") for b in range(4)]
        par_t, par_done, act_s, dve_s = sem("par_t"), sem("par_done"), sem("act_self"), sem("dve_self")
        exp_c = sem("exp_c")
        first_acc = sem("first_acc")
        line_pe, line_sb, line_out = sem("line_pe"), sem("line_sb"), sem("line_out")
        xt_pe, xt_sb, xt_out = sem("xt_pe"), sem("xt_sb"), sem("xt_out")
        rx_done, diag_done, rb_pe, xn_done = sem("rx_done"), sem("diag_done"), sem("rb_pe"), sem("xn_done")
        mod_pe, mod_ready, part_out, small_out = sem("mod_pe"), sem("mod_ready"), sem("part_out"), sem("small_out")
        h_full, h_hi, h_lo = sem("h_full"), sem("h_hi"), sem("h_lo")
        ws_hi, ws_lo, small_pe = sem("ws_hi"), sem("ws_lo"), sem("small_pe")
        gates_e, z_done, fexp, forget_ready, gates_ready, gates_pe, gates_nat = (sem(n) for n in (
            "gates_exp", "z_done", "forget_exp", "forget_ready", "gates_ready", "gates_pe", "gates_nat"))
        stage_in = [sem(f"stage_in{b}") for b in range(NSTAGE)]
        split_in = [sem(f"split_in{b}") for b in range(NSTAGE)]
        w_hi, w_lo, w_used = sem("w_hi"), sem("w_lo"), sem("w_used")
        tile_done = sem("tile_done")
        bank_free = [sem(f"bank_free{b}") for b in range(8)]
        evac, sq_done, ss_pe, ln_done, r_done, norm_done = (sem(n) for n in (
            "evac", "sq_done", "ss_pe", "ln_done", "r_done", "norm_done"))
        ada_in = [sem(f"ada_in{b}") for b in range(3)]
        ada_acc = sem("ada_acc")
        sel_ready, ready_small = sem("sel_ready"), sem("ready_small")
        s_pe, s_max, s_exp, p_done, t_pe, t_act, t_dve, o_pe, o_sb, o_ssq, ss_acc = (sem(n) for n in (
            "scores_pe", "scores_max", "scores_exp", "probs_done", "transposed_pe", "transposed_act",
            "transposed_dve", "out_pe", "out_sb", "out_squared", "squares_summed"))
        rel_in, w1_in, unf, hid_pe, hid_exp, hid_done, kcv_pe, kc_copied, kc_sq, kc_ss, kc_r, kc_ready, vc_ready = (
            sem(n) for n in ("rel_in", "w1_in", "unfolded", "hid_pe", "hid_exp", "hid_done", "kcv_pe",
                             "kc_copied", "kc_squared", "kc_ss", "kc_r", "kc_ready", "vc_ready"))
        sc_pe, sc_sub, sc_exp, pc_done, pct_pe, pct_sb = (sem(n) for n in (
            "cmp_scores", "cmp_shifted", "cmp_exp", "cmp_probs", "cmp_transposed", "cmp_transposed_sb"))
        pv_done, ry_ln, rh_ln, kc_ln = (sem(n) for n in ("pv_done", "ry_ln", "rh_ln", "kc_ln"))
        flip_pe, flip_sb, cmpb_in = sem("flip_pe"), sem("flip_sb"), sem("cmpb_in")
        mod2_pe, mod2_done = sem("mod2_pe"), sem("mod2_done")
        y_full, y_hi, y_lo = sem("y_full"), sem("y_hi"), sem("y_lo")
        ssy_pe, ry_done = sem("ssy_pe"), sem("ry_done")
        xT_in, x1_sq, x1_acc = sem("xT_in"), sem("x1_sq"), sem("x1_acc")
        ssh_pe, rh_done, h2_t, h2_hi, h2_lo = sem("ssh_pe"), sem("rh_done"), sem("h2_t"), sem("h2_hi"), sem("h2_lo")
        g_hi, g_lo, pool_s = sem("g_hi"), sem("g_lo"), sem("pool_self")
        fin_pe, fin_sb, fin_last = sem("fin_pe"), sem("fin_sb"), sem("fin_last")
        out_sent = [sem(f"out_sent{b}") for b in range(2)]

        plan = ada_plan()
        w_in, w_o = A["w_in"][0], A["w_out"][0]
        w_in_t = w_in.rearrange("(k p) n -> p k n", p=P)
        ada_t = A["ada_w"][0].rearrange("(k p) n -> k p n", p=P)

        def group_cols(g):
            if g < 4:
                return [(C_FQ + CW * g, CW)]
            if g < 6:
                return [(C_FV + CW * (g - 4), CW)]
            if g < 8:
                return [(C_NQ + CW * (g - 6), CW)]
            if g == 8:
                return [(C_NK + 256, CW)]
            if g == 9:
                return [(C_NK, 256), (C_NV, 256)]
            return [(C_NV + 256, CW)]

        NATURAL = (4, 5, 10)
        NORMED = (0, 1, 2, 3, 6, 7, 8)

        def tile_of(g, t):
            if g < 2:
                return fq[:, 4 * g + t, :]
            if g < 4:
                return fk[:, 4 * (g - 2) + t, :]
            if g < 6:
                return fv[:, t, CW * (g - 4):CW * (g - 3)]
            if g < 8:
                return nq[:, 4 * (g - 6) + t, :]
            if g == 8:
                return nk[:, t, :]
            if g == 9:
                return nk[:, 4 + t, :]
            return nv[:, t, :]

        def gain_of(g, t):
            r = R_FQ if g < 2 else R_FK if g < 4 else R_NQ if g < 8 else R_NK + 1 + t // 2
            return par[:, r:r + 1]

        def bank(g, t):
            return 4 * (g % 2) + t

        def uses(g):
            return 1 + g // 2

        def normed_before(g):
            return 4 * sum(x < g for x in NORMED)

        def parts(t):
            return P_SB[t], P * (t + 1)

        UF = NH

        def await_tile(eng, g, t):
            if t < 3:
                eng.wait_ge(tile_done, 3 * g + t + 1)
            else:
                eng.wait_ge(w_used, GCH * (g + 1) if g else 2 * GCH - 1)

        def await_ff(eng, t, tiles, chunks):
            if t < 3:
                eng.wait_ge(tile_done, tiles + t + 1)
            else:
                eng.wait_ge(w_used, chunks)

        x1_sqt = at("x1_sqt", [P, 2, S], F32, RQ + 32768)
        h2t = at("h2t", [P, 4, S], F32, RQ + 40960)

        block = ctx.enter_context(nc.Block())

        @block.sync
        def _(sp):
            rows = [("c", R_C, 16), ("norm1_gain", R_N1, 16), ("norm2_gain", R_N2, 16), ("mix_out_gain", R_MIX, 16),
                    ("fox_q_gain", R_FQ, 1), ("fox_k_gain", R_FK, 1), ("nsa_q_gain", R_NQ, 1)]
            for name, r, n in rows:
                sp.dma_start(parn[r:r + n, :], A[name].rearrange("a (r d) -> (a r) d", d=P)).then_inc(par_in, 16)
            sp.dma_start(parn[R_NK:R_NK + 3, :], A["nsa_k_gain"][0]).then_inc(par_in, 16)
            sp.dma_start(adabn[:, :], A["ada_b"].rearrange("a (r d) -> (a r) d", d=P)).then_inc(par_in, 16)
            sp.dma_start(cposn[:, :], A["nsa_cmp_pos"][0].rearrange("a b d -> (a b) d")).then_inc(par_in, 16)
            sp.dma_start(fbias[:, :], A["fox_f_bias"].rearrange("a h -> h a")).then_inc(par_in, 16)
            for t in range(ST):
                sp.dma_start(xnat[:, t, :], A["x"][0, P * t:P * (t + 1), :]).then_inc(x_in[t], 16)

            def free_stage(c):
                if c >= NSTAGE:
                    sp.wait_ge(w_lo, c - NSTAGE + 1)

            ada_p = A["ada_w"][0].rearrange("(k p) n -> p k n", p=P)
            for j in range(GCH):
                for s in range(4):
                    if j >= 1:
                        sp.wait_ge(first_acc, KT * (j - 1) + 4 * (s + 1))
                    for comp in range(2):
                        c0 = D * comp + ACW * j
                        sp.dma_start(ada_first[s][:, :, comp, :], ada_p[:, 4 * s:4 * s + 4, c0:c0 + ACW]
                                     ).then_inc(first_in[s], 16)
                    if s == 1:
                        for g in range(2):
                            c = 2 * j + g
                            free_stage(c)
                            c0 = group_cols(g)[0][0]
                            sp.dma_start(stage[:, c % NSTAGE, :, :],
                                         w_in_t[:, CK * j:CK * j + CK, c0:c0 + CW]).then_inc(stage_in[c % NSTAGE], 16)
                if j == 0:
                    sp.dma_start(relb[0:NBUCKET, :], A["rel_bias"]).then_inc(lines_in, 16)
                    sp.dma_start(onehot[:, :], A["bucket_onehot"]).then_inc(lines_in, 16)
                if j == 2:
                    sp.wait_ge(line_sb, 4)
                    sp.dma_start(line_d, line[:, :]).then_inc(line_out, 16)
                if j == 3:
                    sp.dma_start(wsmall[:, :, 0:8], w_in_t[:, :, C_FF:C_FF + 8]).then_inc(small_in, 16)
                    sp.dma_start(wsmall[:, :, 8:32], w_in_t[:, :, C_NG:C_NG + 24]).then_inc(small_in, 16)

            def ada(a):
                if a >= 3:
                    sp.wait_ge(ada_acc, a - 2)
                comp, k, half = 2 + a // 32, a % 32 // 2, a % 2
                c0 = D * comp + 1024 * half
                sp.dma_start(ada_ring[:, a % 3, :], ada_t[k, :, c0:c0 + 1024]).then_inc(ada_in[a % 3], 16)

            def project_in(g):
                for j in range(GCH):
                    c = GCH * g + j
                    free_stage(c)
                    if g == 6 and j == NSTAGE:
                        sp.wait_ge(pv_done, UF)
                        for a in range(plan[g, 0][0], plan[g, NSTAGE][0]):
                            ada(a)
                    pieces = group_cols(g)
                    if len(pieces) == 2:
                        for (c0, n), n0, landed in zip(pieces, (0, 256), (split_in, stage_in)):
                            sp.dma_start(stage[:, c % NSTAGE, :, n0:n0 + n],
                                         w_in_t[:, CK * j:CK * j + CK, c0:c0 + n]).then_inc(landed[c % NSTAGE], 16)
                    else:
                        c0, n = pieces[0]
                        sp.dma_start(stage[:, c % NSTAGE, :, :],
                                     w_in_t[:, CK * j:CK * j + CK, c0:c0 + n]).then_inc(stage_in[c % NSTAGE], 16)
                    if g == 2 and j == 1:
                        sp.dma_start(xT_d, xt0[:, :, :].rearrange("p k s -> p (k s)")).then_inc(xt_out, 16)
                        sp.wait_ge(h_lo, KT)
                        sp.wait_ge(line_out, 16)
                    if g != 6 or j >= NSTAGE:
                        for a in plan[g, j]:
                            ada(a)

            for g in range(2, 11):
                project_in(g)

            sp.wait_ge(line_out, 16)
            sp.wait_ge(w_lo, 11 * GCH)
            for h in range(NH):
                at_h = h * (NREV + NFWD)
                sp.dma_start(rel_rev[:, h, :], bass.AP(tensor=line_d.tensor, offset=at_h,
                                                       ap=[[1, P], [1, S]])).then_inc(rel_in, 16)
            sp.wait_ge(w_used, 11 * GCH)
            for h in range(NH):
                at_h = h * (NREV + NFWD) + NREV + S - 1 - (CB - 1) - CS * (NCMP - 1)
                sp.dma_start(cmp_bias[:, h, :], bass.AP(tensor=line_d.tensor, offset=at_h,
                                                        ap=[[CS, NCMP], [1, S]])).then_inc(cmpb_in, 16)
            for b in range(2):
                sp.dma_start(w1[b][:, :, :], A["nsa_cmp_w1"][0, b].rearrange("(j d) n -> d j n", d=P)).then_inc(w1_in, 16)
            sp.dma_start(w2[:, :, :], A["nsa_cmp_w2"][0].rearrange("b d n -> d b n")).then_inc(w1_in, 16)

            sp.wait_ge(flip_pe, NH)
            w_o_t = w_o.rearrange("(k p) n -> p k n", p=P)
            for g in range(G_OUT, G_FF):
                for j in range(GCH):
                    c = GCH * g + j
                    free_stage(c)
                    c0 = CW * (g - G_OUT)
                    sp.dma_start(stage[:, c % NSTAGE, :, :],
                                 w_o_t[:, CK * j:CK * j + CK, c0:c0 + CW]).then_inc(stage_in[c % NSTAGE], 16)
                if g == G_OUT:
                    sp.wait_ge(y_full, KT)
                    sp.dma_start(xT[:, :, :].rearrange("p k s -> p (k s)"), xT_d).then_inc(xT_in, 16)

            gate_w = A["ffn_w_gate"][0].rearrange("(k p) n -> p k n", p=P)
            up_w = A["ffn_w_up"][0].rearrange("(k p) n -> p k n", p=P)
            down_w = A["ffn_w_down"][0].rearrange("(k p) n -> p k n", p=P)

            def columns(w, i, c):
                for j in range(GCH):
                    sp.wait_ge(w_lo, c + j - NSTAGE + 1)
                    sp.dma_start(stage[:, j % NSTAGE, :, :],
                                 w[:, CK * j:CK * j + CK, bass.ds(CW * i, CW)]).then_inc(stage_in[j % NSTAGE], 16)

            def rows_of_down(i, c):
                for j in range(GCH):
                    sp.wait_ge(w_lo, c + j - NSTAGE + 1)
                    c0 = CW * (j // 2)
                    sp.dma_start(stage[:, j % NSTAGE, :, :],
                                 down_w[:, bass.ds(4 * i + CK * (j % 2), CK), c0:c0 + CW]
                                 ).then_inc(stage_in[j % NSTAGE], 16)

            c = GCH * G_FF
            columns(gate_w, 0, c)
            with sp.Fori(0, NFB - 1) as i:
                at_i = c + GCH + 3 * GCH * i
                columns(up_w, i, at_i)
                columns(gate_w, i + 1, at_i + GCH)
                rows_of_down(i, at_i + 2 * GCH)
            last = c + GCH + 3 * GCH * (NFB - 1)
            columns(up_w, NFB - 1, last)
            rows_of_down(NFB - 1, last + GCH)

            out_t = out[0].rearrange("(t p) n -> p t n", p=P)
            for dg in range(4):
                for t in range(ST):
                    if dg < 3:
                        sp.wait_ge(fin_sb, 4 * dg + t + 1)
                    elif t % 2 == 0:
                        sp.wait_ge(fin_sb, 12 + t // 2 + 1)
                    else:
                        sp.wait_ge(fin_last, t // 2 + 1)
                    sp.dma_start(out_t[:, t, CW * dg:CW * (dg + 1)], ostage[:, dg % 2, t, :]
                                 ).then_inc(out_sent[dg % 2], 16)
            for b in range(2):
                sp.wait_ge(out_sent[b], 2 * 16 * ST)

        @block.tensor
        def _(pe):
            mm, tr = nc.tensor.matmul, nc.tensor.transpose

            pe.wait_ge(consts, 1)
            pe.wait_ge(par_in, 11 * 16)
            tr(PS[:, 0, 0:NPAR], parn[:, :], ident[0:NPAR, 0:NPAR]).then_inc(par_t, 1)
            tr(PS[:, 1, 0:96], adabn[:, :], ident[0:96, 0:96]).then_inc(par_t, 1)
            tr(PS[:, 2, 0:2 * CB], cposn[:, :], ident[0:2 * CB, 0:2 * CB]).then_inc(par_t, 1)
            for t in range(ST):
                pe.wait_ge(x_in[t], 16)
            for k in range(KT):
                if k == 0:
                    pe.wait_ge(par_done, 3)
                if k >= 8:
                    pe.wait_ge(xt_sb, k - 7)
                for t in range(ST):
                    last = tr(PS[:, k % 8, P * t:P * (t + 1)], xnat[:, t, P * k:P * (k + 1)], ident[:, :])
                last.then_inc(xt_pe, 1)
            pe.wait_ge(diag_done, ST)
            pe.wait_ge(xt_sb, KT)
            for t in range(ST):
                last = mm(PS[:, 7, P * t:P * (t + 1)], ones[:, :], diag[:, t, :], start=True, stop=True)
            last.then_inc(rb_pe, 1)
            pe.wait_ge(lines_in, 32)
            n = (NREV + NFWD) // 4
            for b in range(4):
                mm(PS[0:NH, b, 0:n], relb[:, :], onehot[:, n * b:n * (b + 1)], start=True, stop=True).then_inc(line_pe, 1)

            def columns_tile(b, slot, kk, t, k, start, stop, rhi=None, rlo=None):
                cols = slice(P * t, P * (t + 1))
                rhi = hhi[:, k, :] if rhi is None else rhi
                rlo = hlo[:, k, :] if rlo is None else rlo
                mm(PS[:, b, :], whi[:, slot, kk, cols], rhi, start=start, stop=False)
                mm(PS[:, b, :], whi[:, slot, kk, cols], rlo, start=False, stop=False)
                return mm(PS[:, b, :], wlo[:, slot, kk, cols], rhi, start=False, stop=stop)

            def tokens_tile(b, slot, kk, t, k, start, stop):
                rows = slice(P * t, P * (t + 1))
                mm(PS[:, b, :], hhi[:, k, rows], whi[:, slot, kk, :], start=start, stop=False)
                mm(PS[:, b, :], hhi[:, k, rows], wlo[:, slot, kk, :], start=False, stop=False)
                return mm(PS[:, b, :], hlo[:, k, rows], whi[:, slot, kk, :], start=False, stop=stop)

            def first_groups():
                def shift_and_scale(j):
                    pe.wait_ge(first_acc, KT * (j + 1))
                    if j == 0:
                        pe.wait_ge(bank_free[7], 1)
                    if j >= 2:
                        pe.wait_ge(part_out, j - 1)
                    for n in range(2 * CK):
                        for half in range(2):
                            last = mm(PS[:, 7, n:n + 1], acc_first[:, half, P * n:P * (n + 1)], ones[:, 0:1],
                                      start=half == 0, stop=half == 1)
                    last.then_inc(mod_pe, 1)

                shift_and_scale(0)
                for j in range(GCH):
                    for g in range(2):
                        pe.wait_ge(w_lo, 2 * j + g + 1)
                        for t in range(4):
                            b = 4 * g + t
                            if j == 0 and b < 7:
                                pe.wait_ge(bank_free[b], 1)
                            if b == 7:
                                pe.wait_ge(mod_ready, min(j + 2, GCH))
                            alone = b == 7 and j < GCH - 1
                            if b == 7 and j == GCH - 1:
                                pe.wait_ge(part_out, GCH - 1)
                                mm(PS[:, 7, :], ident[:, :], partial[:, :], start=True, stop=False)
                            for kk in range(CK):
                                k = CK * j + kk
                                if b == 0:
                                    pe.wait_ge(h_lo, k + 1)
                                start = b != 7 and k == 0 or alone and kk == 0
                                last = columns_tile(b, g, kk, t, k, start, (kk == CK - 1) if alone else k == KT - 1)
                            if j == GCH - 1 and t < 3:
                                last.then_inc(tile_done, 1)
                        last.then_inc(w_used, 1)
                        if g == 0 and j < GCH - 1:
                            shift_and_scale(j + 1)

            def small_columns():
                pe.wait_ge(ws_lo, 1)
                pe.wait_ge(bank_free[7], uses(3))
                for k in range(KT):
                    mm(PS[0:NSMALL, 7, :], wsmall_hi[:, k, :], hhi[:, k, :], start=(k == 0), stop=False)
                    mm(PS[0:NSMALL, 7, :], wsmall_hi[:, k, :], hlo[:, k, :], start=False, stop=False)
                    last = mm(PS[0:NSMALL, 7, :], wsmall_lo[:, k, :], hhi[:, k, :], start=False, stop=(k == KT - 1))
                last.then_inc(small_pe, 1)

            def gemm(c, first_bank, free, tile, chunks=GCH, mid=None, before=None, guard=None):
                for j in range(chunks):
                    pe.wait_ge(w_lo, c + j + 1)
                    for t in range(4):
                        if j == 0:
                            pe.wait_ge(bank_free[first_bank + t], free)
                            if t == 3 and guard is not None:
                                guard()
                        for kk in range(CK):
                            k = CK * j + kk
                            if before is not None and t == 0:
                                before(k)
                            last = tile(first_bank + t, j % NW, kk, t, k, k == 0, k == CK * chunks - 1)
                        if j == chunks - 1 and t < 3:
                            last.then_inc(tile_done, 1)
                    last.then_inc(w_used, 1)
                    if mid is not None and j == 3:
                        mid()

            def squares(g):
                for t in range(4):
                    n = normed_before(g) + t + 1
                    pe.wait_ge(sq_done, n)
                    mm(PS[:, bank(g, t), :], ones[:, :], sq[:, t, :], start=True, stop=True).then_inc(ss_pe, 1)

            def project_in(g):
                mid = (lambda: squares(g - 1)) if g - 1 in NORMED and g != 6 else None
                gemm(GCH * g, bank(g, 0), uses(g), tokens_tile if g in NATURAL else columns_tile, mid=mid,
                     guard=(lambda: pe.wait_ge(small_out, 1)) if g == 3 else None)

            def scores(u, q_of, k_of, bias=None):
                for i, t in enumerate(TS):
                    b, c0 = S_AT[t]
                    n = P * (t + 1)
                    o = PS[:, b, c0:c0 + n]
                    last = mm(o, q_of(t), k_of(n), start=True, stop=bias is None)
                    if bias is not None:
                        last = bias(o, t, n)
                    last.then_inc(s_pe, 1)

            def transposes(u):
                for i, t in enumerate(TS):
                    pe.wait_ge(p_done, 4 * u + i + 1)
                    for kb in range(t + 1):
                        b, c0 = T_AT[kb]
                        c0 += P * (t - kb)
                        c1 = parts(t)[0] + P * kb
                        last = tr(PS[:, b, c0:c0 + P], prob[:, c1:c1 + P], ident[:, :])
                    last.then_inc(t_pe, 1)

            def values(u, v_of, start, stop):
                pe.wait_ge(t_act, u + 1)
                pe.wait_ge(t_dve, 2 * (u + 1))
                for kb in range(4):
                    n = S - P * kb
                    last = mm(PS[:, 6, P * kb:S], v_of(kb), probT[:, T_SB[kb]:T_SB[kb] + n],
                              start=start and kb == 0, stop=stop and kb == 3)
                return last

            first_groups()
            squares(0)
            for g in range(2, 6):
                project_in(g)
                if g == 2:
                    small_columns()

            pe.wait_ge(sel_ready, 1)
            pe.wait_ge(forget_ready, 3)
            pe.wait_ge(gates_ready, 1)
            for b in range(8):
                pe.wait_ge(bank_free[b], uses(6 + b // 4))
            pe.wait_ge(norm_done, 16)
            for t in range(ST):
                last = tr(PS[:, 7, NSMALL * t:NSMALL * (t + 1)], fl2[:, P * t:P * (t + 1)],
                          ident[0:NSMALL, 0:NSMALL])
            last.then_inc(gates_pe, 1)
            pe.wait_ge(ada_acc, ADA_STEPS // 2)
            for n in range(2 * KT):
                last = mm(PS[:, 7, 128 + n:129 + n], acc[:, n // KT, P * (n % KT):P * (n % KT + 1)],
                          ones[:, 0:1], start=True, stop=True)
            last.then_inc(mod2_pe, 1)

            def fox_scores(h):
                def bias(o, t, n):
                    mm(o, sel[:, h, :], cumb[:, 0:n], start=False, stop=False)
                    return mm(o[:, n - P:n], identb[:, :], maskb[:, :], start=False, stop=True)

                scores(h, lambda t: fq[:, h, P * t:P * (t + 1)], lambda n: fk[:, h, 0:n], bias)

            fox_scores(0)
            for h in range(NH):
                transposes(h)
                if h + 1 < NH:
                    fox_scores(h + 1)
                if h >= 1:
                    pe.wait_ge(o_sb, h)
                values(h, lambda kb, h=h: fv[:, kb, P * h:P * (h + 1)], True, True).then_inc(pv_done, 1)

            def fox_mean():
                pe.wait_ge(ss_acc, NH)
                pe.wait_ge(gates_nat, 1)
                pe.wait_ge(mod2_done, 1)
                mm(PS[:, 7, :], ones[:, :], ssf[:, :], start=True, stop=True).then_inc(ssy_pe, 1)

            gemm(GCH * 6, 0, uses(6), columns_tile, mid=fox_mean)
            pe.wait_ge(o_sb, NH)
            pe.wait_ge(ry_done, 1)
            for g in range(7, 11):
                project_in(g)

            for b in range(8):
                pe.wait_ge(bank_free[b], uses(12 - b // 4))
            pe.wait_ge(rel_in, 16 * NH)
            for h in range(NH):
                if h >= 3:
                    pe.wait_ge(flip_sb, h - 2)
                mm(PS[:, 4 + h % 3, :], flip[:, :], rel_rev[:, h, :], start=True, stop=True).then_inc(flip_pe, 1)
            pe.wait_ge(w1_in, 48)
            pe.wait_ge(unf, 2)
            for b in range(2):
                for j in range(CB):
                    last = mm(PS[:, b, 0:2 * NCMP], w1[b][:, j, :], unfold[:, b, j, :],
                              start=(j == 0), stop=(j == CB - 1))
                last.then_inc(hid_pe, 1)
            pe.wait_ge(hid_done, 1)
            mm(PS[:, 2, 0:2 * NCMP], w2[:, 0, :], hid[:, 0, :], start=True, stop=True).then_inc(kcv_pe, 1)
            pe.wait_ge(hid_done, 2)
            for kv in range(2):
                mm(PS[0:NCMP, 3, P * kv:P * (kv + 1)], hid[:, 1, NCMP * kv:NCMP * (kv + 1)], w2[:, 1, :],
                   start=True, stop=True).then_inc(kcv_pe, 1)
            pe.wait_ge(kc_sq, 1)
            mm(PS[:, 2, 64:64 + 2 * NCMP], ones[:, :], hid2[:, 0, :], start=True, stop=True).then_inc(kc_ss, 1)
            pe.wait_ge(ada_acc, ADA_STEPS)
            for n in range(2 * KT):
                last = mm(PS[:, 7, 128 + n:129 + n], acc[:, n // KT, P * (n % KT):P * (n % KT + 1)],
                          ones[:, 0:1], start=True, stop=True)
            last.then_inc(mod2_pe, 1)
            pe.wait_ge(norm_done, 28)
            pe.wait_ge(kc_ready, 1)
            pe.wait_ge(vc_ready, 1)
            pe.wait_ge(mod2_done, 2)

            def nsa_scores(h, win):
                kv = h // 4
                scores(UF + 2 * h + win, lambda t: nq[:, h, P * t:P * (t + 1)],
                       lambda n: nk[:, 2 * win + kv, 0:n])

            def cmp_scores(h):
                if h >= 1:
                    pe.wait_ge(pct_sb, h)
                for t in range(ST):
                    o = PS[:, 7, NSMALL * t:NSMALL * t + NCMP]
                    mm(o, nq[:, h, P * t:P * (t + 1)], kc[:, h // 4, 0:NCMP], start=True, stop=False)
                    last = mm(o, cmp_bias[:, h, P * t:P * (t + 1)], flipc[:, :], start=False, stop=True)
                last.then_inc(sc_pe, 1)

            pe.wait_ge(flip_sb, NH)
            pe.wait_ge(cmpb_in, 16 * NH)
            nsa_scores(0, 0)
            for h in range(NH):
                kv = h // 4
                for win in range(2):
                    u = UF + 2 * h + win
                    transposes(u)
                    if win == 0:
                        nsa_scores(h, 1)
                        cmp_scores(h)
                        if h >= 1:
                            pe.wait_ge(o_sb, UF + h)
                    else:
                        if h + 1 < NH:
                            nsa_scores(h + 1, 0)
                        pe.wait_ge(pc_done, h + 1)
                        for t in range(ST):
                            last = tr(PS[0:NCMP, 7, P * t:P * (t + 1)], probc[:, t, 0:NCMP], ident[:, :])
                        last.then_inc(pct_pe, 1)
                    values(u, lambda kb, c0=2 * P * win + P * kv: nv[:, kb, c0:c0 + P], win == 0, False).then_inc(pv_done, 1)
                pe.wait_ge(pct_sb, h + 1)
                mm(PS[:, 6, :], vc[:, kv, :], probcT[:, :], start=False, stop=True).then_inc(o_pe, 1)

            def nsa_mean():
                pe.wait_ge(ss_acc, 2 * NH)
                mm(PS[:, 0, :], ones[:, :], ssn[:, :], start=True, stop=True).then_inc(ssy_pe, 1)

            pe.wait_ge(o_sb, 2 * NH)
            for g in range(G_OUT, G_FF):
                if g == G_OUT + 1:
                    pe.wait_ge(ry_done, 2)
                gemm(GCH * g, bank(g, 0), uses(g), columns_tile,
                     before=(lambda k: pe.wait_ge(y_lo, k + 1)) if g == G_OUT else None,
                     mid=nsa_mean if g == G_OUT else None)
            pe.wait_ge(x1_acc, KT)
            pe.wait_ge(bank_free[0], uses(16))
            mm(PS[:, 0, :], ones[:, :], ssf[:, :], start=True, stop=True).then_inc(ssh_pe, 1)
            pe.wait_ge(rh_done, 1)

            def down_tile(half):
                def tile(b, slot, kk, t, k, start, stop):
                    f = CK * half + kk
                    return columns_tile(b, slot, kk, t, k, half == 0 and kk == 0, half == 1 and kk == 1,
                                        ghi[:, f, :], glo[:, f, :])
                return tile

            def down_group(c, dg, first, used, lots=None, mid=None):
                for half in range(2):
                    j = 2 * dg + half
                    pe.wait_ge(w_lo, c + j + 1)
                    for t in range(4):
                        if half == 0:
                            pe.wait_ge(bank_free[first + t], used)
                        for kk in range(CK):
                            if lots is not None and t == 0:
                                pe.wait_ge(g_lo, lots + CK * half + kk + 1)
                            last = down_tile(half)(first + t, j % NW, kk, t, 0, None, None)
                        if half == 1 and t < 3:
                            last.then_inc(tile_done, 1)
                    last.then_inc(w_used, 1)
                    if half == 0 and mid is not None:
                        mid()

            c = GCH * G_FF
            gemm(c, 4, uses(15), columns_tile, before=lambda k: pe.wait_ge(h2_lo, k + 1))
            with pe.Fori(0, NFB - 1) as i:
                at_i = c + GCH + 3 * GCH * i
                gemm(at_i, 0, uses(16) + 3 * i, columns_tile)
                gemm(at_i + GCH, 4, uses(15) + 1 + 3 * i, columns_tile)
                for dg in range(4):
                    used = (uses(16) + 1 + 3 * i, uses(15) + 2 + 3 * i)[dg % 2] + dg // 2
                    down_group(at_i + 2 * GCH, dg, 4 * (dg % 2), used, 4 * i if dg == 0 else None)
            n = NFB - 1
            last_c = c + GCH + 3 * GCH * n
            gemm(last_c, 0, uses(16) + 3 * n, columns_tile)
            def by_token(dg, first):
                for t in range(4):
                    pe.wait_ge(bank_free[(0, 4, 0, 0)[dg] + t], final[dg])
                for t in range(ST):
                    b = first + t
                    if dg == 0:
                        pe.wait_ge(bank_free[b], final[1])
                    if dg in (1, 2):
                        pe.wait_ge(fin_sb, 4 * (dg - 1) + t + 1)
                    for d in range(4):
                        last = tr(PS[:, b, P * d:P * (d + 1)], xT[:, 4 * dg + d, P * t:P * (t + 1)], ident[:, :])
                    last.then_inc(fin_pe, 1)

            used0, used1 = uses(16) + 1 + 3 * n, uses(15) + 1 + 3 * n
            final = (used0 + 1, used1 + 1, used0 + 2, used0 + 3)
            down_group(last_c + GCH, 0, 0, used0, 4 * n)
            down_group(last_c + GCH, 1, 4, used1)
            down_group(last_c + GCH, 2, 0, used0 + 1)
            by_token(0, 4)
            down_group(last_c + GCH, 3, 0, used0 + 2, mid=lambda: by_token(1, 4))
            by_token(2, 4)
            by_token(3, 0)

        @block.scalar
        def _(act):
            f = nc.scalar.activation
            act.preload_act_table_set("natural_log_exp_and_others")
            act.wait_ge(consts, 1)
            act.wait_ge(par_done, 3)
            f(t16[:, :], par[:, R_C:R_C + KT], ACT.Exp, scale=-1.0).then_inc(exp_c, 1)
            for t in range(ST):
                act.wait_ge(x_in[t], 16)
                f(sq_first[:, :], xnat[:, t, :], ACT.Square, accum_out=ssx[:, t:t + 1]).then_inc(act_s, 1)
                act.wait_ge(act_s, t + 1)
            f(rx[:, :], ssx[:, :], ACT.Ln, bias=eps[:, :], scale=1.0 / D).then_inc(act_s, 1)
            act.wait_ge(act_s, ST + 1)
            f(rx[:, :], rx[:, :], ACT.Exp, scale=-0.5).then_inc(rx_done, 1)
            for k in range(KT):
                act.wait_ge(xt_pe, k + 1)
                f(xt0[:, k, :], PS[:, k % 8, :], ACT.Copy).then_inc(xt_sb, 1)
            for b in range(4):
                act.wait_ge(line_pe, b + 1)
                n = (NREV + NFWD) // 4
                f(line[:, n * b:n * (b + 1)], PS[0:NH, b, 0:n], ACT.Copy).then_inc(line_sb, 1)
            act.wait_ge(line_sb, 4)
            for b in range(7):
                act.sem_inc(bank_free[b], 1)

            def hi(c):
                if c // GCH == 9:
                    act.wait_ge(split_in[c % NSTAGE], 16 * (c % GCH // NSTAGE + 1))
                act.wait_ge(stage_in[c % NSTAGE], 16 * (c // NSTAGE + 1))
                if c >= NW:
                    act.wait_ge(w_used, c - NW + 1)
                f(whi[:, c % NW, :, :], stage[:, c % NSTAGE, :, :], ACT.Copy).then_inc(w_hi, 1)

            def hi_at(c, j):
                act.wait_ge(stage_in[j % NSTAGE], (c + j - j % NSTAGE) * 4 + 16)
                act.wait_ge(w_used, c + j - NW + 1)
                f(whi[:, j % NW, :, :], stage[:, j % NSTAGE, :, :], ACT.Copy).then_inc(w_hi, 1)

            def square_tiles(g):
                for t in range(4):
                    act.wait_ge(evac, normed_before(g) + t + 1)
                    f(sq[:, t, :], PS[:, bank(g, t), :], ACT.Square).then_inc(sq_done, 1)

            def norm_factors(g):
                for t in range(4):
                    n = normed_before(g) + t + 1
                    act.wait_ge(ss_pe, n)
                    if n > 4:
                        act.wait_ge(norm_done, n - 4)
                    b = bank(g, t)
                    f(rb[:, t, :], PS[:, b, :], ACT.Ln, bias=eps[:, :], scale=1.0 / P).then_inc(bank_free[b], 1)
                    act.wait_ge(bank_free[b], uses(g + 2))
                    f(rb[:, t, :], rb[:, t, :], ACT.Exp, scale=-0.5).then_inc(r_done, 1)

            def project_in(g):
                for j in range(2 if g in (2, 6) else 0, GCH):
                    hi(GCH * g + j)
                    if g - 1 in NORMED and j == 1:
                        square_tiles(g - 1)
                    if g == 3 and j == 1:
                        gates()
                    if g == 6 and j == 5:
                        mean_factor(1, 7, ssf, NH * P)
                    if g - 1 in NORMED and j == 5:
                        norm_factors(g - 1)

            for j in range(GCH):
                hi(2 * j)
                act.wait_ge(mod_ready, j + 1)
                for k in (2 * j, 2 * j + 1):
                    act.wait_ge(xn_done, k + 1)
                    if k >= 4:
                        act.wait_ge(h_lo, k - 3)
                    f(h1t[:, k % 4, :], xn[:, k, :], ACT.Identity, bias=mod[:, 0, k:k + 1],
                      scale=mod[:, 1, k:k + 1]).then_inc(h_full, 1)
                for k in (2 * j, 2 * j + 1):
                    act.wait_ge(h_full, k + 1)
                    f(hhi[:, k, :], h1t[:, k % 4, :], ACT.Copy).then_inc(h_hi, 1)
                hi(2 * j + 1)
            square_tiles(0)
            hi(2 * GCH)
            hi(2 * GCH + 1)
            norm_factors(0)
            square_tiles(1)
            act.wait_ge(small_in, 32)
            f(wsmall_hi[:, :, :], wsmall[:, :, :], ACT.Copy).then_inc(ws_hi, 1)

            def gates():
                act.wait_ge(small_pe, 1)
                f(fl2[:, :], PS[0:NSMALL, 7, :], ACT.Exp, scale=-1.0).then_inc(gates_e, 1)
                act.wait_ge(z_done, 1)
                f(fb[:, :], fb[:, :], ACT.Exp, scale=-1.0).then_inc(fexp, 1)
                act.wait_ge(fexp, 1)
                f(fb[:, :], fb[:, :], ACT.Ln, bias=ones[0:NH, 0:1]).then_inc(fexp, 1)

            for g in range(2, 6):
                project_in(g)

            def exp_tiles(u, fox):
                for i, t in enumerate(TS):
                    b, c0 = S_AT[t]
                    p0, n = parts(t)
                    act.wait_ge(s_max, 4 * u + (4 if fox and i == 2 else i + 1))
                    src = PS[:, b, c0:c0 + n] if fox else prob[:, p0:p0 + n]
                    f(prob[:, p0:p0 + n], src, ACT.Exp, bias=nmax[:, t:t + 1], scale=1.0 if fox else -1.0,
                      accum_out=psum_row[:, t:t + 1]).then_inc(s_exp, 1)

            def transposed_out(u):
                act.wait_ge(t_pe, 4 * (u + 1))
                if u >= 1:
                    act.wait_ge(pv_done, u)
                f(probT[:, 0:S], PS[:, 3, :], ACT.Copy).then_inc(t_act, 1)

            def head_out(n, dst):
                if n < UF:
                    act.wait_ge(pv_done, n + 1)
                else:
                    act.wait_ge(o_pe, n - UF + 1)
                f(dst, PS[:, 6, :], ACT.Copy)
                if n >= 1:
                    act.wait_ge(ss_acc, n)
                f(o_sq[:, :], PS[:, 6, :], ACT.Square).then_inc(o_sb, 1)

            def mean_factor(n, b, dst, width):
                act.wait_ge(ssy_pe, n)
                f(dst[:, :], PS[:, b, :], ACT.Ln, bias=eps[:, :], scale=1.0 / width).then_inc(ry_ln, 1)
                act.wait_ge(ry_ln, n)
                f(dst[:, :], dst[:, :], ACT.Exp, scale=-0.5).then_inc(ry_done, 1)

            exp_tiles(0, True)
            for h in range(NH):
                transposed_out(h)
                if h + 1 < NH:
                    exp_tiles(h + 1, True)
                if h == NH - 2:
                    hi(GCH * 6)
                    hi(GCH * 6 + 1)
                head_out(h, fq[:, h, :])

            for g in range(6, 11):
                project_in(g)

            for h in range(NH):
                act.wait_ge(flip_pe, h + 1)
                f(rel[:, h, :], PS[:, 4 + h % 3, :], ACT.Copy).then_inc(flip_sb, 1)
            for b in range(2):
                act.wait_ge(hid_pe, b + 1)
                f(hid2[:, b, :], PS[:, b, 0:2 * NCMP], ACT.Exp, scale=-1.0).then_inc(hid_exp, 1)
            act.wait_ge(kcv_pe, 3)
            act.wait_ge(kc_copied, 1)
            f(hid2[:, 0, :], PS[:, 2, 0:2 * NCMP], ACT.Square).then_inc(kc_sq, 1)
            act.wait_ge(kc_ss, 1)
            f(hid2[:, 1, :], PS[:, 2, 64:64 + 2 * NCMP], ACT.Ln, bias=eps[:, :], scale=1.0 / P).then_inc(kc_ln, 1)
            act.wait_ge(kc_ln, 1)
            f(hid2[:, 1, :], hid2[:, 1, :], ACT.Exp, scale=-0.5).then_inc(kc_r, 1)

            def mixed_hi(k):
                act.wait_ge(y_full, k + 1)
                f(hhi[:, k, :], (fq if k < NH else nq)[:, k % NH, :], ACT.Copy).then_inc(y_hi, 1)

            exp_tiles(UF, False)
            for h in range(NH):
                for win in range(2):
                    u = UF + 2 * h + win
                    transposed_out(u)
                    if win == 0:
                        exp_tiles(u + 1, False)
                        act.wait_ge(sc_sub, h + 1)
                        f(probc[:, :, 0:NCMP], probc[:, :, 0:NCMP], ACT.Exp).then_inc(sc_exp, 1)
                    else:
                        if h + 1 < NH:
                            exp_tiles(u + 1, False)
                        act.wait_ge(pct_pe, h + 1)
                        f(probcT[:, :], PS[0:NCMP, 7, :], ACT.Copy).then_inc(pct_sb, 1)
                mixed_hi(h)
                if h == NH - 2:
                    hi(GCH * G_OUT)
                    hi(GCH * G_OUT + 1)
                head_out(UF + h, nq[:, h, :])

            hi(GCH * G_OUT + 2)
            hi(GCH * G_OUT + 3)
            mean_factor(2, 0, ssn, NH * P)
            for k in range(NH, KT):
                mixed_hi(k)
                if k % 2 == 1:
                    hi(GCH * G_OUT + k // 2)

            def square_x1(g):
                for t in range(4):
                    n = 4 * (g - G_OUT) + t
                    act.wait_ge(bank_free[bank(g, t)], uses(g + 2))
                    if n >= 2:
                        act.wait_ge(x1_acc, n - 1)
                    f(x1_sqt[:, n % 2, :], xT[:, n, :], ACT.Square).then_inc(x1_sq, 1)

            for g in range(G_OUT + 1, G_FF):
                for j in range(GCH):
                    hi(GCH * g + j)
                    if g > G_OUT and j == 1:
                        square_x1(g - 1)
            c = GCH * G_FF
            hi(c)
            hi(c + 1)
            square_x1(G_FF - 1)
            act.wait_ge(ssh_pe, 1)
            f(ssf[:, :], PS[:, 0, :], ACT.Ln, bias=eps[:, :], scale=1.0 / D).then_inc(rh_ln, 1)
            act.wait_ge(rh_ln, 1)
            f(ssf[:, :], ssf[:, :], ACT.Exp, scale=-0.5).then_inc(rh_done, 1)
            for k in range(KT):
                act.wait_ge(h2_t, k + 1)
                f(hhi[:, k, :], h2t[:, k % 4, :], ACT.Identity, bias=mod[:, 3, k:k + 1]).then_inc(h2_hi, 1)
                if k >= 3 and k % 2 == 1:
                    hi(c + (k + 1) // 2)

            def silu_tiles(tiles, chunks):
                for t in range(4):
                    await_ff(act, t, tiles, chunks)
                    f(silu_g[:, t, :], PS[:, 4 + t, :], ACT.Silu).then_inc(bank_free[4 + t], 1)

            def high_of_g(i):
                for t in range(4):
                    act.wait_ge(bank_free[t], uses(16) + 3 * i + 1)
                    f(ghi[:, t, :], gfull[:, t, :], ACT.Copy).then_inc(g_hi, 1)

            hi(c + GCH + 1)
            silu_tiles(3 * G_FF, c + GCH)
            with act.Fori(0, NFB - 1) as i:
                at_i = c + GCH + 3 * GCH * i
                for j in range(2, 3 * GCH + 2):
                    hi_at(at_i, j)
                    if j == GCH + 2:
                        high_of_g(i)
                    if j == 2 * GCH + 1:
                        silu_tiles(3 * (G_FF + 2) + 18 * i, at_i + 2 * GCH)
            n = NFB - 1
            at_n = c + GCH + 3 * GCH * n
            for j in range(2, 2 * GCH):
                hi(at_n + j)
                if j == GCH + 1:
                    high_of_g(n)
            for dg in range(4):
                if dg >= 2:
                    act.wait_ge(out_sent[dg % 2], 16 * ST)
                for t in range(ST) if dg < 3 else (0, 2):
                    act.wait_ge(fin_pe, 4 * dg + t + 1)
                    b = (4 if dg < 3 else 0) + t
                    f(ostage[:, dg % 2, t, :], PS[:, b, :], ACT.Copy).then_inc(fin_sb, 1)

        @block.vector
        def _(dve):
            v = nc.vector
            own = [0]

            def then(ins):
                own[0] += 1
                ins.then_inc(dve_s, 1)
                dve.wait_ge(dve_s, own[0])

            dve.wait_ge(par_t, 3)
            v.tensor_copy(par[:, :], PS[:, 0, 0:NPAR]).then_inc(par_done, 1)
            v.tensor_copy(adab[:, :], PS[:, 1, 0:96]).then_inc(par_done, 1)
            v.tensor_copy(cpos[:, :], PS[:, 2, 0:2 * CB]).then_inc(par_done, 1)
            dve.wait_ge(par_done, 3)
            then(v.tensor_scalar(par[:, R_FQ:R_FQ + 1], par[:, R_FQ:R_FQ + 1], SCALE, None, ALU.mult))
            then(v.tensor_scalar(par[:, R_NQ:R_NQ + 1], par[:, R_NQ:R_NQ + 1], SCALE, None, ALU.mult))
            dve.wait_ge(exp_c, 1)
            then(v.tensor_scalar(t16[:, :], t16[:, :], 1.0, None, ALU.add))
            then(v.reciprocal(t16[:, :], t16[:, :]))
            then(v.tensor_tensor(silu_c[:, :], t16[:, :], par[:, R_C:R_C + KT], ALU.mult))
            dve.wait_ge(rx_done, 1)
            dve.wait_ge(consts, 1)
            for t in range(ST):
                v.tensor_scalar(diag[:, t, :], ident[:, :], rx[:, t:t + 1], None, ALU.mult).then_inc(diag_done, 1)
            dve.wait_ge(rb_pe, 1)
            v.tensor_copy(ssf[:, :], PS[:, 7, :]).then_inc(bank_free[7], 1)

            def lo(c):
                dve.wait_ge(w_hi, c + 1)
                v.tensor_tensor(wlo[:, c % NW, :, :], stage[:, c % NSTAGE, :, :], whi[:, c % NW, :, :].bitcast(F32),
                                ALU.subtract).then_inc(w_lo, 1)

            def h_low(k):
                dve.wait_ge(h_hi, k + 1)
                v.tensor_tensor(hlo[:, k, :], h1t[:, k % 4, :], hhi[:, k, :].bitcast(F32),
                                ALU.subtract).then_inc(h_lo, 1)

            def partial_out(j):
                dve.wait_ge(w_used, 2 * j + 2)
                if j == 0:
                    v.tensor_copy(partial[:, :], PS[:, 7, :]).then_inc(part_out, 1)
                else:
                    dve.wait_ge(part_out, j)
                    v.tensor_tensor(partial[:, :], PS[:, 7, :], partial[:, :], ALU.add).then_inc(part_out, 1)

            for j in range(GCH):
                for k in range(KT):
                    if k % 4 == 0:
                        dve.wait_ge(first_in[k // 4], 32 * (j + 1))
                    part = acc_first[:, k % 2, :]
                    src = ada_first[k // 4][:, k % 4, :, :].rearrange("p c n -> p (c n)")
                    if k < 2:
                        v.tensor_scalar(part, src, silu_c[:, k:k + 1], None, ALU.mult).then_inc(first_acc, 1)
                    else:
                        dve.wait_ge(first_acc, KT * j + k - 1)
                        v.scalar_tensor_tensor(out=part, in0=src, scalar=silu_c[:, k:k + 1], in1=part,
                                               op0=ALU.mult, op1=ALU.add).then_inc(first_acc, 1)
                    if k == 3 and j >= 1:
                        h_low(2 * j - 2)
                        h_low(2 * j - 1)
                    if k == 9 and j >= 1:
                        lo(2 * j - 1)
                    if k == 11 and j >= 2:
                        partial_out(j - 2)
                lo(2 * j)
                dve.wait_ge(mod_pe, j + 1)
                ks = slice(CK * j, CK * (j + 1))
                then(v.tensor_tensor(mod[:, 0:2, ks], PS[:, 7, 0:2 * CK].rearrange("p (c k) -> p c k", c=2),
                                     adab[:, 0:2 * KT].rearrange("p (c k) -> p c k", c=2)[:, :, ks], ALU.add))
                v.scalar_tensor_tensor(out=mod[:, 1, ks], in0=mod[:, 1, ks], scalar=1.0,
                                       in1=par[:, R_N1 + CK * j:R_N1 + CK * (j + 1)],
                                       op0=ALU.add, op1=ALU.mult).then_inc(mod_ready, 1)
            h_low(KT - 2)
            h_low(KT - 1)
            lo(2 * GCH - 1)
            partial_out(GCH - 2)

            def lo_at(c, j):
                dve.wait_ge(w_hi, c + j + 1)
                v.tensor_tensor(wlo[:, j % NW, :, :], stage[:, j % NSTAGE, :, :], whi[:, j % NW, :, :].bitcast(F32),
                                ALU.subtract).then_inc(w_lo, 1)

            def ada(a):
                k, half = a % 32 // 2, a % 2
                part = acc[:, a // 32 % 2, 1024 * half:1024 * (half + 1)]
                dve.wait_ge(ada_in[a % 3], 16 * (a // 3 + 1))
                src = ada_ring[:, a % 3, :]
                if k == 0:
                    v.tensor_scalar(part, src, silu_c[:, 0:1], None, ALU.mult).then_inc(ada_acc, 1)
                else:
                    dve.wait_ge(ada_acc, a - 1)
                    v.scalar_tensor_tensor(out=part, in0=src, scalar=silu_c[:, k:k + 1], in1=part,
                                           op0=ALU.mult, op1=ALU.add).then_inc(ada_acc, 1)

            def tiles_out(g):
                for t in range(4):
                    await_tile(dve, g, t)
                    if g in NORMED:
                        v.tensor_scalar(tile_of(g, t), PS[:, bank(g, t), :], gain_of(g, t), None,
                                        ALU.mult).then_inc(evac, 1)
                    else:
                        v.tensor_copy(tile_of(g, t), PS[:, bank(g, t), :]).then_inc(bank_free[bank(g, t)], 1)

            def normalise(g):
                for t in range(4):
                    dve.wait_ge(r_done, normed_before(g) + t + 1)
                    v.tensor_tensor(tile_of(g, t), tile_of(g, t), rb[:, t, :], ALU.mult).then_inc(norm_done, 1)

            def mixed(k, low):
                y = (fq if k < NH else nq)[:, k % NH, :]
                if not low:
                    dve.wait_ge(ry_done, 1 if k < NH else 2)
                    v.scalar_tensor_tensor(out=y, in0=y, scalar=par[:, R_MIX + k:R_MIX + k + 1],
                                           in1=(ssf if k < NH else ssn)[:, :], op0=ALU.mult,
                                           op1=ALU.mult).then_inc(y_full, 1)
                else:
                    dve.wait_ge(y_hi, k + 1)
                    v.tensor_tensor(hlo[:, k, :], y, hhi[:, k, :].bitcast(F32), ALU.subtract).then_inc(y_lo, 1)

            def project_in(g, first=0):
                for j in range(first, GCH):
                    lo(GCH * g + j)
                    for a in plan[g, j]:
                        ada(a)
                    if g != 6 and j == 1:
                        if g == 3:
                            dve.wait_ge(xt_out, 16)
                        tiles_out(g - 1)
                    if g == 3 and j == 1:
                        forget_and_gates()
                    if g - 1 in NORMED and j == 6:
                        normalise(g - 1)

            def forget_and_gates():
                dve.wait_ge(gates_e, 1)
                then(v.tensor_scalar(fl[0:NH, :], PS[0:NH, 7, :], fbias[:, :], None, ALU.add))
                dve.sem_inc(small_out, 1)
                then(v.tensor_scalar(fa[:, :], fl[0:NH, :], -1.0, None, ALU.mult))
                v.tensor_tensor(fb[:, :], fl[0:NH, :], fa[:, :], ALU.max).then_inc(z_done, 1)
                dve.wait_ge(z_done, 1)
                then(v.tensor_scalar(fa[:, :], fl[0:NH, :], 0.0, None, ALU.min))
                dve.wait_ge(fexp, 2)
                then(v.tensor_tensor(fa[:, :], fb[:, :], fa[:, :], ALU.subtract))
                then(v.memset(fb[:, :], 1.0))
                then(v.tensor_tensor_scan(fl[0:NH, :], fb[:, :], fa[:, :], 0.0, ALU.mult, ALU.add))
                dve.wait_ge(sel_ready, 1)
                v.tensor_copy(cumb[0:NH, :], fl[0:NH, :]).then_inc(forget_ready, 1)
                dve.wait_ge(forget_ready, 1)
                then(v.tensor_tensor(fa[:, :], fl[0:NH, :], cumb[0:NH, :], ALU.subtract))
                then(v.tensor_copy(cumt[:, :], fa[:, :]))
                v.tensor_copy(cumb[32:32 + NH, :], cumt[:, :]).then_inc(forget_ready, 1)
                then(v.tensor_tensor(fa[:, :], fa[:, :], cumt[:, :], ALU.subtract))
                v.tensor_copy(cumb[64:64 + NH, :], fa[:, :]).then_inc(forget_ready, 1)
                then(v.tensor_scalar(fl2[:, :], fl2[:, :], 1.0, None, ALU.add))
                v.reciprocal(fl2[:, :], fl2[:, :]).then_inc(gates_ready, 1)
            tiles_out(0)
            lo(2 * GCH)
            lo(2 * GCH + 1)
            tiles_out(1)
            normalise(0)
            dve.wait_ge(ws_hi, 1)
            v.tensor_tensor(wsmall_lo[:, :, :], wsmall[:, :, :], wsmall_hi[:, :, :].bitcast(F32),
                            ALU.subtract).then_inc(ws_lo, 1)
            project_in(2, 2)
            for g in range(3, 6):
                project_in(g)
            tiles_out(5)

            def modulation(n, first):
                dve.wait_ge(mod2_pe, n)
                then(v.tensor_tensor(mod[:, first:first + 2, :],
                                     PS[:, 7, 128:128 + 2 * KT].rearrange("p (c k) -> p c k", c=2),
                                     adab[:, KT * first:KT * (first + 2)].rearrange("p (c k) -> p c k", c=2), ALU.add))

            def score_tile(u, i, h):
                t = TS[i]
                b, c0 = S_AT[t]
                n = P * (t + 1)
                dve.wait_ge(s_pe, 4 * u + (i + 1 if i < 2 else 4))
                src = PS[:, b, c0:c0 + n]
                if u < UF:
                    v.tensor_reduce(nmax[:, t:t + 1], src, AX.X, ALU.max, negate=True).then_inc(s_max, 1)
                else:
                    p0 = P_SB[t]
                    v.tensor_tensor_reduce(out=prob[:, p0:p0 + n], in0=src, in1=rel[:, h, P * (3 - t):S],
                                           scale=-1.0, scalar=3e38, op0=ALU.add, op1=ALU.min,
                                           accum_out=nmax[:, t:t + 1]).then_inc(s_max, 1)

            def prob_tile(u, i, gate_of):
                t = TS[i]
                p0, n = parts(t)
                dve.wait_ge(s_exp, 4 * u + i + 1)
                then(v.reciprocal(rinv[:, t:t + 1], psum_row[:, t:t + 1]))
                v.tensor_scalar(prob[:, p0:p0 + n], prob[:, p0:p0 + n], rinv[:, t:t + 1], gate_of(t),
                                ALU.mult, ALU.mult if gate_of(t) is not None else ALU.bypass).then_inc(p_done, 1)

            def unit_scores(u, h, gate_of):
                score_tile(u, 0, h)
                score_tile(u, 1, h)
                prob_tile(u, 0, gate_of)
                score_tile(u, 2, h)
                score_tile(u, 3, h)
                prob_tile(u, 1, gate_of)
                prob_tile(u, 2, gate_of)
                prob_tile(u, 3, gate_of)

            def transposed_out(u):
                if u >= 1:
                    dve.wait_ge(pv_done, u)
                dve.wait_ge(t_pe, 4 * u + 2)
                v.tensor_copy(probT[:, T_SB[2]:T_SB[2] + 256], PS[:, 5, 0:256]).then_inc(t_dve, 1)
                dve.wait_ge(t_pe, 4 * u + 3)
                v.tensor_copy(probT[:, T_SB[1]:T_SB[1] + S], PS[:, 4, :]).then_inc(t_dve, 1)

            def sum_squares(n, dst):
                dve.wait_ge(o_sb, n + 1)
                if n % NH == 0:
                    v.tensor_copy(dst[:, :], o_sq[:, :]).then_inc(ss_acc, 1)
                else:
                    dve.wait_ge(ss_acc, n)
                    v.tensor_tensor(dst[:, :], dst[:, :], o_sq[:, :], ALU.add).then_inc(ss_acc, 1)

            unit_scores(0, 0, lambda t: None)
            dve.wait_ge(gates_pe, 1)
            dve.wait_ge(mod2_pe, 1)
            v.tensor_copy(gate[:, :, :], PS[:, 7, 0:ST * NSMALL].rearrange("p (t n) -> p t n", t=ST)).then_inc(gates_nat, 1)
            modulation(1, 2)
            dve.sem_inc(mod2_done, 1)
            for h in range(NH):
                transposed_out(h)
                if h + 1 < NH:
                    unit_scores(h + 1, h + 1, lambda t: None)
                if h >= 1:
                    sum_squares(h - 1, ssf)
                if h == NH - 2:
                    lo(GCH * 6)
                    lo(GCH * 6 + 1)
            sum_squares(NH - 1, ssf)

            for a in (*plan[6, 0], *plan[6, 1]):
                ada(a)
            project_in(6, 2)
            for g in range(7, 11):
                project_in(g)
            tiles_out(10)

            for b in range(2):
                for j in range(CB):
                    for kv in range(2):
                        src = nk[:, 4 + 2 * b + kv, j:j + CS * (NCMP - 1) + 1:CS]
                        last = v.tensor_scalar(unfold[:, b, j, NCMP * kv:NCMP * (kv + 1)], src,
                                               cpos[:, CB * b + j:CB * b + j + 1], None, ALU.add)
                last.then_inc(unf, 1)
            for b in range(2):
                dve.wait_ge(hid_exp, b + 1)
                then(v.tensor_scalar(hid2[:, b, :], hid2[:, b, :], 1.0, None, ALU.add))
                then(v.reciprocal(hid2[:, b, :], hid2[:, b, :]))
                v.tensor_tensor(hid[:, b, :], hid2[:, b, :], PS[:, b, 0:2 * NCMP], ALU.mult).then_inc(hid_done, 1)
            dve.wait_ge(kcv_pe, 1)
            kcs = PS[:, 2, 0:2 * NCMP].rearrange("p (h c) -> p h c", h=2)
            v.tensor_scalar(kc[:, :, 0:NCMP], kcs, par[:, R_NK:R_NK + 1], None, ALU.mult).then_inc(kc_copied, 1)
            dve.wait_ge(kc_r, 1)
            v.tensor_tensor(kc[:, :, 0:NCMP], kc[:, :, 0:NCMP], hid2[:, 1, :].rearrange("p (h c) -> p h c", h=2),
                            ALU.mult).then_inc(kc_ready, 1)
            dve.wait_ge(kcv_pe, 3)
            v.tensor_copy(vc[:, :, :], PS[0:NCMP, 3, 0:2 * P].rearrange("p (h d) -> p h d", h=2)).then_inc(vc_ready, 1)
            modulation(2, 4)
            then(v.scalar_tensor_tensor(out=mod[:, 4, :], in0=mod[:, 4, :], scalar=1.0, in1=par[:, R_N2:R_N2 + KT],
                                        op0=ALU.add, op1=ALU.mult))
            dve.sem_inc(mod2_done, 1)
            dve.wait_ge(flip_sb, NH)
            dve.wait_ge(consts, 1)

            def gate_at(h, branch):
                return lambda t: gate[:, t, NH + 3 * h + branch:NH + 3 * h + branch + 1]

            def cmp_probs(h):
                dve.wait_ge(sc_pe, h + 1)
                s = PS[:, 7, 0:ST * NSMALL].rearrange("p (t n) -> p t n", t=ST)[:, :, 0:NCMP]
                then(v.tensor_reduce(cmax[:, :], s, AX.X, ALU.max))
                if h >= 1:
                    dve.wait_ge(pct_pe, h)
                v.tensor_tensor(probc[:, :, 0:NCMP], s, cmax[:, :].unsqueeze(2).to_broadcast([P, ST, NCMP]),
                                ALU.subtract).then_inc(sc_sub, 1)

            def cmp_weights(h):
                dve.wait_ge(sc_exp, h + 1)
                then(v.tensor_reduce(csum[:, :], probc[:, :, 0:NCMP], AX.X, ALU.add))
                then(v.reciprocal(csum[:, :], csum[:, :]))
                then(v.tensor_tensor(csum[:, :], csum[:, :], gate[:, :, NH + 3 * h], ALU.mult))
                then(v.tensor_tensor(csum[:, :], csum[:, :], rowok[:, :], ALU.mult))
                v.tensor_tensor(probc[:, :, 0:NCMP], probc[:, :, 0:NCMP],
                                csum[:, :].unsqueeze(2).to_broadcast([P, ST, NCMP]), ALU.mult).then_inc(pc_done, 1)

            unit_scores(UF, 0, gate_at(0, 1))
            for h in range(NH):
                for win in range(2):
                    u = UF + 2 * h + win
                    transposed_out(u)
                    if win == 0:
                        unit_scores(u + 1, h, gate_at(h, 2))
                        cmp_probs(h)
                        mixed(h, False)
                        if h >= 1:
                            sum_squares(UF + h - 1, ssn)
                    else:
                        cmp_weights(h)
                        if h + 1 < NH:
                            unit_scores(u + 1, h + 1, gate_at(h + 1, 1))
                if h == NH - 2:
                    lo(GCH * G_OUT)
                    lo(GCH * G_OUT + 1)
                mixed(h, True)
            sum_squares(2 * NH - 1, ssn)

            lo(GCH * G_OUT + 2)
            lo(GCH * G_OUT + 3)
            for k in range(NH, KT + 1):
                if k < KT:
                    mixed(k, False)
                if k > NH:
                    mixed(k - 1, True)
                    if k % 2 == 0:
                        lo(GCH * G_OUT + k // 2 - 1)

            def x1_tiles(g):
                dve.wait_ge(xT_in, 16)
                for t in range(4):
                    n = 4 * (g - G_OUT) + t
                    await_tile(dve, g, t)
                    v.scalar_tensor_tensor(out=xT[:, n, :], in0=PS[:, bank(g, t), :], scalar=mod[:, 2, n:n + 1],
                                           in1=xT[:, n, :], op0=ALU.mult, op1=ALU.add).then_inc(bank_free[bank(g, t)], 1)
                for n in range(4 * (g - G_OUT), 4 * (g - G_OUT) + 4):
                    dve.wait_ge(x1_sq, n + 1)
                    if n == 0:
                        v.tensor_copy(ssf[:, :], x1_sqt[:, 0, :]).then_inc(x1_acc, 1)
                    else:
                        dve.wait_ge(x1_acc, n)
                        v.tensor_tensor(ssf[:, :], ssf[:, :], x1_sqt[:, n % 2, :], ALU.add).then_inc(x1_acc, 1)

            for g in range(G_OUT + 1, G_FF):
                for j in range(GCH):
                    lo(GCH * g + j)
                    if g > G_OUT and j == 1:
                        x1_tiles(g - 1)
            c = GCH * G_FF
            lo(c)
            lo(c + 1)
            x1_tiles(G_FF - 1)
            dve.wait_ge(rh_done, 1)
            for k in range(KT + 1):
                if k < KT:
                    if k >= 4:
                        dve.wait_ge(h2_lo, k - 3)
                    v.scalar_tensor_tensor(out=h2t[:, k % 4, :], in0=xT[:, k, :], scalar=mod[:, 4, k:k + 1],
                                           in1=ssf[:, :], op0=ALU.mult, op1=ALU.mult).then_inc(h2_t, 1)
                if k >= 1:
                    dve.wait_ge(h2_hi, k)
                    v.scalar_tensor_tensor(out=hlo[:, k - 1, :], in0=h2t[:, (k - 1) % 4, :], scalar=mod[:, 3, k - 1:k],
                                           in1=hhi[:, k - 1, :].bitcast(F32), op0=ALU.add,
                                           op1=ALU.subtract).then_inc(h2_lo, 1)
                    if k >= 4 and k % 2 == 0:
                        lo(c + k // 2)

            def silu_times_up(i, c, tiles=range(4)):
                for t in tiles:
                    await_ff(dve, t, 3 * (G_FF + 1) + 18 * i, c + GCH)
                    v.tensor_tensor(gfull[:, t, :], PS[:, t, :], silu_g[:, t, :], ALU.mult).then_inc(bank_free[t], 1)

            def low_of_g(i, tiles=range(4)):
                for t in tiles:
                    dve.wait_ge(g_hi, 4 * i + t + 1)
                    v.tensor_tensor(glo[:, t, :], gfull[:, t, :], ghi[:, t, :].bitcast(F32),
                                    ALU.subtract).then_inc(g_lo, 1)

            def down_out(dg, tiles, chunks, first=None):
                for t in range(4):
                    n = 4 * dg + t
                    await_ff(dve, t, tiles + 3 * dg, chunks + 2 * dg + 2)
                    b = (4 * (dg % 2) if first is None else first) + t
                    v.scalar_tensor_tensor(out=xT[:, n, :], in0=PS[:, b, :], scalar=mod[:, 5, n:n + 1],
                                           in1=xT[:, n, :], op0=ALU.mult, op1=ALU.add).then_inc(bank_free[b], 1)

            lo(c + GCH + 1)
            with dve.Fori(0, NFB - 1) as i:
                at_i = c + GCH + 3 * GCH * i
                for j in range(2, 3 * GCH + 2):
                    lo_at(at_i, j)
                    if j == GCH + 1:
                        silu_times_up(i, at_i)
                    if j == GCH + 3:
                        low_of_g(i)
                    if j > 2 * GCH + 2 and j % 2 == 1:
                        down_out((j - 2 * GCH - 3) // 2, 3 * (G_FF + 3) + 18 * i, at_i + 2 * GCH)
            n = NFB - 1
            at_n = c + GCH + 3 * GCH * n
            for j in range(2, GCH):
                lo(at_n + j)
            lo(at_n + GCH)
            lo(at_n + GCH + 1)
            for t in range(5):
                if t < 4:
                    silu_times_up(n, at_n, (t,))
                if t >= 1:
                    low_of_g(n, (t - 1,))
            for j in range(2, GCH + 2):
                if j < GCH:
                    lo(at_n + GCH + j)
                if j % 2 == 1:
                    dg = (j - 3) // 2
                    down_out(dg, 3 * (G_FF + 2) + 18 * n, at_n + GCH, (0, 4, 0, 0)[dg])
            dve.wait_ge(out_sent[1], 16 * ST)
            for t in (1, 3):
                dve.wait_ge(fin_pe, 12 + t + 1)
                v.tensor_copy(ostage[:, 1, t, :], PS[:, t, :]).then_inc(fin_last, 1)

        @block.gpsimd
        def _(pool):
            g = nc.gpsimd
            done = [0]

            def then(ins):
                done[0] += 1
                ins.then_inc(pool_s, 1)
                pool.wait_ge(pool_s, done[0])

            then(g.memset(ident[:, :], 0.0))
            then(g.affine_select(out=ident[:, :], in_=ident[:, :], pattern=[[-1, P]], compare_op=ALU.not_equal,
                                 fill=1.0, base=0, channel_multiplier=1))
            for f, n in ((flip, P), (flipc, NCMP)):
                then(g.memset(f[:, :], 0.0))
                then(g.affine_select(out=f[:, :], in_=f[:, :], pattern=[[1, n]], compare_op=ALU.not_equal,
                                     fill=1.0, base=1 - n, channel_multiplier=1))
            then(g.memset(ones[:, :], 1.0))
            then(g.memset(eps[:, :], EPS))
            then(g.memset(relb[NBUCKET:NBUCKET + 1, :], NEG))
            then(g.tensor_copy(identb[:, :], ident[:, :]))
            then(g.memset(maskb[:, :], 0.0))
            then(g.affine_select(out=maskb[:, :], in_=maskb[:, :], pattern=[[-1, P]], compare_op=ALU.is_ge,
                                 fill=NEG, base=0, channel_multiplier=1))
            then(g.memset(rowok[:, :], 1.0))
            g.affine_select(out=rowok[:, 0:1], in_=rowok[:, 0:1], pattern=[[0, 1]], compare_op=ALU.is_ge,
                            fill=0.0, base=-(CB - 1), channel_multiplier=1).then_inc(consts, 1)
            pool.wait_ge(bank_free[7], 1)
            for k in range(KT):
                pool.wait_ge(xt_sb, k + 1)
                g.tensor_tensor(xn[:, k, :], xt0[:, k, :], ssf[:, :], ALU.mult).then_inc(xn_done, 1)
            pool.wait_ge(small_pe, 1)
            then(g.memset(cumb[:, :], 0.0))
            then(g.memset(sel[:, :, :], 0.0))
            for q in range(3):
                last = g.affine_select(out=sel[:, :, :], in_=sel[:, :, :], pattern=[[-1, NH], [0, P]],
                                       compare_op=ALU.not_equal, fill=1.0, base=-32 * q, channel_multiplier=1)
                if q < 2:
                    then(last)
            last.then_inc(sel_ready, 1)


_INS = ['x', 'c', 'ada_w', 'ada_b', 'norm1_gain', 'norm2_gain', 'w_in', 'fox_f_bias', 'fox_q_gain', 'fox_k_gain',
        'nsa_q_gain', 'nsa_k_gain', 'nsa_cmp_pos', 'nsa_cmp_w1', 'nsa_cmp_w2', 'rel_bias', 'mix_out_gain', 'w_out',
        'ffn_w_gate', 'ffn_w_up', 'ffn_w_down']


def bucket_onehot():
    d = np.concatenate([S - 1 - np.arange(NREV), np.arange(NFWD) - (S - 1)])
    exact = NBUCKET // 2
    n = np.maximum(d, 1).astype(np.float64)
    large = exact + (np.log(n / exact) / np.log(MAXDIST / exact) * (NBUCKET - exact)).astype(np.int64)
    b = np.where(d < exact, d, np.minimum(large, NBUCKET - 1))
    b = np.where(d < 0, NBUCKET, b)
    return (np.arange(NBUCKET + 1)[:, None] == b[None, :]).astype(np.float32)


def kernel(**inputs):
    import concourse.bacc as bacc
    from concourse.bass_utils import run_bass_kernel_spmd

    nc = bacc.Bacc("TRN2", target_bir_lowering=False, num_devices=1)
    arrays, aps = {}, {}
    given = {name: np.ascontiguousarray(inputs[name]) for name in _INS}
    given["bucket_onehot"] = bucket_onehot()
    for name, a in given.items():
        arrays[f"in_{name}"] = a
        aps[name] = nc.dram_tensor(f"in_{name}", a.shape, mybir.dt.from_np(a.dtype), kind="ExternalInput").ap()
    out = nc.dram_tensor("out_0", (1, S, D), F32, kind="ExternalOutput").ap()
    hybrid_layer(nc, aps, out)
    r = run_bass_kernel_spmd(nc, [arrays], core_ids=[0])
    return r.results[0]["out_0"]
```

```python
from contextlib import ExitStack

import numpy as np

import concourse.bass as bass
from concourse import mybir

F32 = mybir.dt.float32
F32R = mybir.dt.float32r
BF16 = mybir.dt.bfloat16
ALU = mybir.AluOpType
ACT = mybir.ActivationFunctionType
AX = mybir.AxisListType

P = 128
S = 512
ST = S // P
D = 2048
KT = D // P
NH = 8
DFF = 5632
NBUCKET, MAXDIST = 32, 128
CB, CS = 32, 16
NCMP = (S - CB) // CS + 1
SCALE = P ** -0.5
EPS = 1e-6
NEG = -1e30
C_FQ, C_FV, C_FF, C_NQ, C_NK = 0, 2048, 3072, 3080, 4104
C_NV = C_NK + 768
C_NG = C_NV + 768
NSMALL = 32
CK = 2
CW = 512
NSTAGE, NW = 4, 2
GCH = KT // CK
G_OUT, G_FF = 11, 15
NFB = DFF // CW
NREV, NFWD = 640, 992
R_C, R_N1, R_N2, R_MIX, R_FQ, R_FK, R_NQ, R_NK = 0, 16, 32, 48, 64, 65, 66, 67
NPAR = 70
TS = (3, 2, 1, 0)
S_AT = {3: (0, 0), 2: (1, 0), 1: (2, 0), 0: (2, 256)}
T_AT = {0: (3, 0), 1: (4, 0), 3: (4, 384), 2: (5, 0)}
T_SB = {0: 0, 1: 512, 3: 896, 2: 1024}
P_SB = {3: 0, 2: 512, 1: 896, 0: 1152}
ACW = 256
ADA_STEPS = 128


def ada_plan():
    plan = {}
    for groups, first in ((range(2, 6), 0), (range(6, 11), ADA_STEPS // 2)):
        slots = [(g, j) for g in groups for j in range(GCH)]
        if first == 0:
            plan.update({slot: range(0) for slot in slots[:2]})
            slots = slots[2:]
        n = ADA_STEPS // 2
        for i, slot in enumerate(slots):
            plan[slot] = range(first + i * n // len(slots), first + (i + 1) * n // len(slots))
    return plan


def hybrid_layer(nc, A, out):
    with ExitStack() as ctx:
        base = (nc.sbuf_base + 63) // 64 * 64
        RH, RQ = base, base + 65536
        RW = RQ + 57344
        RX = RW + 32768
        RM = RX + 32768

        def at(name, shape, dt, offset):
            return nc.alloc_sbuf_tensor_at(name, shape, dt, offset=offset)

        def sem(name):
            return ctx.enter_context(nc.semaphore(name))

        hhi = at("hhi", [P, KT, S], F32R, RH)
        hlo = at("hlo", [P, KT, S], F32R, RH + 32768)
        xnat = at("xnat", [P, ST, D], F32, RH)
        xn = at("xn", [P, KT, S], F32, RH + 32768)
        sq_first = at("sq_first", [P, D], F32, RH + 32768)
        cmp_bias = at("cmp_bias", [NCMP, NH, S], F32, RH + 49152)
        rel = at("rel", [P, NH, S], F32, RH + 16384)
        rel_rev = at("rel_rev", [P, NH, S], F32, RW)
        w1 = [at(f"w1_{b}", [P, CB, P], F32, RH + 32768 * b) for b in range(2)]
        xt0 = at("xt0", [P, KT, S], F32, RQ + 16384)
        acc_first = at("acc_first", [P, 2, 2 * ACW], F32, RQ + 8192)
        partial = at("partial", [P, S], F32, RQ + 12288)
        wsmall_hi = at("wsmall_hi", [P, KT, NSMALL], F32R, RQ + 49152)
        wsmall_lo = at("wsmall_lo", [P, KT, NSMALL], F32R, RQ + 51200)
        wsmall = at("wsmall", [P, KT, NSMALL], F32, RQ + 53248)
        fl = at("fl", [NSMALL, S], F32, RQ + 53248)
        fl2 = at("fl2", [NSMALL, S], F32, RQ + 55296)
        fq = at("fq", [P, NH, S], F32, RQ)
        fk = at("fk", [P, NH, S], F32, RQ + 16384)
        fv = at("fv", [P, ST, 2 * CW], F32, RQ + 32768)
        nq = at("nq", [P, NH, S], F32, RQ + 16384)
        nk = at("nk", [P, NH, S], F32, RQ + 32768)
        nv = at("nv", [P, ST, CW], F32, RQ + 49152)
        silu_g = at("silu_g", [P, 4, S], F32, RQ)
        ghi = at("ghi", [P, 4, S], F32R, RQ + 8192)
        glo = at("glo", [P, 4, S], F32R, RQ + 16384)
        gfull = at("gfull", [P, 4, S], F32, RQ + 24576)
        ostage = at("ostage", [P, 2, ST, CW], F32, RQ + 32768)
        stage = at("stage", [P, NSTAGE, CK, CW], F32, RW)
        whi = at("whi", [P, NW, CK, CW], F32R, RW + 16384)
        wlo = at("wlo", [P, NW, CK, CW], F32R, RW + 24576)
        ada_first = [at(f"ada_first{b}", [P, 4, 2, ACW], F32, offset)
                     for b, offset in enumerate((RX, RX + 8192, RX + 16384, RQ))]
        h1t = at("h1t", [P, 4, S], F32, RX + 24576)
        sq = at("sq", [P, 4, S], F32, RX)
        rb = at("rb", [P, 4, S], F32, RX + 8192)
        sq_hi = at("sq_hi", [P, 4, S], F32R, RX + 8192)
        sq_lo = at("sq_lo", [P, 4, S], F32R, RX)
        ada_ring = at("ada_ring", [P, 3, D // 2], F32, RX + 16384)
        prob = [at(f"prob{b}", [P, 1280], F32, offset) for b, offset in enumerate((RX + 16384, RX + 4096))]
        probT = [at(f"probT{b}", [P, 1280], F32, offset) for b, offset in enumerate((RX + 21504, RX + 9216))]
        probc = at("probc", [P, ST, NCMP + 1], F32, RX + 26624)
        probcT = at("probcT", [NCMP, S], F32, RX + 27136)
        o_sq = at("o_sq", [P, S], F32, RX)
        ssn = at("ssn", [P, S], F32, RX + 2048)
        fa = at("fa", [NH, S], F32, RX + 28672)
        fb = at("fb", [NH, S], F32, RX + 30720)
        sel = at("sel", [72, NH, P], BF16, RQ + 49152)
        cumb = at("cumb", [72, S], BF16, RQ + 51200)
        cumt = at("cumt", [NH, S], BF16, RQ + 52224)
        unfold = at("unfold", [P, 2, CB, 2 * NCMP], F32, RX)
        xT = at("xT", [P, KT, S], F32, RX)
        acc = at("acc", [P, 2, D], F32, RM)
        m = RM + 16384

        def small(name, shape, dt=F32):
            nonlocal m
            size = 2 if dt == BF16 else 4
            for n in shape[1:]:
                size *= n
            t = at(name, shape, dt, m)
            m += (size + 31) // 32 * 32
            return t

        par = small("par", [P, NPAR])
        adab = small("adab", [P, 96])
        mod = small("mod", [P, 6, KT])
        fbias = small("fbias", [NH, 1])
        cpos = small("cpos", [P, 2 * CB])
        silu_c = small("silu_c", [P, KT])
        t16 = small("t16", [P, KT])
        ident = small("ident", [P, P])
        flip = small("flip", [P, P])
        flipc = small("flipc", [NCMP, NCMP])
        ones_r = small("ones_r", [P, P], F32R)
        ones = ones_r[:, :].bitcast(F32)
        identb = small("identb", [P, P], BF16)
        maskb = small("maskb", [P, P], BF16)
        eps = small("eps", [P, 1])
        ssx = small("ssx", [P, ST])
        rx = small("rx", [P, ST])
        nmax = small("nmax", [P, ST])
        psum_row = small("psum_row", [P, ST])
        rinv = small("rinv", [P, ST])
        cmax = small("cmax", [P, ST])
        csum = small("csum", [P, ST])
        gate = small("gate", [P, ST, NSMALL])
        rowok = small("rowok", [P, ST])
        kc = small("kc", [P, 2, NCMP + 1])
        vc = small("vc", [NCMP, 2, P])
        ssf = small("ssf", [P, S])
        assert m <= nc.sbuf_usable_end, m - nc.sbuf_usable_end
        parn = at("parn", [NPAR, P], F32, RM)
        adabn = at("adabn", [96, P], F32, RM + 512)
        cposn = at("cposn", [2 * CB, P], F32, RM + 1024)
        relb = at("relb", [NBUCKET + 1, NH], F32, RM + 1536)
        onehot = at("onehot", [NBUCKET + 1, NREV + NFWD], F32, RM + 2048)
        line = at("line", [NH, NREV + NFWD], F32, RM + 2048 + 6656)
        diag = at("diag", [P, ST, P], F32, RX + 24576)
        w2 = at("w2", [P, 2, P], F32, RX + 29184)
        hid = at("hid", [P, 2, 2 * NCMP], F32, RX + 30208)
        hid2 = at("hid2", [P, 2, 2 * NCMP], F32, RX + 30720)

        PS = ctx.enter_context(nc.psum_tensor("PS", [P, 8, S], F32))
        xT_d = nc.dram_tensor("xT_d", [P, KT * S], F32, kind="Internal").ap()
        line_d = nc.dram_tensor("line_d", [NH, NREV + NFWD], F32, kind="Internal").ap()

        consts = sem("consts")
        par_in, lines_in, small_in = sem("par_in"), sem("lines_in"), sem("small_in")
        x_in = [sem(f"x_in{t}") for t in range(ST)]
        first_in = [sem(f"ada_first_in{b}") for b in range(4)]
        par_t, par_done, act_s, dve_s = sem("par_t"), sem("par_done"), sem("act_self"), sem("dve_self")
        exp_c = sem("exp_c")
        first_acc = sem("first_acc")
        line_pe, line_sb, line_out = sem("line_pe"), sem("line_sb"), sem("line_out")
        xt_pe, xt_sb, xt_out = sem("xt_pe"), sem("xt_sb"), sem("xt_out")
        rx_done, diag_done, rb_pe, xn_done = sem("rx_done"), sem("diag_done"), sem("rb_pe"), sem("xn_done")
        mod_pe, mod_ready, part_out, small_out = sem("mod_pe"), sem("mod_ready"), sem("part_out"), sem("small_out")
        h_full, h_hi, h_lo = sem("h_full"), sem("h_hi"), sem("h_lo")
        ws_hi, ws_lo, small_pe = sem("ws_hi"), sem("ws_lo"), sem("small_pe")
        gates_e, z_done, fexp, forget_ready, gates_ready, gates_pe, gates_nat = (sem(n) for n in (
            "gates_exp", "z_done", "forget_exp", "forget_ready", "gates_ready", "gates_pe", "gates_nat"))
        stage_in = [sem(f"stage_in{b}") for b in range(NSTAGE)]
        split_in = [sem(f"split_in{b}") for b in range(NSTAGE)]
        w_hi, w_lo, w_used = sem("w_hi"), sem("w_lo"), sem("w_used")
        tile_done = sem("tile_done")
        bank_free = [sem(f"bank_free{b}") for b in range(8)]
        evac, sq_done, sq_split, ss_pe, r_done, norm_done = (sem(n) for n in (
            "evac", "sq_done", "sq_split", "ss_pe", "r_done", "norm_done"))
        ada_in = [sem(f"ada_in{b}") for b in range(3)]
        ada_acc = sem("ada_acc")
        sel_ready = sem("sel_ready")
        s_pe, s_max, s_exp, p_done, t_pe, t_act, t_dve, o_pe, o_sb, ss_acc = (sem(n) for n in (
            "scores_pe", "scores_max", "scores_exp", "probs_done", "transposed_pe", "transposed_act",
            "transposed_dve", "out_pe", "out_sb", "squares_summed"))
        w1_in, w2_in = [sem(f"w1_in{i}") for i in range(8)], sem("w2_in")
        rel_in = [sem(f"rel_in{h}") for h in range(NH)]
        unf, hid_pe, hid_exp, hid_done, kcv_pe, kc_copied, kc_sq, kc_ss, kc_r, kc_ready, vc_ready = (
            sem(n) for n in ("unfolded", "hid_pe", "hid_exp", "hid_done", "kcv_pe",
                             "kc_copied", "kc_squared", "kc_ss", "kc_r", "kc_ready", "vc_ready"))
        sc_pe, sc_sub, sc_exp, pc_done, pct_pe, pct_sb = (sem(n) for n in (
            "cmp_scores", "cmp_shifted", "cmp_exp", "cmp_probs", "cmp_transposed", "cmp_transposed_sb"))
        pv_done, ry_ln, rh_ln, kc_ln = (sem(n) for n in ("pv_done", "ry_ln", "rh_ln", "kc_ln"))
        flip_pe, flip_sb, cmpb_in = sem("flip_pe"), sem("flip_sb"), sem("cmpb_in")
        mod2_pe, mod2_done = sem("mod2_pe"), sem("mod2_done")
        y_full, y_hi, y_lo = sem("y_full"), sem("y_hi"), sem("y_lo")
        ssy_pe, ry_done = sem("ssy_pe"), sem("ry_done")
        xT_in = [sem(f"xT_in{i}") for i in range(4)]
        x1_sq, x1_acc = sem("x1_sq"), sem("x1_acc")
        ssh_pe, rh_done, h2_t, h2_hi, h2_lo = sem("ssh_pe"), sem("rh_done"), sem("h2_t"), sem("h2_hi"), sem("h2_lo")
        g_hi, g_lo, pool_s = sem("g_hi"), sem("g_lo"), sem("pool_self")
        fin_pe, fin_sb, fin_last = sem("fin_pe"), sem("fin_sb"), sem("fin_last")
        out_sent = [sem(f"out_sent{b}") for b in range(2)]

        plan = ada_plan()
        w_in, w_o = A["w_in"][0], A["w_out"][0]
        w_in_t = w_in.rearrange("(k p) n -> p k n", p=P)
        ada_t = A["ada_w"][0].rearrange("(k p) n -> k p n", p=P)

        def group_cols(g):
            if g < 4:
                return [(C_FQ + CW * g, CW)]
            if g < 6:
                return [(C_FV + CW * (g - 4), CW)]
            if g < 8:
                return [(C_NQ + CW * (g - 6), CW)]
            if g == 8:
                return [(C_NK + 256, CW)]
            if g == 9:
                return [(C_NK, 256), (C_NV, 256)]
            return [(C_NV + 256, CW)]

        NATURAL = (4, 5, 10)
        NORMED = (0, 1, 2, 3, 6, 7, 8)

        def tile_of(g, t):
            if g < 2:
                return fq[:, 4 * g + t, :]
            if g < 4:
                return fk[:, 4 * (g - 2) + t, :]
            if g < 6:
                return fv[:, t, CW * (g - 4):CW * (g - 3)]
            if g < 8:
                return nq[:, 4 * (g - 6) + t, :]
            if g == 8:
                return nk[:, t, :]
            if g == 9:
                return nk[:, 4 + t, :]
            return nv[:, t, :]

        def gain_of(g, t):
            r = R_FQ if g < 2 else R_FK if g < 4 else R_NQ if g < 8 else R_NK + 1 + t // 2
            return par[:, r:r + 1]

        def bank(g, t):
            return 4 * (g % 2) + t

        def uses(g):
            return 1 + g // 2

        def normed_before(g):
            return 4 * sum(x < g for x in NORMED)

        def parts(t):
            return P_SB[t], P * (t + 1)

        UF = NH

        def await_tile(eng, g, t):
            if t < 3:
                eng.wait_ge(tile_done, 3 * g + t + 1)
            else:
                eng.wait_ge(w_used, GCH * (g + 1) if g else 2 * GCH - 1)

        def await_ff(eng, t, tiles, chunks):
            if t < 3:
                eng.wait_ge(tile_done, tiles + t + 1)
            else:
                eng.wait_ge(w_used, chunks)

        x1_sqt = at("x1_sqt", [P, 4, S], F32, RQ + 32768)
        h2t = at("h2t", [P, 4, S], F32, RQ + 40960)

        block = ctx.enter_context(nc.Block())

        @block.sync
        def _(sp):
            for t in range(ST):
                sp.dma_start(xnat[:, t, :], A["x"][0, P * t:P * (t + 1), :]).then_inc(x_in[t], 16)
            rows = [("c", R_C, 16), ("norm1_gain", R_N1, 16), ("norm2_gain", R_N2, 16), ("mix_out_gain", R_MIX, 16),
                    ("fox_q_gain", R_FQ, 1), ("fox_k_gain", R_FK, 1), ("nsa_q_gain", R_NQ, 1)]
            for name, r, n in rows:
                sp.dma_start(parn[r:r + n, :], A[name].rearrange("a (r d) -> (a r) d", d=P)).then_inc(par_in, 16)
            sp.dma_start(parn[R_NK:R_NK + 3, :], A["nsa_k_gain"][0]).then_inc(par_in, 16)
            sp.dma_start(adabn[:, :], A["ada_b"].rearrange("a (r d) -> (a r) d", d=P)).then_inc(par_in, 16)
            sp.dma_start(cposn[:, :], A["nsa_cmp_pos"][0].rearrange("a b d -> (a b) d")).then_inc(par_in, 16)
            sp.dma_start(fbias[:, :], A["fox_f_bias"].rearrange("a h -> h a")).then_inc(par_in, 16)

            sp.dma_start(relb[0:NBUCKET, :], A["rel_bias"]).then_inc(lines_in, 16)
            sp.dma_start(onehot[:, :], A["bucket_onehot"]).then_inc(lines_in, 16)

            def free_stage(c):
                if c >= NSTAGE:
                    sp.wait_ge(w_lo, c - NSTAGE + 1)

            ada_p = A["ada_w"][0].rearrange("(k p) n -> p k n", p=P)
            for j in range(GCH):
                for s in range(4):
                    if j >= 1:
                        sp.wait_ge(first_acc, KT * (j - 1) + 4 * (s + 1))
                    for comp in range(2):
                        c0 = D * comp + ACW * j
                        sp.dma_start(ada_first[s][:, :, comp, :], ada_p[:, 4 * s:4 * s + 4, c0:c0 + ACW]
                                     ).then_inc(first_in[s], 16)
                    if s == 1:
                        for g in range(2):
                            c = 2 * j + g
                            free_stage(c)
                            c0 = group_cols(g)[0][0]
                            sp.dma_start(stage[:, c % NSTAGE, :, :],
                                         w_in_t[:, CK * j:CK * j + CK, c0:c0 + CW]).then_inc(stage_in[c % NSTAGE], 16)
                if j == 2:
                    sp.wait_ge(line_sb, 4)
                    sp.dma_start(line_d, line[:, :]).then_inc(line_out, 16)

            def ada(a):
                if a >= 3:
                    sp.wait_ge(ada_acc, a - 2)
                comp, k, half = 2 + a // 32, a % 32 // 2, a % 2
                c0 = D * comp + 1024 * half
                sp.dma_start(ada_ring[:, a % 3, :], ada_t[k, :, c0:c0 + 1024]).then_inc(ada_in[a % 3], 16)

            def project_in(g):
                for j in range(GCH):
                    c = GCH * g + j
                    free_stage(c)
                    if g == 6 and j == NSTAGE:
                        sp.wait_ge(pv_done, UF)
                        for a in range(plan[g, 0][0], plan[g, NSTAGE][0]):
                            ada(a)
                    pieces = group_cols(g)
                    if len(pieces) == 2:
                        for (c0, n), n0, landed in zip(pieces, (0, 256), (split_in, stage_in)):
                            sp.dma_start(stage[:, c % NSTAGE, :, n0:n0 + n],
                                         w_in_t[:, CK * j:CK * j + CK, c0:c0 + n]).then_inc(landed[c % NSTAGE], 16)
                    else:
                        c0, n = pieces[0]
                        sp.dma_start(stage[:, c % NSTAGE, :, :],
                                     w_in_t[:, CK * j:CK * j + CK, c0:c0 + n]).then_inc(stage_in[c % NSTAGE], 16)
                    if g == 2 and j == 3:
                        sp.dma_start(wsmall[:, :, 0:8], w_in_t[:, :, C_FF:C_FF + 8]).then_inc(small_in, 16)
                        sp.dma_start(wsmall[:, :, 8:32], w_in_t[:, :, C_NG:C_NG + 24]).then_inc(small_in, 16)
                    if g == 2 and j == 1:
                        sp.dma_start(xT_d, xt0[:, :, :].rearrange("p k s -> p (k s)")).then_inc(xt_out, 16)
                        sp.wait_ge(h_lo, KT)
                        sp.wait_ge(line_out, 16)
                    if g != 6 or j >= NSTAGE:
                        for a in plan[g, j]:
                            ada(a)

            for g in range(2, 11):
                project_in(g)

            sp.wait_ge(line_out, 16)
            sp.wait_ge(w_lo, 11 * GCH)
            for h in range(NH):
                at_h = h * (NREV + NFWD)
                sp.dma_start(rel_rev[:, h, :], bass.AP(tensor=line_d.tensor, offset=at_h,
                                                       ap=[[1, P], [1, S]])).then_inc(rel_in[h], 16)
            sp.wait_ge(w_used, 11 * GCH)
            sp.dma_start(w2[:, :, :], A["nsa_cmp_w2"][0].rearrange("b d n -> d b n")).then_inc(w2_in, 16)
            for i in range(8):
                b, js = i // 4, slice(8 * (i % 4), 8 * (i % 4) + 8)
                sp.dma_start(w1[b][:, js, :], A["nsa_cmp_w1"][0, b].rearrange("(j d) n -> d j n", d=P)[:, js, :]
                             ).then_inc(w1_in[i], 16)
            for h in range(NH):
                at_h = h * (NREV + NFWD) + NREV + S - 1 - (CB - 1) - CS * (NCMP - 1)
                sp.dma_start(cmp_bias[:, h, :], bass.AP(tensor=line_d.tensor, offset=at_h,
                                                        ap=[[CS, NCMP], [1, S]])).then_inc(cmpb_in, 16)

            sp.wait_ge(flip_pe, NH)
            w_o_t = w_o.rearrange("(k p) n -> p k n", p=P)
            for g in range(G_OUT, G_FF):
                for j in range(GCH):
                    c = GCH * g + j
                    free_stage(c)
                    c0 = CW * (g - G_OUT)
                    sp.dma_start(stage[:, c % NSTAGE, :, :],
                                 w_o_t[:, CK * j:CK * j + CK, c0:c0 + CW]).then_inc(stage_in[c % NSTAGE], 16)
                    if g == G_OUT and j == GCH - 1 or g == G_OUT + 1 and j < 3:
                        i = (j + 1) % GCH
                        sp.wait_ge(y_full, KT)
                        sp.dma_start(xT[:, 4 * i:4 * i + 4, :].rearrange("p k s -> p (k s)"),
                                     xT_d[:, 4 * i * S:4 * (i + 1) * S]).then_inc(xT_in[i], 16)

            gate_w = A["ffn_w_gate"][0].rearrange("(k p) n -> p k n", p=P)
            up_w = A["ffn_w_up"][0].rearrange("(k p) n -> p k n", p=P)
            down_w = A["ffn_w_down"][0].rearrange("(k p) n -> p k n", p=P)

            def columns(w, i, c):
                for j in range(GCH):
                    sp.wait_ge(w_lo, c + j - NSTAGE + 1)
                    sp.dma_start(stage[:, j % NSTAGE, :, :],
                                 w[:, CK * j:CK * j + CK, bass.ds(CW * i, CW)]).then_inc(stage_in[j % NSTAGE], 16)

            def rows_of_down(i, c):
                for j in range(GCH):
                    sp.wait_ge(w_lo, c + j - NSTAGE + 1)
                    c0 = CW * (j // 2)
                    sp.dma_start(stage[:, j % NSTAGE, :, :],
                                 down_w[:, bass.ds(4 * i + CK * (j % 2), CK), c0:c0 + CW]
                                 ).then_inc(stage_in[j % NSTAGE], 16)

            c = GCH * G_FF
            columns(gate_w, 0, c)
            with sp.Fori(0, NFB - 1) as i:
                at_i = c + GCH + 3 * GCH * i
                columns(up_w, i, at_i)
                columns(gate_w, i + 1, at_i + GCH)
                rows_of_down(i, at_i + 2 * GCH)
            last = c + GCH + 3 * GCH * (NFB - 1)
            columns(up_w, NFB - 1, last)
            rows_of_down(NFB - 1, last + GCH)

            out_t = out[0].rearrange("(t p) n -> p t n", p=P)
            for dg in range(4):
                for t in range(ST):
                    if dg < 3:
                        sp.wait_ge(fin_sb, 4 * dg + t + 1)
                    elif t % 2 == 0:
                        sp.wait_ge(fin_sb, 12 + t // 2 + 1)
                    else:
                        sp.wait_ge(fin_last, t // 2 + 1)
                    sp.dma_start(out_t[:, t, CW * dg:CW * (dg + 1)], ostage[:, dg % 2, t, :]
                                 ).then_inc(out_sent[dg % 2], 16)
            for b in range(2):
                sp.wait_ge(out_sent[b], 2 * 16 * ST)

        @block.tensor
        def _(pe):
            mm, tr = nc.tensor.matmul, nc.tensor.transpose

            pe.wait_ge(consts, 1)
            pe.wait_ge(par_in, 11 * 16)
            tr(PS[:, 0, 0:NPAR], parn[:, :], ident[0:NPAR, 0:NPAR]).then_inc(par_t, 1)
            tr(PS[:, 1, 0:96], adabn[:, :], ident[0:96, 0:96]).then_inc(par_t, 1)
            tr(PS[:, 2, 0:2 * CB], cposn[:, :], ident[0:2 * CB, 0:2 * CB]).then_inc(par_t, 1)
            for t in range(ST):
                pe.wait_ge(x_in[t], 16)
            for k in range(KT):
                if k == 0:
                    pe.wait_ge(par_done, 3)
                if k >= 8:
                    pe.wait_ge(xt_sb, k - 7)
                for t in range(ST):
                    last = tr(PS[:, k % 8, P * t:P * (t + 1)], xnat[:, t, P * k:P * (k + 1)], ident[:, :])
                last.then_inc(xt_pe, 1)
            pe.wait_ge(lines_in, 32)
            n = (NREV + NFWD) // 4
            for b in range(4):
                pe.wait_ge(xt_sb, 8 + b + 1)
                mm(PS[0:NH, b, 0:n], relb[:, :], onehot[:, n * b:n * (b + 1)], start=True, stop=True).then_inc(line_pe, 1)
            pe.wait_ge(diag_done, ST)
            pe.wait_ge(xt_sb, KT)
            for t in range(ST):
                last = mm(PS[:, 7, P * t:P * (t + 1)], ones[:, :], diag[:, t, :], start=True, stop=True)
            last.then_inc(rb_pe, 1)

            def columns_tile(b, slot, kk, t, k, start, stop, rhi=None, rlo=None):
                cols = slice(P * t, P * (t + 1))
                rhi = hhi[:, k, :] if rhi is None else rhi
                rlo = hlo[:, k, :] if rlo is None else rlo
                mm(PS[:, b, :], whi[:, slot, kk, cols], rhi, start=start, stop=False)
                mm(PS[:, b, :], whi[:, slot, kk, cols], rlo, start=False, stop=False)
                return mm(PS[:, b, :], wlo[:, slot, kk, cols], rhi, start=False, stop=stop)

            def tokens_tile(b, slot, kk, t, k, start, stop):
                rows = slice(P * t, P * (t + 1))
                mm(PS[:, b, :], hhi[:, k, rows], whi[:, slot, kk, :], start=start, stop=False)
                mm(PS[:, b, :], hhi[:, k, rows], wlo[:, slot, kk, :], start=False, stop=False)
                return mm(PS[:, b, :], hlo[:, k, rows], whi[:, slot, kk, :], start=False, stop=stop)

            def first_groups():
                def shift_and_scale(j):
                    pe.wait_ge(first_acc, KT * (j + 1))
                    if j == 0:
                        pe.wait_ge(bank_free[7], 1)
                    if j >= 2:
                        pe.wait_ge(part_out, j - 1)
                    for n in range(2 * CK):
                        for half in range(2):
                            last = mm(PS[:, 7, n:n + 1], acc_first[:, half, P * n:P * (n + 1)], ones[:, 0:1],
                                      start=half == 0, stop=half == 1)
                    last.then_inc(mod_pe, 1)

                shift_and_scale(0)
                for j in range(GCH):
                    for g in range(2):
                        pe.wait_ge(w_lo, 2 * j + g + 1)
                        for t in range(4):
                            b = 4 * g + t
                            if j == 0 and b < 7:
                                pe.wait_ge(bank_free[b], 1)
                            if b == 7:
                                pe.wait_ge(mod_ready, min(j + 2, GCH))
                            alone = b == 7 and j < GCH - 1
                            if b == 7 and j == GCH - 1:
                                pe.wait_ge(part_out, GCH - 1)
                                mm(PS[:, 7, :], ident[:, :], partial[:, :], start=True, stop=False)
                            for kk in range(CK):
                                k = CK * j + kk
                                if b == 0:
                                    pe.wait_ge(h_lo, k + 1)
                                start = b != 7 and k == 0 or alone and kk == 0
                                last = columns_tile(b, g, kk, t, k, start, (kk == CK - 1) if alone else k == KT - 1)
                            if j == GCH - 1 and t < 3:
                                last.then_inc(tile_done, 1)
                        last.then_inc(w_used, 1)
                        if g == 0 and j < GCH - 1:
                            shift_and_scale(j + 1)

            def small_columns():
                pe.wait_ge(ws_lo, 1)
                pe.wait_ge(bank_free[7], uses(3))
                for k in range(KT):
                    mm(PS[0:NSMALL, 7, :], wsmall_hi[:, k, :], hhi[:, k, :], start=(k == 0), stop=False)
                    mm(PS[0:NSMALL, 7, :], wsmall_hi[:, k, :], hlo[:, k, :], start=False, stop=False)
                    last = mm(PS[0:NSMALL, 7, :], wsmall_lo[:, k, :], hhi[:, k, :], start=False, stop=(k == KT - 1))
                last.then_inc(small_pe, 1)

            def gemm(c, first_bank, free, tile, chunks=GCH, mid=None, mid_at=3, before=None, guard=None):
                for j in range(chunks):
                    pe.wait_ge(w_lo, c + j + 1)
                    for t in range(4):
                        if j == 0:
                            pe.wait_ge(bank_free[first_bank + t], free)
                            if t == 3 and guard is not None:
                                guard()
                        for kk in range(CK):
                            k = CK * j + kk
                            if before is not None and t == 0:
                                before(k)
                            last = tile(first_bank + t, j % NW, kk, t, k, k == 0, k == CK * chunks - 1)
                        if j == chunks - 1 and t < 3:
                            last.then_inc(tile_done, 1)
                    last.then_inc(w_used, 1)
                    if mid is not None and j == mid_at:
                        mid()

            def squares(g):
                for t in range(4):
                    n = normed_before(g) + t + 1
                    pe.wait_ge(sq_split, n)
                    mm(PS[:, bank(g, t), :], ones_r[:, :], sq_hi[:, t, :], start=True, stop=False)
                    mm(PS[:, bank(g, t), :], ones_r[:, :], sq_lo[:, t, :], start=False, stop=True).then_inc(ss_pe, 1)

            def project_in(g):
                mid = (lambda: squares(g - 1)) if g - 1 in NORMED and g != 6 else None
                gemm(GCH * g, bank(g, 0), uses(g), tokens_tile if g in NATURAL else columns_tile, mid=mid, mid_at=4,
                     guard=(lambda: pe.wait_ge(small_out, 1)) if g == 3 else None)

            def scores(u, q_of, k_of, bias=None):
                for i, t in enumerate(TS):
                    if u not in (0, UF):
                        pe.wait_ge(s_exp if u < UF else s_max, 4 * (u - 1) + (i + 1 if i < 2 else 4))
                    b, c0 = S_AT[t]
                    n = P * (t + 1)
                    o = PS[:, b, c0:c0 + n]
                    last = mm(o, q_of(t), k_of(n), start=True, stop=bias is None)
                    if bias is not None:
                        last = bias(o, t, n)
                    last.then_inc(s_pe, 1)

            def transposes(u):
                if u >= 1:
                    pe.wait_ge(t_act, 2 * u)
                    pe.wait_ge(t_dve, u)
                for i, t in enumerate(TS):
                    pe.wait_ge(p_done, 4 * u + i + 1)
                    for kb in range(t + 1):
                        b, c0 = T_AT[kb]
                        c0 += P * (t - kb)
                        c1 = parts(t)[0] + P * kb
                        last = tr(PS[:, b, c0:c0 + P], prob[u % 2][:, c1:c1 + P], ident[:, :])
                    last.then_inc(t_pe, 1)

            def values(u, v_of, start, stop):
                pe.wait_ge(t_act, 2 * (u + 1))
                pe.wait_ge(t_dve, u + 1)
                for kb in range(4):
                    n = S - P * kb
                    last = mm(PS[:, 6, P * kb:S], v_of(kb), probT[u % 2][:, T_SB[kb]:T_SB[kb] + n],
                              start=start and kb == 0, stop=stop and kb == 3)
                return last

            first_groups()
            squares(0)
            for g in range(2, 6):
                project_in(g)
                if g == 2:
                    small_columns()

            pe.wait_ge(sel_ready, 1)
            pe.wait_ge(forget_ready, 3)
            pe.wait_ge(gates_ready, 1)
            for b in range(8):
                pe.wait_ge(bank_free[b], uses(6 + b // 4))
            pe.wait_ge(norm_done, 16)
            for t in range(ST):
                last = tr(PS[:, 7, NSMALL * t:NSMALL * (t + 1)], fl2[:, P * t:P * (t + 1)],
                          ident[0:NSMALL, 0:NSMALL])
            last.then_inc(gates_pe, 1)

            def fox_scores(h):
                def bias(o, t, n):
                    mm(o, sel[:, h, :], cumb[:, 0:n], start=False, stop=False)
                    return mm(o[:, n - P:n], identb[:, :], maskb[:, :], start=False, stop=True)

                scores(h, lambda t: fq[:, h, P * t:P * (t + 1)], lambda n: fk[:, h, 0:n], bias)

            fox_scores(0)
            for h in range(NH + 1):
                if h + 1 < NH:
                    fox_scores(h + 1)
                if h >= 2:
                    pe.wait_ge(o_sb, h - 1)
                if h >= 1:
                    values(h - 1, lambda kb, h=h - 1: fv[:, kb, P * h:P * (h + 1)], True, True).then_inc(pv_done, 1)
                if h < NH:
                    transposes(h)
                    pe.wait_ge(gates_nat, 1)
                    pe.wait_ge(ada_acc, ADA_STEPS // 2)
                    for n in range(4 * h, 4 * h + 4):
                        last = mm(PS[:, 7, 128 + n:129 + n], acc[:, n // KT, P * (n % KT):P * (n % KT + 1)],
                                  ones[:, 0:1], start=True, stop=True)
                    if h == NH - 1:
                        last.then_inc(mod2_pe, 1)

            def fox_mean():
                pe.wait_ge(ss_acc, NH)
                pe.wait_ge(gates_nat, 1)
                pe.wait_ge(mod2_done, 1)
                mm(PS[:, 7, :], ones[:, :], ssf[:, :], start=True, stop=True).then_inc(ssy_pe, 1)

            gemm(GCH * 6, 0, uses(6), columns_tile, mid=fox_mean)
            pe.wait_ge(o_sb, NH)
            pe.wait_ge(ry_done, 1)
            for g in range(7, 11):
                project_in(g)

            for b in range(8):
                pe.wait_ge(bank_free[b], uses(12 - b // 4))
            for h in range(NH):
                pe.wait_ge(rel_in[h], 16)
                if h >= 3:
                    pe.wait_ge(flip_sb, h - 2)
                mm(PS[:, 4 + h % 3, :], flip[:, :], rel_rev[:, h, :], start=True, stop=True).then_inc(flip_pe, 1)
            def nsa_scores(h, win):
                kv = h // 4
                scores(UF + 2 * h + win, lambda t: nq[:, h, P * t:P * (t + 1)],
                       lambda n: nk[:, 2 * win + kv, 0:n])

            def cmp_scores(h):
                if h == 0:
                    pe.wait_ge(kc_ready, 1)
                    pe.wait_ge(cmpb_in, 16 * NH)
                    pe.wait_ge(ada_acc, ADA_STEPS)
                else:
                    pe.wait_ge(pct_sb, h)
                for n in range(4 * h, 4 * h + 4):
                    mm(PS[:, 7, 128 + n:129 + n], acc[:, n // KT, P * (n % KT):P * (n % KT + 1)],
                       ones[:, 0:1], start=True, stop=True)
                for t in range(ST):
                    o = PS[:, 7, NSMALL * t:NSMALL * t + NCMP]
                    mm(o, nq[:, h, P * t:P * (t + 1)], kc[:, h // 4, 0:NCMP], start=True, stop=False)
                    last = mm(o, cmp_bias[:, h, P * t:P * (t + 1)], flipc[:, :], start=False, stop=True)
                last.then_inc(sc_pe, 1)

            pe.wait_ge(norm_done, 28)
            nsa_scores(0, 0)
            pe.wait_ge(unf, 4)
            for b in range(2):
                for j in range(CB):
                    if j % 8 == 0:
                        pe.wait_ge(w1_in[4 * b + j // 8], 16)
                    last = mm(PS[:, 7, 64 * b:64 * b + 2 * NCMP], w1[b][:, j, :], unfold[:, b, j, :],
                              start=(j == 0), stop=(j == CB - 1))
            last.then_inc(hid_pe, 1)
            nsa_scores(0, 1)
            pe.wait_ge(hid_done, 2)
            pe.wait_ge(w2_in, 16)
            pe.wait_ge(flip_sb, NH)
            mm(PS[:, 6, 0:2 * NCMP], w2[:, 0, :], hid[:, 0, :], start=True, stop=True)
            for kv in range(2):
                last = mm(PS[0:NCMP, 6, 256 + P * kv:256 + P * (kv + 1)], hid[:, 1, NCMP * kv:NCMP * (kv + 1)],
                          w2[:, 1, :], start=True, stop=True)
            last.then_inc(kcv_pe, 1)

            def cmp_key_squares():
                pe.wait_ge(kc_sq, 1)
                pe.wait_ge(vc_ready, 1)
                mm(PS[:, 6, 64:64 + 2 * NCMP], ones[:, :], hid2[:, 0, :], start=True, stop=True).then_inc(kc_ss, 1)

            for step in range(2 * NH + 1):
                if 1 <= step < 2 * NH - 1:
                    nsa_scores((step + 1) // 2, (step + 1) % 2)
                if step == 0:
                    cmp_key_squares()
                if step >= 1:
                    h, win = divmod(step - 1, 2)
                    kv = h // 4
                    if win == 0 and h >= 1:
                        pe.wait_ge(o_sb, UF + h)
                    values(UF + step - 1, lambda kb, c0=2 * P * win + P * kv: nv[:, kb, c0:c0 + P],
                           win == 0, False).then_inc(pv_done, 1)
                    if win == 1:
                        pe.wait_ge(pct_sb, h + 1)
                        mm(PS[:, 6, :], vc[:, kv, :], probcT[:, :], start=False, stop=True).then_inc(o_pe, 1)
                if step < 2 * NH:
                    h, win = divmod(step, 2)
                    transposes(UF + step)
                    if win == 0:
                        cmp_scores(h)
                    else:
                        pe.wait_ge(pc_done, h + 1)
                        for t in range(ST):
                            last = tr(PS[0:NCMP, 7, P * t:P * (t + 1)], probc[:, t, 0:NCMP], ident[:, :])
                        last.then_inc(pct_pe, 1)

            def nsa_mean():
                pe.wait_ge(ss_acc, 2 * NH)
                mm(PS[:, 0, :], ones[:, :], ssn[:, :], start=True, stop=True).then_inc(ssy_pe, 1)

            pe.wait_ge(o_sb, 2 * NH)
            for g in range(G_OUT, G_FF):
                if g == G_OUT + 1:
                    pe.wait_ge(ry_done, 2)
                gemm(GCH * g, bank(g, 0), uses(g), columns_tile,
                     before=(lambda k: pe.wait_ge(y_lo, k + 1)) if g == G_OUT else None,
                     mid=nsa_mean if g == G_OUT else None, mid_at=0)
            pe.wait_ge(x1_acc, KT - 4)
            pe.wait_ge(bank_free[0], uses(16))
            mm(PS[:, 0, :], ones[:, :], ssf[:, :], start=True, stop=False)
            for t in range(4):
                pe.wait_ge(x1_sq, KT - 4 + t + 1)
                last = mm(PS[:, 0, :], ones[:, :], x1_sqt[:, t, :], start=False, stop=t == 3)
            last.then_inc(ssh_pe, 1)
            pe.wait_ge(rh_done, 1)

            def down_tile(half):
                def tile(b, slot, kk, t, k, start, stop):
                    f = CK * half + kk
                    return columns_tile(b, slot, kk, t, k, half == 0 and kk == 0, half == 1 and kk == 1,
                                        ghi[:, f, :], glo[:, f, :])
                return tile

            def down_group(c, dg, first, used, lots=None, mid=None):
                for half in range(2):
                    j = 2 * dg + half
                    pe.wait_ge(w_lo, c + j + 1)
                    for t in range(4):
                        if half == 0:
                            pe.wait_ge(bank_free[first + t], used)
                        for kk in range(CK):
                            if lots is not None and t == 0:
                                pe.wait_ge(g_lo, lots + CK * half + kk + 1)
                            last = down_tile(half)(first + t, j % NW, kk, t, 0, None, None)
                        if half == 1 and t < 3:
                            last.then_inc(tile_done, 1)
                    last.then_inc(w_used, 1)
                    if half == 0 and mid is not None:
                        mid()

            c = GCH * G_FF
            gemm(c, 4, uses(15), columns_tile, before=lambda k: pe.wait_ge(h2_lo, k + 1))
            with pe.Fori(0, NFB - 1) as i:
                at_i = c + GCH + 3 * GCH * i
                gemm(at_i, 0, uses(16) + 3 * i, columns_tile)
                gemm(at_i + GCH, 4, uses(15) + 1 + 3 * i, columns_tile)
                for dg in range(4):
                    used = (uses(16) + 1 + 3 * i, uses(15) + 2 + 3 * i)[dg % 2] + dg // 2
                    down_group(at_i + 2 * GCH, dg, 4 * (dg % 2), used, 4 * i if dg == 0 else None)
            n = NFB - 1
            last_c = c + GCH + 3 * GCH * n
            gemm(last_c, 0, uses(16) + 3 * n, columns_tile)
            def by_token(dg, first):
                for t in range(4):
                    pe.wait_ge(bank_free[(0, 4, 0, 0)[dg] + t], final[dg])
                for t in range(ST):
                    b = first + t
                    if dg == 0:
                        pe.wait_ge(bank_free[b], final[1])
                    if dg in (1, 2):
                        pe.wait_ge(fin_sb, 4 * (dg - 1) + t + 1)
                    for d in range(4):
                        last = tr(PS[:, b, P * d:P * (d + 1)], xT[:, 4 * dg + d, P * t:P * (t + 1)], ident[:, :])
                    last.then_inc(fin_pe, 1)

            used0, used1 = uses(16) + 1 + 3 * n, uses(15) + 1 + 3 * n
            final = (used0 + 1, used1 + 1, used0 + 2, used0 + 3)
            down_group(last_c + GCH, 0, 0, used0, 4 * n)
            down_group(last_c + GCH, 1, 4, used1)
            down_group(last_c + GCH, 2, 0, used0 + 1)
            by_token(0, 4)
            down_group(last_c + GCH, 3, 0, used0 + 2, mid=lambda: by_token(1, 4))
            by_token(2, 4)
            by_token(3, 0)

        @block.scalar
        def _(act):
            f = nc.scalar.activation
            act.preload_act_table_set("natural_log_exp_and_others")
            act.wait_ge(consts, 1)
            for t in range(ST):
                act.wait_ge(x_in[t], 16)
                f(sq_first[:, :], xnat[:, t, :], ACT.Square, accum_out=ssx[:, t:t + 1]).then_inc(act_s, 1)
                act.wait_ge(act_s, t + 1)
            act.wait_ge(par_done, 3)
            f(t16[:, :], par[:, R_C:R_C + KT], ACT.Exp, scale=-1.0).then_inc(exp_c, 1)
            f(rx[:, :], ssx[:, :], ACT.Ln, bias=eps[:, :], scale=1.0 / D).then_inc(act_s, 1)
            act.wait_ge(act_s, ST + 1)
            f(rx[:, :], rx[:, :], ACT.Exp, scale=-0.5).then_inc(rx_done, 1)
            for k in range(KT):
                act.wait_ge(xt_pe, k + 1)
                f(xt0[:, k, :], PS[:, k % 8, :], ACT.Copy).then_inc(xt_sb, 1)
            for b in range(4):
                act.wait_ge(line_pe, b + 1)
                n = (NREV + NFWD) // 4
                f(line[:, n * b:n * (b + 1)], PS[0:NH, b, 0:n], ACT.Copy).then_inc(line_sb, 1)
            act.wait_ge(line_sb, 4)
            for b in range(7):
                act.sem_inc(bank_free[b], 1)

            def hi(c):
                if c // GCH == 9:
                    act.wait_ge(split_in[c % NSTAGE], 16 * (c % GCH // NSTAGE + 1))
                act.wait_ge(stage_in[c % NSTAGE], 16 * (c // NSTAGE + 1))
                if c >= NW:
                    act.wait_ge(w_used, c - NW + 1)
                f(whi[:, c % NW, :, :], stage[:, c % NSTAGE, :, :], ACT.Copy).then_inc(w_hi, 1)

            def hi_at(c, j):
                act.wait_ge(stage_in[j % NSTAGE], (c + j - j % NSTAGE) * 4 + 16)
                act.wait_ge(w_used, c + j - NW + 1)
                f(whi[:, j % NW, :, :], stage[:, j % NSTAGE, :, :], ACT.Copy).then_inc(w_hi, 1)

            def square_tiles(g, tiles=range(4)):
                for t in tiles:
                    n = normed_before(g) + t + 1
                    act.wait_ge(evac, n)
                    if n > 4:
                        act.wait_ge(norm_done, n - 4)
                    f(sq[:, t, :], PS[:, bank(g, t), :], ACT.Square).then_inc(sq_done, 1)
                    f(sq_hi[:, t, :], PS[:, bank(g, t), :], ACT.Square).then_inc(sq_done, 1)

            def norm_factors(g):
                for t in range(4):
                    n = normed_before(g) + t + 1
                    act.wait_ge(ss_pe, n)
                    if n > 4:
                        act.wait_ge(norm_done, n - 4)
                    b = bank(g, t)
                    f(rb[:, t, :], PS[:, b, :], ACT.Ln, bias=eps[:, :], scale=1.0 / P).then_inc(bank_free[b], 1)
                    act.wait_ge(bank_free[b], uses(g + 2))
                    f(rb[:, t, :], rb[:, t, :], ACT.Exp, scale=-0.5).then_inc(r_done, 1)

            def project_in(g):
                for j in range(2 if g in (2, 6) else 0, GCH):
                    hi(GCH * g + j)
                    if g - 1 in NORMED and g > 2 and j in (1, 2):
                        square_tiles(g - 1, range(2 * j - 2, 2 * j))
                    if g == 2 and j == 6:
                        act.wait_ge(small_in, 32)
                        f(wsmall_hi[:, :, :], wsmall[:, :, :], ACT.Copy).then_inc(ws_hi, 1)
                    if g == 3 and j == 1:
                        gates()
                    if g == 6 and j == 5:
                        mean_factor(1, 7, ssf, NH * P)
                    if g - 1 in NORMED and j == 6:
                        norm_factors(g - 1)

            for j in range(GCH):
                hi(2 * j)
                act.wait_ge(mod_ready, j + 1)
                for k in (2 * j, 2 * j + 1):
                    act.wait_ge(xn_done, k + 1)
                    if k >= 4:
                        act.wait_ge(h_lo, k - 3)
                    f(h1t[:, k % 4, :], xn[:, k, :], ACT.Identity, bias=mod[:, 0, k:k + 1],
                      scale=mod[:, 1, k:k + 1]).then_inc(h_full, 1)
                for k in (2 * j, 2 * j + 1):
                    act.wait_ge(h_full, k + 1)
                    f(hhi[:, k, :], h1t[:, k % 4, :], ACT.Copy).then_inc(h_hi, 1)
                hi(2 * j + 1)
            square_tiles(0)
            hi(2 * GCH)
            hi(2 * GCH + 1)
            norm_factors(0)
            square_tiles(1)

            def gates():
                act.wait_ge(small_pe, 1)
                f(fl2[:, :], PS[0:NSMALL, 7, :], ACT.Exp, scale=-1.0).then_inc(gates_e, 1)
                act.wait_ge(z_done, 1)
                f(fb[:, :], fb[:, :], ACT.Exp, scale=-1.0).then_inc(fexp, 1)
                act.wait_ge(fexp, 1)
                f(fb[:, :], fb[:, :], ACT.Ln, bias=ones[0:NH, 0:1]).then_inc(fexp, 1)

            for g in range(2, 6):
                project_in(g)

            def exp_tiles(u, tiles=range(ST)):
                for i in tiles:
                    t = TS[i]
                    fox = u < UF
                    b, c0 = S_AT[t]
                    p0, n = parts(t)
                    act.wait_ge(s_max, 4 * u + (4 if fox and i == 2 else i + 1))
                    if fox and u >= 2 and i == 0:
                        act.wait_ge(t_pe, 4 * (u - 1))
                    src = PS[:, b, c0:c0 + n] if fox else prob[u % 2][:, p0:p0 + n]
                    f(prob[u % 2][:, p0:p0 + n], src, ACT.Exp, bias=nmax[:, t:t + 1], scale=1.0 if fox else -1.0,
                      accum_out=psum_row[:, t:t + 1]).then_inc(s_exp, 1)

            def transposed_out(u, blocks):
                for kb in blocks:
                    if u >= 2:
                        act.wait_ge(pv_done, u - 1)
                    act.wait_ge(t_pe, 4 * u + (2 if kb == 2 else 4))
                    b = T_AT[kb][0]
                    n = S - P * kb if kb else S
                    f(probT[u % 2][:, T_SB[kb]:T_SB[kb] + n], PS[:, b, 0:n], ACT.Copy).then_inc(t_act, 1)

            def head_out(n, dst):
                if n < UF:
                    act.wait_ge(pv_done, n + 1)
                else:
                    act.wait_ge(o_pe, n - UF + 1)
                f(dst, PS[:, 6, :], ACT.Copy)
                if n >= 1:
                    act.wait_ge(ss_acc, n)
                f(o_sq[:, :], PS[:, 6, :], ACT.Square).then_inc(o_sb, 1)

            def mean_factor(n, b, dst, width):
                act.wait_ge(ssy_pe, n)
                f(dst[:, :], PS[:, b, :], ACT.Ln, bias=eps[:, :], scale=1.0 / width).then_inc(ry_ln, 1)
                act.wait_ge(ry_ln, n)
                f(dst[:, :], dst[:, :], ACT.Exp, scale=-0.5).then_inc(ry_done, 1)

            exp_tiles(0)
            for h in range(NH):
                if h + 1 < NH:
                    exp_tiles(h + 1)
                if h >= 1:
                    head_out(h - 1, fq[:, h - 1, :])
                transposed_out(h, (2, 0))
                if h == NH - 2:
                    hi(GCH * 6)
                    hi(GCH * 6 + 1)
            head_out(NH - 1, fq[:, NH - 1, :])

            for g in range(6, 11):
                project_in(g)

            for h in range(NH):
                act.wait_ge(flip_pe, h + 1)
                f(rel[:, h, :], PS[:, 4 + h % 3, :], ACT.Copy).then_inc(flip_sb, 1)
            exp_tiles(UF)
            act.wait_ge(hid_pe, 1)
            for b in range(2):
                f(hid2[:, b, :], PS[:, 7, 64 * b:64 * b + 2 * NCMP], ACT.Exp, scale=-1.0).then_inc(hid_exp, 1)
            act.wait_ge(kc_copied, 1)
            f(hid2[:, 0, :], PS[:, 6, 0:2 * NCMP], ACT.Square).then_inc(kc_sq, 1)
            act.wait_ge(kc_ss, 1)
            f(hid2[:, 1, :], PS[:, 6, 64:64 + 2 * NCMP], ACT.Ln, bias=eps[:, :], scale=1.0 / P).then_inc(kc_ln, 1)
            act.wait_ge(kc_ln, 1)
            f(hid2[:, 1, :], hid2[:, 1, :], ACT.Exp, scale=-0.5).then_inc(kc_r, 1)

            def mixed_hi(k):
                act.wait_ge(y_full, k + 1)
                f(hhi[:, k, :], (fq if k < NH else nq)[:, k % NH, :], ACT.Copy).then_inc(y_hi, 1)

            for step in range(2 * NH):
                h, win = divmod(step, 2)
                if step + 1 < 2 * NH:
                    exp_tiles(UF + step + 1)
                if win == 0 and h >= 1:
                    head_out(UF + h - 1, nq[:, h - 1, :])
                transposed_out(UF + step, (2, 0))
                if win == 0:
                    act.wait_ge(sc_sub, h + 1)
                    f(probc[:, :, 0:NCMP], probc[:, :, 0:NCMP], ACT.Exp).then_inc(sc_exp, 1)
                else:
                    act.wait_ge(pct_pe, h + 1)
                    f(probcT[:, :], PS[0:NCMP, 7, :], ACT.Copy).then_inc(pct_sb, 1)
                    mixed_hi(h)
                    if h == NH - 2:
                        hi(GCH * G_OUT)
                        hi(GCH * G_OUT + 1)
            head_out(2 * NH - 1, nq[:, NH - 1, :])

            hi(GCH * G_OUT + 2)
            hi(GCH * G_OUT + 3)
            mean_factor(2, 0, ssn, NH * P)
            for k in range(NH, KT):
                mixed_hi(k)
                if k % 2 == 1:
                    hi(GCH * G_OUT + k // 2)

            def square_x1(g):
                for t in range(4):
                    n = 4 * (g - G_OUT) + t
                    act.wait_ge(bank_free[bank(g, t)], uses(g + 2))
                    if n >= 4:
                        act.wait_ge(x1_acc, n - 3)
                    f(x1_sqt[:, t, :], xT[:, n, :], ACT.Square).then_inc(x1_sq, 1)

            for g in range(G_OUT + 1, G_FF):
                for j in range(GCH):
                    hi(GCH * g + j)
                    if g > G_OUT and j == 1:
                        square_x1(g - 1)
            c = GCH * G_FF
            hi(c)
            square_x1(G_FF - 1)
            hi(c + 1)
            act.wait_ge(ssh_pe, 1)
            f(ssf[:, :], PS[:, 0, :], ACT.Ln, bias=eps[:, :], scale=1.0 / D).then_inc(rh_ln, 1)
            act.wait_ge(rh_ln, 1)
            f(ssf[:, :], ssf[:, :], ACT.Exp, scale=-0.5).then_inc(rh_done, 1)
            for k in range(KT):
                act.wait_ge(h2_t, k + 1)
                f(hhi[:, k, :], h2t[:, k % 4, :], ACT.Identity, bias=mod[:, 3, k:k + 1]).then_inc(h2_hi, 1)
                if k >= 3 and k % 2 == 1:
                    hi(c + (k + 1) // 2)

            def silu_tiles(tiles, chunks):
                for t in range(4):
                    await_ff(act, t, tiles, chunks)
                    f(silu_g[:, t, :], PS[:, 4 + t, :], ACT.Silu).then_inc(bank_free[4 + t], 1)

            def high_of_g(i):
                for t in range(4):
                    act.wait_ge(bank_free[t], uses(16) + 3 * i + 1)
                    f(ghi[:, t, :], gfull[:, t, :], ACT.Copy).then_inc(g_hi, 1)

            hi(c + GCH + 1)
            silu_tiles(3 * G_FF, c + GCH)
            with act.Fori(0, NFB - 1) as i:
                at_i = c + GCH + 3 * GCH * i
                for j in range(2, 3 * GCH + 2):
                    hi_at(at_i, j)
                    if j == GCH + 2:
                        high_of_g(i)
                    if j == 2 * GCH + 1:
                        silu_tiles(3 * (G_FF + 2) + 18 * i, at_i + 2 * GCH)
            n = NFB - 1
            at_n = c + GCH + 3 * GCH * n
            for j in range(2, 2 * GCH):
                hi(at_n + j)
                if j == GCH:
                    high_of_g(n)
            for dg in range(4):
                if dg >= 2:
                    act.wait_ge(out_sent[dg % 2], 16 * ST)
                for t in range(ST) if dg < 3 else (0, 2):
                    act.wait_ge(fin_pe, 4 * dg + t + 1)
                    b = (4 if dg < 3 else 0) + t
                    f(ostage[:, dg % 2, t, :], PS[:, b, :], ACT.Copy).then_inc(fin_sb, 1)

        @block.vector
        def _(dve):
            v = nc.vector
            own = [0]

            def then(ins):
                own[0] += 1
                ins.then_inc(dve_s, 1)
                dve.wait_ge(dve_s, own[0])

            dve.wait_ge(par_t, 3)
            v.tensor_copy(par[:, :], PS[:, 0, 0:NPAR]).then_inc(par_done, 1)
            v.tensor_copy(adab[:, :], PS[:, 1, 0:96]).then_inc(par_done, 1)
            v.tensor_copy(cpos[:, :], PS[:, 2, 0:2 * CB]).then_inc(par_done, 1)
            dve.wait_ge(par_done, 3)
            then(v.tensor_scalar(par[:, R_FQ:R_FQ + 1], par[:, R_FQ:R_FQ + 1], SCALE, None, ALU.mult))
            then(v.tensor_scalar(par[:, R_NQ:R_NQ + 1], par[:, R_NQ:R_NQ + 1], SCALE, None, ALU.mult))
            dve.wait_ge(exp_c, 1)
            then(v.tensor_scalar(t16[:, :], t16[:, :], 1.0, None, ALU.add))
            then(v.reciprocal(t16[:, :], t16[:, :]))
            then(v.tensor_tensor(silu_c[:, :], t16[:, :], par[:, R_C:R_C + KT], ALU.mult))
            dve.wait_ge(rx_done, 1)
            dve.wait_ge(consts, 1)
            for t in range(ST):
                v.tensor_scalar(diag[:, t, :], ident[:, :], rx[:, t:t + 1], None, ALU.mult).then_inc(diag_done, 1)

            def lo(c):
                dve.wait_ge(w_hi, c + 1)
                v.tensor_tensor(wlo[:, c % NW, :, :], stage[:, c % NSTAGE, :, :], whi[:, c % NW, :, :].bitcast(F32),
                                ALU.subtract).then_inc(w_lo, 1)

            def h_low(k):
                dve.wait_ge(h_hi, k + 1)
                v.tensor_tensor(hlo[:, k, :], h1t[:, k % 4, :], hhi[:, k, :].bitcast(F32),
                                ALU.subtract).then_inc(h_lo, 1)

            def partial_out(j):
                dve.wait_ge(w_used, 2 * j + 2)
                if j == 0:
                    v.tensor_copy(partial[:, :], PS[:, 7, :]).then_inc(part_out, 1)
                else:
                    dve.wait_ge(part_out, j)
                    v.tensor_tensor(partial[:, :], PS[:, 7, :], partial[:, :], ALU.add).then_inc(part_out, 1)

            for j in range(GCH):
                for k in range(KT):
                    if k % 4 == 0:
                        dve.wait_ge(first_in[k // 4], 32 * (j + 1))
                    part = acc_first[:, k % 2, :]
                    src = ada_first[k // 4][:, k % 4, :, :].rearrange("p c n -> p (c n)")
                    if k < 2:
                        v.tensor_scalar(part, src, silu_c[:, k:k + 1], None, ALU.mult).then_inc(first_acc, 1)
                    else:
                        dve.wait_ge(first_acc, KT * j + k - 1)
                        v.scalar_tensor_tensor(out=part, in0=src, scalar=silu_c[:, k:k + 1], in1=part,
                                               op0=ALU.mult, op1=ALU.add).then_inc(first_acc, 1)
                    if k == 11 and j == 0:
                        dve.wait_ge(rb_pe, 1)
                        v.tensor_copy(ssf[:, :], PS[:, 7, :]).then_inc(bank_free[7], 1)
                    if k == 3 and j >= 1:
                        h_low(2 * j - 2)
                        h_low(2 * j - 1)
                    if k == 11 and j >= 2:
                        partial_out(j - 2)
                dve.wait_ge(mod_pe, j + 1)
                ks = slice(CK * j, CK * (j + 1))
                then(v.tensor_tensor(mod[:, 0:2, ks], PS[:, 7, 0:2 * CK].rearrange("p (c k) -> p c k", c=2),
                                     adab[:, 0:2 * KT].rearrange("p (c k) -> p c k", c=2)[:, :, ks], ALU.add))
                v.scalar_tensor_tensor(out=mod[:, 1, ks], in0=mod[:, 1, ks], scalar=1.0,
                                       in1=par[:, R_N1 + CK * j:R_N1 + CK * (j + 1)],
                                       op0=ALU.add, op1=ALU.mult).then_inc(mod_ready, 1)
            h_low(KT - 2)
            h_low(KT - 1)
            partial_out(GCH - 2)

            def lo_at(c, j):
                dve.wait_ge(w_hi, c + j + 1)
                v.tensor_tensor(wlo[:, j % NW, :, :], stage[:, j % NSTAGE, :, :], whi[:, j % NW, :, :].bitcast(F32),
                                ALU.subtract).then_inc(w_lo, 1)

            def ada(a):
                k, half = a % 32 // 2, a % 2
                part = acc[:, a // 32 % 2, 1024 * half:1024 * (half + 1)]
                dve.wait_ge(ada_in[a % 3], 16 * (a // 3 + 1))
                src = ada_ring[:, a % 3, :]
                if k == 0:
                    v.tensor_scalar(part, src, silu_c[:, 0:1], None, ALU.mult).then_inc(ada_acc, 1)
                else:
                    dve.wait_ge(ada_acc, a - 1)
                    v.scalar_tensor_tensor(out=part, in0=src, scalar=silu_c[:, k:k + 1], in1=part,
                                           op0=ALU.mult, op1=ALU.add).then_inc(ada_acc, 1)

            def tiles_out(g):
                for t in range(4):
                    await_tile(dve, g, t)
                    if g in NORMED:
                        v.tensor_scalar(tile_of(g, t), PS[:, bank(g, t), :], gain_of(g, t), None,
                                        ALU.mult).then_inc(evac, 1)
                    else:
                        v.tensor_copy(tile_of(g, t), PS[:, bank(g, t), :]).then_inc(bank_free[bank(g, t)], 1)

            def normalise(g):
                for t in range(4):
                    dve.wait_ge(r_done, normed_before(g) + t + 1)
                    v.tensor_tensor(tile_of(g, t), tile_of(g, t), rb[:, t, :], ALU.mult).then_inc(norm_done, 1)

            def mixed(k, low):
                y = (fq if k < NH else nq)[:, k % NH, :]
                if not low:
                    dve.wait_ge(ry_done, 1 if k < NH else 2)
                    v.scalar_tensor_tensor(out=y, in0=y, scalar=par[:, R_MIX + k:R_MIX + k + 1],
                                           in1=(ssf if k < NH else ssn)[:, :], op0=ALU.mult,
                                           op1=ALU.mult).then_inc(y_full, 1)
                else:
                    dve.wait_ge(y_hi, k + 1)
                    v.tensor_tensor(hlo[:, k, :], y, hhi[:, k, :].bitcast(F32), ALU.subtract).then_inc(y_lo, 1)

            def unfolded(i):
                b, kv = i // 2, i % 2
                row = nk[:, 4 + i, :]
                windows = bass.AP(tensor=row.tensor, offset=row.offset, ap=[row.ap[0], [1, CB], [CS, NCMP]])
                if i == 0:
                    dve.wait_ge(bank_free[7], uses(11))
                v.tensor_tensor(unfold[:, b, :, NCMP * kv:NCMP * (kv + 1)], windows,
                                cpos[:, CB * b:CB * (b + 1)].unsqueeze(2).to_broadcast([P, CB, NCMP]),
                                ALU.add).then_inc(unf, 1)

            def project_in(g, first=0):
                for j in range(first, GCH):
                    lo(GCH * g + j)
                    for a in plan[g, j]:
                        ada(a)
                    if g != 6 and j == 1:
                        if g == 3:
                            dve.wait_ge(xt_out, 16)
                        tiles_out(g - 1)
                    if g == 2 and j == 6:
                        dve.wait_ge(ws_hi, 1)
                        v.tensor_tensor(wsmall_lo[:, :, :], wsmall[:, :, :], wsmall_hi[:, :, :].bitcast(F32),
                                        ALU.subtract).then_inc(ws_lo, 1)
                    if g == 3 and j in (1, 3, 5):
                        {1: forget_logits, 3: forget_gates, 5: branch_gates}[j]()
                    if g == 10 and 2 <= j < 6:
                        unfolded(j - 2)
                    if g - 1 in NORMED and j == 7:
                        normalise(g - 1)

            def forget_logits():
                dve.wait_ge(gates_e, 1)
                then(v.tensor_scalar(fl[0:NH, :], PS[0:NH, 7, :], fbias[:, :], None, ALU.add))
                dve.sem_inc(small_out, 1)
                then(v.tensor_scalar(fa[:, :], fl[0:NH, :], -1.0, None, ALU.mult))
                v.tensor_tensor(fb[:, :], fl[0:NH, :], fa[:, :], ALU.max).then_inc(z_done, 1)

            def forget_gates():
                dve.wait_ge(z_done, 1)
                then(v.tensor_scalar(fa[:, :], fl[0:NH, :], 0.0, None, ALU.min))
                dve.wait_ge(fexp, 2)
                then(v.tensor_tensor(fa[:, :], fb[:, :], fa[:, :], ALU.subtract))
                then(v.memset(fb[:, :], 1.0))
                then(v.tensor_tensor_scan(fl[0:NH, :], fb[:, :], fa[:, :], 0.0, ALU.mult, ALU.add))
                dve.wait_ge(sel_ready, 1)
                v.tensor_copy(cumb[0:NH, :], fl[0:NH, :]).then_inc(forget_ready, 1)
                dve.wait_ge(forget_ready, 1)
                then(v.tensor_tensor(fa[:, :], fl[0:NH, :], cumb[0:NH, :], ALU.subtract))
                then(v.tensor_copy(cumt[:, :], fa[:, :]))
                v.tensor_copy(cumb[32:32 + NH, :], cumt[:, :]).then_inc(forget_ready, 1)
                then(v.tensor_tensor(fa[:, :], fa[:, :], cumt[:, :], ALU.subtract))
                v.tensor_copy(cumb[64:64 + NH, :], fa[:, :]).then_inc(forget_ready, 1)

            def branch_gates():
                then(v.tensor_scalar(fl2[:, :], fl2[:, :], 1.0, None, ALU.add))
                v.reciprocal(fl2[:, :], fl2[:, :]).then_inc(gates_ready, 1)
            tiles_out(0)
            dve.wait_ge(w_lo, 2 * GCH)
            lo(2 * GCH)
            lo(2 * GCH + 1)
            tiles_out(1)
            normalise(0)
            project_in(2, 2)
            for g in range(3, 6):
                project_in(g)
            tiles_out(5)

            def score_tile(u, i, h):
                t = TS[i]
                b, c0 = S_AT[t]
                n = P * (t + 1)
                dve.wait_ge(s_pe, 4 * u + (i + 1 if i < 2 else 4))
                if u >= 2 and i == 0:
                    dve.wait_ge(t_pe, 4 * (u - 1))
                src = PS[:, b, c0:c0 + n]
                if u < UF:
                    v.tensor_reduce(nmax[:, t:t + 1], src, AX.X, ALU.max, negate=True).then_inc(s_max, 1)
                else:
                    p0 = P_SB[t]
                    v.tensor_tensor_reduce(out=prob[u % 2][:, p0:p0 + n], in0=src, in1=rel[:, h, P * (3 - t):S],
                                           scale=-1.0, scalar=3e38, op0=ALU.add, op1=ALU.min,
                                           accum_out=nmax[:, t:t + 1]).then_inc(s_max, 1)

            def prob_tile(u, i, gate_of):
                t = TS[i]
                p0, n = parts(t)
                dve.wait_ge(s_exp, 4 * u + i + 1)
                then(v.reciprocal(rinv[:, t:t + 1], psum_row[:, t:t + 1]))
                v.tensor_scalar(prob[u % 2][:, p0:p0 + n], prob[u % 2][:, p0:p0 + n], rinv[:, t:t + 1], gate_of(t),
                                ALU.mult, ALU.mult if gate_of(t) is not None else ALU.bypass).then_inc(p_done, 1)

            def transposed_out(u):
                if u >= 2:
                    dve.wait_ge(pv_done, u - 1)
                dve.wait_ge(t_pe, 4 * u + 3)
                v.tensor_copy(probT[u % 2][:, T_SB[1]:T_SB[1] + S], PS[:, 4, :]).then_inc(t_dve, 1)

            def unit_scores(u, h, gate_of, out=None):
                score_tile(u, 0, h)
                score_tile(u, 1, h)
                prob_tile(u, 0, gate_of)
                score_tile(u, 2, h)
                score_tile(u, 3, h)
                prob_tile(u, 1, gate_of)
                prob_tile(u, 2, gate_of)
                prob_tile(u, 3, gate_of)
                if out is not None:
                    transposed_out(out)

            unit_scores(0, 0, lambda t: None)
            dve.wait_ge(gates_pe, 1)
            v.tensor_copy(gate[:, :, :], PS[:, 7, 0:ST * NSMALL].rearrange("p (t n) -> p t n", t=ST)).then_inc(gates_nat, 1)
            for h in range(NH):
                if h + 1 < NH:
                    unit_scores(h + 1, h + 1, lambda t: None, h)
                else:
                    transposed_out(h)
                if h == NH - 2:
                    lo(GCH * 6)
                    lo(GCH * 6 + 1)
            dve.wait_ge(mod2_pe, 1)
            v.tensor_tensor(mod[:, 2:4, :], PS[:, 7, 128:128 + 2 * KT].rearrange("p (c k) -> p c k", c=2),
                            adab[:, 2 * KT:4 * KT].rearrange("p (c k) -> p c k", c=2), ALU.add).then_inc(mod2_done, 1)

            for a in (*plan[6, 0], *plan[6, 1]):
                ada(a)
            project_in(6, 2)
            for g in range(7, 11):
                project_in(g)
            tiles_out(10)

            def gate_at(h, branch):
                return lambda t: gate[:, t, NH + 3 * h + branch:NH + 3 * h + branch + 1]

            dve.wait_ge(flip_sb, NH)
            dve.wait_ge(consts, 1)
            unit_scores(UF, 0, gate_at(0, 1))
            for b in range(2):
                dve.wait_ge(hid_exp, 2)
                then(v.tensor_scalar(hid2[:, b, :], hid2[:, b, :], 1.0, None, ALU.add))
                then(v.reciprocal(hid2[:, b, :], hid2[:, b, :]))
                v.tensor_tensor(hid[:, b, :], hid2[:, b, :], PS[:, 7, 64 * b:64 * b + 2 * NCMP],
                                ALU.mult).then_inc(hid_done, 1)
            dve.wait_ge(kcv_pe, 1)
            dve.wait_ge(hid_done, 2)
            kcs = PS[:, 6, 0:2 * NCMP].rearrange("p (h c) -> p h c", h=2)
            v.tensor_copy(vc[:, :, :], PS[0:NCMP, 6, 256:S].rearrange("p (h d) -> p h d", h=2)).then_inc(vc_ready, 1)
            v.tensor_scalar(kc[:, :, 0:NCMP], kcs, par[:, R_NK:R_NK + 1], None, ALU.mult).then_inc(kc_copied, 1)
            dve.wait_ge(kc_r, 1)
            dve.wait_ge(kc_copied, 1)
            v.tensor_tensor(kc[:, :, 0:NCMP], kc[:, :, 0:NCMP], hid2[:, 1, :].rearrange("p (h c) -> p h c", h=2),
                            ALU.mult).then_inc(kc_ready, 1)

            def cmp_probs(h):
                dve.wait_ge(sc_pe, h + 1)
                s = PS[:, 7, 0:ST * NSMALL].rearrange("p (t n) -> p t n", t=ST)[:, :, 0:NCMP]
                then(v.tensor_reduce(cmax[:, :], s, AX.X, ALU.max))
                if h >= 1:
                    dve.wait_ge(pct_pe, h)
                v.tensor_tensor(probc[:, :, 0:NCMP], s, cmax[:, :].unsqueeze(2).to_broadcast([P, ST, NCMP]),
                                ALU.subtract).then_inc(sc_sub, 1)
                n = 4 * h
                then(v.tensor_tensor(mod[:, 4 + n // KT, n % KT:n % KT + 4], PS[:, 7, 128 + n:132 + n],
                                     adab[:, 4 * KT + n:4 * KT + n + 4], ALU.add))

            def cmp_weights(h):
                dve.wait_ge(sc_exp, h + 1)
                then(v.tensor_reduce(csum[:, :], probc[:, :, 0:NCMP], AX.X, ALU.add))
                then(v.reciprocal(csum[:, :], csum[:, :]))
                then(v.tensor_tensor(csum[:, :], csum[:, :], gate[:, :, NH + 3 * h], ALU.mult))
                then(v.tensor_tensor(csum[:, :], csum[:, :], rowok[:, :], ALU.mult))
                v.tensor_tensor(probc[:, :, 0:NCMP], probc[:, :, 0:NCMP],
                                csum[:, :].unsqueeze(2).to_broadcast([P, ST, NCMP]), ALU.mult).then_inc(pc_done, 1)

            for h in range(NH):
                for win in range(2):
                    u = UF + 2 * h + win
                    if win == 0:
                        unit_scores(u + 1, h, gate_at(h, 2), u)
                        cmp_probs(h)
                        mixed(h, False)
                    else:
                        cmp_weights(h)
                        if h + 1 < NH:
                            unit_scores(u + 1, h + 1, gate_at(h + 1, 1), u)
                        else:
                            transposed_out(u)
                if h == NH - 2:
                    lo(GCH * G_OUT)
                    lo(GCH * G_OUT + 1)
            then(v.scalar_tensor_tensor(out=mod[:, 4, :], in0=mod[:, 4, :], scalar=1.0, in1=par[:, R_N2:R_N2 + KT],
                                        op0=ALU.add, op1=ALU.mult))

            lo(GCH * G_OUT + 2)
            lo(GCH * G_OUT + 3)
            dve.wait_ge(y_lo, NH)
            for k in range(NH, KT + 1):
                if k < KT:
                    mixed(k, False)
                if k > NH:
                    mixed(k - 1, True)
                    if k % 2 == 0:
                        lo(GCH * G_OUT + k // 2 - 1)

            def x1_tiles(g):
                dve.wait_ge(xT_in[g - G_OUT], 16)
                for t in range(4):
                    n = 4 * (g - G_OUT) + t
                    await_tile(dve, g, t)
                    v.scalar_tensor_tensor(out=xT[:, n, :], in0=PS[:, bank(g, t), :], scalar=mod[:, 2, n:n + 1],
                                           in1=xT[:, n, :], op0=ALU.mult, op1=ALU.add).then_inc(bank_free[bank(g, t)], 1)
                for n in range(4 * (g - G_OUT), 4 * (g - G_OUT) + 4) if g < G_FF - 1 else ():
                    dve.wait_ge(x1_sq, n + 1)
                    if n == 0:
                        v.tensor_copy(ssf[:, :], x1_sqt[:, 0, :]).then_inc(x1_acc, 1)
                    else:
                        dve.wait_ge(x1_acc, n)
                        v.tensor_tensor(ssf[:, :], ssf[:, :], x1_sqt[:, n % 4, :], ALU.add).then_inc(x1_acc, 1)

            for g in range(G_OUT + 1, G_FF):
                for j in range(GCH):
                    lo(GCH * g + j)
                    if g > G_OUT and j == 1:
                        x1_tiles(g - 1)
            c = GCH * G_FF
            lo(c)
            x1_tiles(G_FF - 1)
            lo(c + 1)
            dve.wait_ge(rh_done, 1)
            for k in range(KT + 1):
                if k < KT:
                    if k >= 4:
                        dve.wait_ge(h2_lo, k - 3)
                    v.scalar_tensor_tensor(out=h2t[:, k % 4, :], in0=xT[:, k, :], scalar=mod[:, 4, k:k + 1],
                                           in1=ssf[:, :], op0=ALU.mult, op1=ALU.mult).then_inc(h2_t, 1)
                if k >= 1:
                    dve.wait_ge(h2_hi, k)
                    v.scalar_tensor_tensor(out=hlo[:, k - 1, :], in0=h2t[:, (k - 1) % 4, :], scalar=mod[:, 3, k - 1:k],
                                           in1=hhi[:, k - 1, :].bitcast(F32), op0=ALU.add,
                                           op1=ALU.subtract).then_inc(h2_lo, 1)
                    if k >= 4 and k % 2 == 0:
                        lo(c + k // 2)

            def silu_times_up(i, c, tiles=range(4)):
                for t in tiles:
                    await_ff(dve, t, 3 * (G_FF + 1) + 18 * i, c + GCH)
                    v.tensor_tensor(gfull[:, t, :], PS[:, t, :], silu_g[:, t, :], ALU.mult).then_inc(bank_free[t], 1)

            def low_of_g(i, tiles=range(4)):
                for t in tiles:
                    dve.wait_ge(g_hi, 4 * i + t + 1)
                    v.tensor_tensor(glo[:, t, :], gfull[:, t, :], ghi[:, t, :].bitcast(F32),
                                    ALU.subtract).then_inc(g_lo, 1)

            def down_out(dg, tiles, chunks, first=None):
                for t in range(4):
                    n = 4 * dg + t
                    await_ff(dve, t, tiles + 3 * dg, chunks + 2 * dg + 2)
                    b = (4 * (dg % 2) if first is None else first) + t
                    v.scalar_tensor_tensor(out=xT[:, n, :], in0=PS[:, b, :], scalar=mod[:, 5, n:n + 1],
                                           in1=xT[:, n, :], op0=ALU.mult, op1=ALU.add).then_inc(bank_free[b], 1)

            lo(c + GCH + 1)
            with dve.Fori(0, NFB - 1) as i:
                at_i = c + GCH + 3 * GCH * i
                for j in range(2, 3 * GCH + 2):
                    lo_at(at_i, j)
                    if j == GCH + 1:
                        silu_times_up(i, at_i)
                    if j == GCH + 3:
                        low_of_g(i)
                    if j > 2 * GCH + 2 and j % 2 == 1:
                        down_out((j - 2 * GCH - 3) // 2, 3 * (G_FF + 3) + 18 * i, at_i + 2 * GCH)
            n = NFB - 1
            at_n = c + GCH + 3 * GCH * n
            for j in range(2, GCH):
                lo(at_n + j)
            lo(at_n + GCH)
            for t in range(5):
                if t < 4:
                    silu_times_up(n, at_n, (t,))
                if t >= 1:
                    low_of_g(n, (t - 1,))
            lo(at_n + GCH + 1)
            for j in range(2, GCH + 2):
                if j < GCH:
                    lo(at_n + GCH + j)
                if j % 2 == 1:
                    dg = (j - 3) // 2
                    down_out(dg, 3 * (G_FF + 2) + 18 * n, at_n + GCH, (0, 4, 0, 0)[dg])
            dve.wait_ge(out_sent[1], 16 * ST)
            for t in (1, 3):
                dve.wait_ge(fin_pe, 12 + t + 1)
                v.tensor_copy(ostage[:, 1, t, :], PS[:, t, :]).then_inc(fin_last, 1)

        @block.gpsimd
        def _(pool):
            g = nc.gpsimd
            done = [0]

            def then(ins):
                done[0] += 1
                ins.then_inc(pool_s, 1)
                pool.wait_ge(pool_s, done[0])

            then(g.memset(ident[:, :], 0.0))
            then(g.affine_select(out=ident[:, :], in_=ident[:, :], pattern=[[-1, P]], compare_op=ALU.not_equal,
                                 fill=1.0, base=0, channel_multiplier=1))
            for f, n in ((flip, P), (flipc, NCMP)):
                then(g.memset(f[:, :], 0.0))
                then(g.affine_select(out=f[:, :], in_=f[:, :], pattern=[[1, n]], compare_op=ALU.not_equal,
                                     fill=1.0, base=1 - n, channel_multiplier=1))
            then(g.memset(diag[:, 0, :], 1.0))
            then(g.tensor_copy(ones_r[:, :], diag[:, 0, :]))
            then(g.memset(eps[:, :], EPS))
            then(g.memset(relb[NBUCKET:NBUCKET + 1, :], NEG))
            then(g.tensor_copy(identb[:, :], ident[:, :]))
            then(g.memset(maskb[:, :], 0.0))
            then(g.affine_select(out=maskb[:, :], in_=maskb[:, :], pattern=[[-1, P]], compare_op=ALU.is_ge,
                                 fill=NEG, base=0, channel_multiplier=1))
            then(g.memset(rowok[:, :], 1.0))
            g.affine_select(out=rowok[:, 0:1], in_=rowok[:, 0:1], pattern=[[0, 1]], compare_op=ALU.is_ge,
                            fill=0.0, base=-(CB - 1), channel_multiplier=1).then_inc(consts, 1)
            pool.wait_ge(bank_free[7], 1)
            for k in range(KT):
                pool.wait_ge(xt_sb, k + 1)
                g.tensor_tensor(xn[:, k, :], xt0[:, k, :], ssf[:, :], ALU.mult).then_inc(xn_done, 1)
                for c in ((k - 2,) if 2 <= k < KT - 1 else (k - 2, k - 1, k) if k == KT - 1 else ()):
                    pool.wait_ge(w_hi, c + 1)
                    g.tensor_tensor(wlo[:, c % NW, :, :], stage[:, c % NSTAGE, :, :],
                                    whi[:, c % NW, :, :].bitcast(F32), ALU.subtract).then_inc(w_lo, 1)

            def squares_low(group):
                for t in range(4):
                    n = normed_before(group) + t + 1
                    pool.wait_ge(sq_done, 2 * n)
                    g.tensor_tensor(sq_lo[:, t, :], sq[:, t, :], sq_hi[:, t, :].bitcast(F32),
                                    ALU.subtract).then_inc(sq_split, 1)

            squares_low(0)
            squares_low(1)
            pool.wait_ge(small_pe, 1)
            then(g.memset(cumb[:, :], 0.0))
            then(g.memset(sel[:, :, :], 0.0))
            for q in range(3):
                last = g.affine_select(out=sel[:, :, :], in_=sel[:, :, :], pattern=[[-1, NH], [0, P]],
                                       compare_op=ALU.not_equal, fill=1.0, base=-32 * q, channel_multiplier=1)
                if q < 2:
                    then(last)
            last.then_inc(sel_ready, 1)

            def sum_squares(n, dst):
                pool.wait_ge(o_sb, n + 1)
                if n % NH == 0:
                    g.tensor_copy(dst[:, :], o_sq[:, :]).then_inc(ss_acc, 1)
                else:
                    pool.wait_ge(ss_acc, n)
                    g.tensor_tensor(dst[:, :], dst[:, :], o_sq[:, :], ALU.add).then_inc(ss_acc, 1)

            squares_low(2)
            squares_low(3)
            for h in range(NH):
                sum_squares(h, ssf)
            for group in (6, 7, 8):
                squares_low(group)
            for h in range(NH):
                if h >= 1:
                    sum_squares(UF + h - 1, ssn)
                pool.wait_ge(y_hi, h + 1)
                g.tensor_tensor(hlo[:, h, :], fq[:, h, :], hhi[:, h, :].bitcast(F32), ALU.subtract).then_inc(y_lo, 1)
            sum_squares(2 * NH - 1, ssn)


_INS = ['x', 'c', 'ada_w', 'ada_b', 'norm1_gain', 'norm2_gain', 'w_in', 'fox_f_bias', 'fox_q_gain', 'fox_k_gain',
        'nsa_q_gain', 'nsa_k_gain', 'nsa_cmp_pos', 'nsa_cmp_w1', 'nsa_cmp_w2', 'rel_bias', 'mix_out_gain', 'w_out',
        'ffn_w_gate', 'ffn_w_up', 'ffn_w_down']


def bucket_onehot():
    d = np.concatenate([S - 1 - np.arange(NREV), np.arange(NFWD) - (S - 1)])
    exact = NBUCKET // 2
    n = np.maximum(d, 1).astype(np.float64)
    large = exact + (np.log(n / exact) / np.log(MAXDIST / exact) * (NBUCKET - exact)).astype(np.int64)
    b = np.where(d < exact, d, np.minimum(large, NBUCKET - 1))
    b = np.where(d < 0, NBUCKET, b)
    return (np.arange(NBUCKET + 1)[:, None] == b[None, :]).astype(np.float32)


def kernel(**inputs):
    import concourse.bacc as bacc
    from concourse.bass_utils import run_bass_kernel_spmd

    nc = bacc.Bacc("TRN2", target_bir_lowering=False, num_devices=1)
    arrays, aps = {}, {}
    given = {name: np.ascontiguousarray(inputs[name]) for name in _INS}
    given["bucket_onehot"] = bucket_onehot()
    for name, a in given.items():
        arrays[f"in_{name}"] = a
        aps[name] = nc.dram_tensor(f"in_{name}", a.shape, mybir.dt.from_np(a.dtype), kind="ExternalInput").ap()
    out = nc.dram_tensor("out_0", (1, S, D), F32, kind="ExternalOutput").ap()
    hybrid_layer(nc, aps, out)
    r = run_bass_kernel_spmd(nc, [arrays], core_ids=[0])
    return r.results[0]["out_0"]
```
